# Optimizing a Trainium2 kernel written in Bass

```python
import math
import jax, jax.numpy as jnp
from jax import lax
import numpy as np

D_MODEL = 2048
BATCH = 1
SEQ = 256
DEPTH = 2

N_META = 16
LN_EPS = 1e-5
RMS_EPS = 1e-6
DEEPNORM_ALPHA = (2.0 * DEPTH) ** 0.25
DEEPNORM_BETA = (8.0 * DEPTH) ** -0.25
N_EVEN = (DEPTH + 1) // 2
N_ODD = DEPTH // 2

SSD_D_INNER = D_MODEL
SSD_HEAD_DIM = 64
SSD_HEADS = SSD_D_INNER // SSD_HEAD_DIM
SSD_GROUPS = 8
SSD_HPG = SSD_HEADS // SSD_GROUPS
SSD_STATE = 128
SSD_CONV = 4
SSD_CHUNK = 128
SSD_CONV_DIM = SSD_D_INNER + 2 * SSD_GROUPS * SSD_STATE
SSD_DT_MIN = 1e-3
SSD_DT_MAX = 1e-1

GLA_HEADS = 4
GLA_DK = D_MODEL // 2
GLA_DV = D_MODEL
GLA_HEAD_DK = GLA_DK // GLA_HEADS
GLA_HEAD_DV = GLA_DV // GLA_HEADS
GLA_GATE_RANK = 16
GLA_GATE_TAU = 16.0
GLA_CHUNK = 64

HYB_SIZES = (SSD_D_INNER, SSD_CONV_DIM, SSD_HEADS, GLA_DK, GLA_DK, GLA_DV, GLA_GATE_RANK, GLA_DV)
HYB_IN_COLS = sum(HYB_SIZES)
HYB_MIX_WIDTH = SSD_D_INNER + GLA_DV

SWA_HEAD_DIM = 64
SWA_Q_HEADS = D_MODEL // SWA_HEAD_DIM
SWA_KV_HEADS = 8
SWA_GROUP = SWA_Q_HEADS // SWA_KV_HEADS
SWA_WINDOW = 128
SWA_Q_DIM = SWA_Q_HEADS * SWA_HEAD_DIM
SWA_KV_DIM = SWA_KV_HEADS * SWA_HEAD_DIM
SWA_QKV_COLS = SWA_Q_DIM + 2 * SWA_KV_DIM
ROPE_THETA = 500000.0
ROPE_DIM = SWA_HEAD_DIM // 4

D_FF = 5504
FFN_CONV = 3

kernel_name = 'hybrid_ssd_gla_swa_convffn_deepnorm'

def _split_points(sizes):
    pts, acc = [], 0
    for s in sizes[:-1]:
        acc += s
        pts.append(acc)
    return pts

def _pad_front(t, n):
    return jnp.pad(t, ((0, 0), (n, 0)) + ((0, 0),) * (t.ndim - 2))

def layer_norm(x, g, b):
    xf = x.astype(jnp.float32)
    mu = jnp.mean(xf, axis=-1, keepdims=True)
    var = jnp.mean(jnp.square(xf - mu), axis=-1, keepdims=True)
    return ((xf - mu) * lax.rsqrt(var + LN_EPS) * g + b).astype(x.dtype)

def rms_norm_groups(x, w, group):
    shp = x.shape
    xf = x.astype(jnp.float32).reshape(shp[:-1] + (shp[-1] // group, group))
    y = xf * lax.rsqrt(jnp.mean(jnp.square(xf), axis=-1, keepdims=True) + RMS_EPS)
    return (y.reshape(shp) * w).astype(x.dtype)

def causal_depthwise_conv(x, w, b):
    k_size = w.shape[0]
    length = x.shape[1]
    xp = jnp.pad(x, ((0, 0), (k_size - 1, 0), (0, 0)))
    y = b + w[0] * xp[:, 0:length]
    for kk in range(1, k_size):
        y = y + w[kk] * xp[:, kk:kk + length]
    return y

def partial_rotary(x, pos):
    half = ROPE_DIM // 2
    inv_freq = ROPE_THETA ** (-jnp.arange(half, dtype=jnp.float32) / half)
    ang = pos.astype(jnp.float32)[:, None] * inv_freq[None, :]
    cos = jnp.cos(ang)[None, :, None, :]
    sin = jnp.sin(ang)[None, :, None, :]
    x1, x2, rest = x[..., :half], x[..., half:ROPE_DIM], x[..., ROPE_DIM:]
    rot = jnp.concatenate([x1 * cos - x2 * sin, x2 * cos + x1 * sin], axis=-1).astype(x.dtype)
    return jnp.concatenate([rot, rest], axis=-1)

def ssd_chunked_scan(xs, dt, a, bm, cm):
    bsz, length, g, hg, p = xs.shape
    n = bm.shape[-1]
    q = SSD_CHUNK
    nc = length // q
    xd = (xs * dt[..., None]).reshape(bsz, nc, q, g, hg, p)
    a_cs = jnp.cumsum((dt * a).astype(jnp.float32).reshape(bsz, nc, q, g, hg), axis=2)
    bm = bm.reshape(bsz, nc, q, g, n)
    cm = cm.reshape(bsz, nc, q, g, n)
    seg = a_cs[:, :, :, None] - a_cs[:, :, None, :]
    causal = jnp.tril(jnp.ones((q, q), bool))[:, :, None, None]
    decay = jnp.exp(jnp.where(causal, seg, -jnp.inf))
    cb = jnp.einsum('bcign,bcjgn->bcijg', cm, bm)
    y_diag = jnp.einsum('bcijgh,bcjghp->bcighp', cb[..., None] * decay, xd)
    decay_to_end = jnp.exp(a_cs[:, :, -1:] - a_cs)
    states = jnp.einsum('bcjgn,bcjgh,bcjghp->bcghpn', bm, decay_to_end, xd)
    chunk_decay = jnp.exp(a_cs[:, :, -1])

    def step(h, inp):
        s, d = inp
        return h * d[..., None, None] + s, h

    h0 = jnp.zeros_like(states[:, 0])
    _, prev = lax.scan(step, h0, (jnp.moveaxis(states, 1, 0), jnp.moveaxis(chunk_decay, 1, 0)))
    prev = jnp.moveaxis(prev, 0, 1)
    y_off = jnp.einsum('bcign,bcghpn,bcigh->bcighp', cm, prev, jnp.exp(a_cs))
    return (y_diag + y_off).reshape(bsz, length, g, hg, p)

def gla_chunked(q, k, v, g):
    bsz, length, h, dk = q.shape
    dv = v.shape[-1]
    qs = GLA_CHUNK
    nc = length // qs

    def to_chunks(t):
        return jnp.moveaxis(t.reshape((bsz, nc, qs) + t.shape[2:]), 1, 0)

    gc = jnp.cumsum(to_chunks(g.astype(jnp.float32)), axis=2)
    causal = jnp.tril(jnp.ones((qs, qs), bool))[:, :, None, None]

    def step(s_state, inp):
        qi, ki, vi, gi = inp
        rel = gi[:, :, None] - gi[:, None, :]
        wdec = jnp.exp(jnp.where(causal, rel, -jnp.inf))
        scores = jnp.einsum('bihd,bjhd,bijhd->bhij', qi, ki, wdec)
        o = jnp.einsum('bhij,bjhv->bihv', scores, vi) + jnp.einsum('bihd,bhdv->bihv', qi * jnp.exp(gi), s_state)
        g_last = gi[:, -1]
        s_state = s_state * jnp.exp(g_last)[..., None] + jnp.einsum('bjhd,bjhv->bhdv', ki * jnp.exp(g_last[:, None] - gi), vi)
        return s_state, o

    s0 = jnp.zeros((bsz, h, dk, dv), jnp.float32)
    _, o = lax.scan(step, s0, (to_chunks(q), to_chunks(k), to_chunks(v), gc))
    return jnp.moveaxis(o, 0, 1).reshape(bsz, length, h, dv)

def ssd_gla_mixer(x, w_in, conv_w, conv_b, dt_bias, a_log, d_skip, ssd_norm_w, gate_w2, gate_b, gla_norm_w, w_out):
    bsz, length, _ = x.shape
    u = x @ w_in
    z, xbc, dt_raw, q, k, v, g_lr, r = jnp.split(u, _split_points(HYB_SIZES), axis=-1)
    xbc = jax.nn.silu(causal_depthwise_conv(xbc, conv_w, conv_b))
    xs, bm, cm = jnp.split(xbc, [SSD_D_INNER, SSD_D_INNER + SSD_GROUPS * SSD_STATE], axis=-1)
    xs = xs.reshape(bsz, length, SSD_GROUPS, SSD_HPG, SSD_HEAD_DIM)
    bm = bm.reshape(bsz, length, SSD_GROUPS, SSD_STATE)
    cm = cm.reshape(bsz, length, SSD_GROUPS, SSD_STATE)
    dt = jax.nn.softplus((dt_raw + dt_bias).astype(jnp.float32)).reshape(bsz, length, SSD_GROUPS, SSD_HPG)
    a = -jnp.exp(a_log.astype(jnp.float32)).reshape(SSD_GROUPS, SSD_HPG)
    pad = SSD_CHUNK - N_META
    y = ssd_chunked_scan(_pad_front(xs, pad), _pad_front(dt, pad), a, _pad_front(bm, pad), _pad_front(cm, pad))[:, pad:]
    y = y + xs * d_skip.reshape(SSD_GROUPS, SSD_HPG, 1)
    y = y.reshape(bsz, length, SSD_D_INNER).astype(x.dtype)
    y_ssd = rms_norm_groups(y * jax.nn.silu(z), ssd_norm_w, SSD_D_INNER // SSD_GROUPS)
    gk = jax.nn.log_sigmoid((g_lr @ gate_w2 + gate_b).astype(jnp.float32)) / GLA_GATE_TAU
    shp_k = (bsz, length, GLA_HEADS, GLA_HEAD_DK)
    qh = q.reshape(shp_k) * (GLA_HEAD_DK ** -0.5)
    kh = k.reshape(shp_k)
    vh = v.reshape(bsz, length, GLA_HEADS, GLA_HEAD_DV)
    gh = gk.reshape(shp_k)
    pad = GLA_CHUNK - N_META
    o = gla_chunked(_pad_front(qh, pad), _pad_front(kh, pad), _pad_front(vh, pad), _pad_front(gh, pad))[:, pad:]
    o = rms_norm_groups(o.reshape(bsz, length, GLA_DV).astype(x.dtype), gla_norm_w, GLA_HEAD_DV)
    y_gla = o * jax.nn.silu(r)
    return jnp.concatenate([y_ssd, y_gla], axis=-1) @ w_out

def swa_with_sinks(q, k, v, sinks):
    bsz, length = q.shape[:2]
    w = SWA_WINDOW
    nb = (length - N_META) // w
    scale = SWA_HEAD_DIM ** -0.5
    q = q.reshape(bsz, length, SWA_KV_HEADS, SWA_GROUP, SWA_HEAD_DIM)
    sink = sinks.astype(jnp.float32).reshape(SWA_KV_HEADS, SWA_GROUP)
    qm, km, vm = q[:, :N_META], k[:, :N_META], v[:, :N_META]
    s_mm = jnp.einsum('bqkgd,bskd->bkgqs', qm, km).astype(jnp.float32) * scale
    s_mm = jnp.where(jnp.tril(jnp.ones((N_META, N_META), bool)), s_mm, -jnp.inf)
    sink_m = jnp.broadcast_to(sink[None, :, :, None, None], s_mm.shape[:-1] + (1,))
    p_mm = jax.nn.softmax(jnp.concatenate([s_mm, sink_m], axis=-1), axis=-1)[..., :N_META]
    o_meta = jnp.einsum('bkgqs,bskd->bqkgd', p_mm, vm).reshape(bsz, N_META, SWA_Q_DIM)
    qb = q[:, N_META:].reshape(bsz, nb, w, SWA_KV_HEADS, SWA_GROUP, SWA_HEAD_DIM)
    kb = k[:, N_META:].reshape(bsz, nb, w, SWA_KV_HEADS, SWA_HEAD_DIM)
    vb = v[:, N_META:].reshape(bsz, nb, w, SWA_KV_HEADS, SWA_HEAD_DIM)

    def with_prev(t):
        prev = jnp.pad(t, ((0, 0), (1, 0), (0, 0), (0, 0), (0, 0)))[:, :-1]
        return jnp.concatenate([prev, t], axis=2)

    kw, vw = with_prev(kb), with_prev(vb)
    i = jnp.arange(w)[:, None]
    j = jnp.arange(2 * w)[None, :]
    band = (j > i) & (j <= i + w)
    first_ok = (jnp.arange(nb)[:, None, None] > 0) | (j >= w)[None]
    mask = (band[None] & first_ok)[None, :, None, None]
    s_w = jnp.einsum('bnqkgd,bnskd->bnkgqs', qb, kw).astype(jnp.float32) * scale
    s_w = jnp.where(mask, s_w, -jnp.inf)
    s_m = jnp.einsum('bnqkgd,bmkd->bnkgqm', qb, km).astype(jnp.float32) * scale
    sink_b = jnp.broadcast_to(sink[None, None, :, :, None, None], s_m.shape[:-1] + (1,))
    p = jax.nn.softmax(jnp.concatenate([s_m, s_w, sink_b], axis=-1), axis=-1)
    o = (jnp.einsum('bnkgqm,bmkd->bnqkgd', p[..., :N_META], vm)
         + jnp.einsum('bnkgqs,bnskd->bnqkgd', p[..., N_META:N_META + 2 * w], vw))
    o_real = o.reshape(bsz, nb * w, SWA_Q_DIM)
    return jnp.concatenate([o_meta, o_real], axis=1).astype(q.dtype)

def swa_mixer(x, w_qkv, sinks, w_out):
    bsz, length, _ = x.shape
    q, k, v = jnp.split(x @ w_qkv, [SWA_Q_DIM, SWA_Q_DIM + SWA_KV_DIM], axis=-1)
    pos = jnp.arange(length, dtype=jnp.int32)
    q = partial_rotary(q.reshape(bsz, length, SWA_Q_HEADS, SWA_HEAD_DIM), pos)
    k = partial_rotary(k.reshape(bsz, length, SWA_KV_HEADS, SWA_HEAD_DIM), pos)
    v = v.reshape(bsz, length, SWA_KV_HEADS, SWA_HEAD_DIM)
    return swa_with_sinks(q, k, v, sinks) @ w_out

def conv_glu_ffn(x, w_up, conv_w, conv_b, w_down):
    h = causal_depthwise_conv(x @ w_up, conv_w, conv_b)
    gate, val = jnp.split(h, 2, axis=-1)
    return (jax.nn.silu(gate) * val) @ w_down

def setup_inputs(seed: int = 0) -> dict:
    key = jax.random.key(seed)
    ks = jax.random.split(key, 24)

    def nrm(k, shape, s):
        return s * jax.random.normal(k, shape, jnp.float32)

    dt0 = jnp.exp(jax.random.uniform(ks[5], (N_EVEN, SSD_HEADS), jnp.float32, math.log(SSD_DT_MIN), math.log(SSD_DT_MAX)))
    return {
        'x': nrm(ks[0], (BATCH, SEQ, D_MODEL), 1.0),
        'meta_tokens': nrm(ks[1], (N_META, D_MODEL), 1.0),
        'hyb_w_in': nrm(ks[2], (N_EVEN, D_MODEL, HYB_IN_COLS), D_MODEL ** -0.5),
        'hyb_conv_w': nrm(ks[3], (N_EVEN, SSD_CONV, SSD_CONV_DIM), SSD_CONV ** -0.5),
        'hyb_conv_b': nrm(ks[4], (N_EVEN, SSD_CONV_DIM), 0.02),
        'ssd_dt_bias': dt0 + jnp.log(-jnp.expm1(-dt0)),
        'ssd_a_log': jnp.log(jax.random.uniform(ks[6], (N_EVEN, SSD_HEADS), jnp.float32, 1.0, 16.0)),
        'ssd_d': 1.0 + nrm(ks[7], (N_EVEN, SSD_HEADS), 0.1),
        'ssd_norm_w': 1.0 + nrm(ks[8], (N_EVEN, SSD_D_INNER), 0.05),
        'gla_gate_w2': nrm(ks[9], (N_EVEN, GLA_GATE_RANK, GLA_DK), GLA_GATE_RANK ** -0.5),
        'gla_gate_b': nrm(ks[10], (N_EVEN, GLA_DK), 0.1),
        'gla_norm_w': 1.0 + nrm(ks[11], (N_EVEN, GLA_DV), 0.05),
        'hyb_w_out': nrm(ks[12], (N_EVEN, HYB_MIX_WIDTH, D_MODEL), HYB_MIX_WIDTH ** -0.5 * DEEPNORM_BETA),
        'swa_w_qkv': nrm(ks[13], (N_ODD, D_MODEL, SWA_QKV_COLS), D_MODEL ** -0.5),
        'swa_sinks': nrm(ks[14], (N_ODD, SWA_Q_HEADS), 0.5),
        'swa_w_out': nrm(ks[15], (N_ODD, SWA_Q_DIM, D_MODEL), SWA_Q_DIM ** -0.5 * DEEPNORM_BETA),
        'ffn_w_up': nrm(ks[16], (DEPTH, D_MODEL, 2 * D_FF), D_MODEL ** -0.5),
        'ffn_conv_w': nrm(ks[17], (DEPTH, FFN_CONV, 2 * D_FF), FFN_CONV ** -0.5),
        'ffn_conv_b': nrm(ks[18], (DEPTH, 2 * D_FF), 0.02),
        'ffn_w_down': nrm(ks[19], (DEPTH, D_FF, D_MODEL), D_FF ** -0.5 * DEEPNORM_BETA),
        'ln_mix_g': 1.0 + nrm(ks[20], (DEPTH, D_MODEL), 0.05),
        'ln_mix_b': nrm(ks[21], (DEPTH, D_MODEL), 0.02),
        'ln_ffn_g': 1.0 + nrm(ks[22], (DEPTH, D_MODEL), 0.05),
        'ln_ffn_b': nrm(ks[23], (DEPTH, D_MODEL), 0.02),
    }

def reference(x, meta_tokens, hyb_w_in, hyb_conv_w, hyb_conv_b, ssd_dt_bias, ssd_a_log, ssd_d, ssd_norm_w,
              gla_gate_w2, gla_gate_b, gla_norm_w, hyb_w_out, swa_w_qkv, swa_sinks, swa_w_out,
              ffn_w_up, ffn_conv_w, ffn_conv_b, ffn_w_down, ln_mix_g, ln_mix_b, ln_ffn_g, ln_ffn_b):
    bsz = x.shape[0]
    meta = jnp.broadcast_to(meta_tokens.astype(x.dtype)[None], (bsz, N_META, D_MODEL))
    h = jnp.concatenate([meta, x], axis=1)
    for layer in range(DEPTH):
        j = layer // 2
        if layer % 2 == 0:
            mix = ssd_gla_mixer(h, hyb_w_in[j], hyb_conv_w[j], hyb_conv_b[j], ssd_dt_bias[j], ssd_a_log[j], ssd_d[j],
                                ssd_norm_w[j], gla_gate_w2[j], gla_gate_b[j], gla_norm_w[j], hyb_w_out[j])
        else:
            mix = swa_mixer(h, swa_w_qkv[j], swa_sinks[j], swa_w_out[j])
        h = layer_norm(DEEPNORM_ALPHA * h + mix, ln_mix_g[layer], ln_mix_b[layer])
        ffn = conv_glu_ffn(h, ffn_w_up[layer], ffn_conv_w[layer], ffn_conv_b[layer], ffn_w_down[layer])
        h = layer_norm(DEEPNORM_ALPHA * h + ffn, ln_ffn_g[layer], ln_ffn_b[layer])
    return h[:, N_META:]


_drawn_inputs = setup_inputs


def setup_inputs(seed=0):
    import zlib

    import numpy as np

    out = dict(_drawn_inputs(seed))
    spreads = {}
    factors = {'hyb_conv_b': 8.0,
     'ssd_d': 3.424,
     'ssd_norm_w': 4.56,
     'gla_gate_w2': 3.631,
     'gla_gate_b': 8.0,
     'gla_norm_w': 7.686,
     'swa_sinks': 24.158,
     'ffn_conv_b': 6.719}
    for name, (base, spread) in spreads.items():
        noise = np.random.default_rng([zlib.crc32(name.encode()), seed]).standard_normal(out[name].shape)
        drawn = base * np.exp(spread * noise) if base else spread * noise
        out[name] = __import__('jax').numpy.asarray(drawn.astype(out[name].dtype))
    for name, factor in factors.items():
        out[name] = (out[name] * factor).astype(out[name].dtype)
    return out
```

```python
from contextlib import ExitStack

import numpy as np

import concourse.bass as bass
from concourse import mybir

F32, F32R = mybir.dt.float32, mybir.dt.float32r
ALU, ACT, AX = mybir.AluOpType, mybir.ActivationFunctionType, mybir.AxisListType

D_MODEL, SEQ, N_META, DEPTH = 2048, 256, 16, 2
T = SEQ + N_META
P = 128
KT = D_MODEL // P
ALPHA = (2.0 * DEPTH) ** 0.25
LN_EPS, RMS_EPS = 1e-5, 1e-6

SSD_HEADS, SSD_GROUPS, SSD_HPG, SSD_P, SSD_N, SSD_TAPS = 32, 8, 4, 64, 128, 4
SSD_INNER = SSD_HEADS * SSD_P
SSD_CONV_DIM = SSD_INNER + 2 * SSD_GROUPS * SSD_N
GLA_HEADS, GLA_DK, GLA_DV, GLA_RANK, GLA_TAU = 4, 256, 512, 16, 16.0
SWA_Q_HEADS, SWA_KV_HEADS, SWA_D, SWA_WINDOW = 32, 8, 64, 128
ROPE_DIM, ROPE_THETA = SWA_D // 4, 500000.0
D_FF, FFN_TAPS = 5504, 3
FF_TILES = D_FF // P

M0, B1, B2 = (0, N_META), (N_META, N_META + P), (N_META + P, T)
RING = 3
LEVELS = [1, 2, 4, 8, 16, 32, 64]

SSD_PER, GLA_PER, SWA_PER = 6, 12, 6
FFN_PASSES = [(0, 15), (15, 14), (29, 14)]


def chunk_bases():
    at, base = 0, {}

    def take(name, n):
        nonlocal at
        base[name] = at
        at += n

    take("gates", 1)
    take("ssd", SSD_GROUPS * SSD_PER)
    take("ssd_out", KT)
    take("gla", GLA_HEADS * GLA_PER)
    take("gla_out", KT)
    for layer in range(DEPTH):
        if layer == 1:
            take("swa", SWA_PER * SWA_KV_HEADS // 2)
            take("swa_out", KT)
        for n, (_, tiles) in enumerate(FFN_PASSES):
            take(f"up{layer}{n}", 2 * tiles)
            take(f"down{layer}{n}", KT)
    return base, at


BASE, N_CHUNKS = chunk_bases()


class Chunks:

    def __init__(self, base, per, g):
        self.base, self.per, self.g = base, per, g

    def number(self, k):
        return self.base + k + self.g * self.per

    def slot(self, k):
        return (self.base + k) % RING if self.per % RING == 0 else (self.base + k + self.g * self.per) % RING

    def turn(self, k):
        if self.per % RING:
            return (self.base + k + self.g * self.per) // RING
        return (self.base + k) // RING + self.g * (self.per // RING)

    def first_turn(self, k):
        return isinstance(self.g, int) and self.base + k + self.per * self.g < RING


class Steps:

    def __init__(self, engine, sem):
        self.engine, self.sem, self.count, self.before, self.per, self.i = engine, sem, 0, 0, 0, None

    def __call__(self, ins):
        ins.then_inc(self.sem, 1)
        self.count += 1
        return self.count

    def after(self, step):
        self.engine.wait_ge(self.sem, self.before + step + (0 if self.i is None else self.i * self.per))

    def link(self, ins):
        self.after(self(ins))

    def loop(self, turns, per, body):
        outer = self.before + self.count
        with self.engine.Fori(0, turns) as i:
            self.before, self.count, self.per, self.i = outer, 0, per, i
            body(i)
            assert self.count == per, f"{self.count} steps in a body, not {per}"
        self.before, self.count, self.per, self.i = 0, outer + turns * per, 0, None


DVE_STEPS = {"ssd": 12, "gla": 34, "swa": 45, "up": 18}
ACT_STEPS = {"ssd": 0, "gla": 2, "swa": 0}


class Columns:

    def __init__(self, tile=None):
        self.tile, self.at, self.where = tile, 0, {}

    def take(self, name, n):
        self.where[name] = (self.at, n)
        self.at += n
        return self.tile[:, self.at - n:self.at] if self.tile is not None else None

    def __getitem__(self, name):
        a, n = self.where[name]
        return self.tile[:, a:a + n]


def table_columns(tile=None):
    t = Columns(tile)
    t.take("ssd_conv", SSD_GROUPS * 4 * 5)
    t.take("ssd_d", KT)
    t.take("ssd_norm", KT)
    t.take("gla_norm", KT)
    t.take("gate_b", GLA_HEADS * 2)
    t.take("ln", 4 * 2 * KT)
    t.take("ffn", DEPTH * FF_TILES * 8)
    t.take("sinks", SWA_Q_HEADS)
    t.take("dt_bias", 1)
    t.take("a_log", 1)
    return t


def mask_columns(layer, tile=None):
    t = Columns(tile)
    t.take("ident", P)
    if layer == 0:
        t.take("causal", 3 * P)
        t.take("causal_meta", T)
        t.take("levels", (1 + len(LEVELS)) * P)
    else:
        t.take("swap", P)
        t.take("cos", T)
        t.take("sin", T)
        t.take("window", 2 * T - P)
        t.take("window_meta", N_META)
    return t


TABLE_COLS = table_columns().at
MASK_COLS = max(mask_columns(0).at, mask_columns(1).at)


def trunk_kernel(nc, stream, h0, table, masks, gate_w2, out):
    ctx = ExitStack()
    with ctx:
        def sb(name, shape, dt=F32):
            return ctx.enter_context(nc.sbuf_tensor(name, shape, dt))

        def sem(name):
            return ctx.enter_context(nc.semaphore(name))

        raw = sb("raw", [P, RING, KT, P])
        w_hi = sb("w_hi", [P, RING, KT, P], F32R)
        w_lo = sb("w_lo", [P, RING, KT, P], F32R)
        res = sb("res", [P, KT, T])
        h_hi = sb("h_hi", [P, KT, T], F32R)
        h_lo = sb("h_lo", [P, KT, T], F32R)
        feat_hi = sb("feat_hi", [P, KT, T], F32R)
        feat_lo = sb("feat_lo", [P, KT, T], F32R)
        tab = sb("tab", [P, TABLE_COLS])
        msk = sb("msk", [P, MASK_COLS])
        ones = sb("ones", [P, P])
        eps = sb("eps", [P, 3])
        gate_w = sb("gate_w", [3 * GLA_RANK, GLA_DK])
        g_lr = sb("g_lr", [3 * GLA_RANK, T])
        SCRATCH = 9400
        scratch = sb("scratch", [P, SCRATCH])
        psum = ctx.enter_context(nc.psum_tensor("psum", [P, 8, 512], F32))
        banks = [psum[:, b, :] for b in range(8)]
        tb, mk0, mk1 = table_columns(tab), mask_columns(0, msk), mask_columns(1, msk)
        ident = mk0["ident"]
        ln_tab = tb["ln"].rearrange("p (l w n) -> p l w n", l=4, w=2)
        ffn_tab = tb["ffn"].rearrange("p (l n w) -> p l n w", l=DEPTH, n=FF_TILES)

        s = Columns(scratch)
        conv_out = s.take("conv_out", 4 * T).rearrange("p (k t) -> p k t", k=4)
        pre = s.take("pre", 2 * T).rearrange("p (k t) -> p k t", k=2)
        th = s.take("th", 2 * T).rearrange("p (k t) -> p k t", k=2)
        s_g1 = s.take("s_g1", 3 * P)
        s_g0 = s.take("s_g0", T)
        head_rows = s.take("head_rows", 4 * T).rearrange("p (h t) -> p h t", h=4)
        dec1 = s.take("dec1", 4 * 3 * P).rearrange("p (h t) -> p h t", h=4)
        dec0 = s.take("dec0", 4 * T).rearrange("p (h t) -> p h t", h=4)
        xd1 = s.take("xd1", 4 * P).rearrange("p (b f) -> p b f", b=2)
        xd0 = s.take("xd0", 2 * P)
        ssd_y = s.take("ssd_y", 2 * T).rearrange("p (k t) -> p k t", k=2)
        ssd_z = s.take("ssd_z", 2 * T).rearrange("p (k t) -> p k t", k=2)
        ssd_rstd = s.take("ssd_rstd", T)
        acs = s.take("acs", T)
        cols1 = s.take("cols1", 5 * 32)
        cols0 = s.take("cols0", 4 * 32)
        assert s.at <= SCRATCH, s.at
        th_z = pre
        gt = Columns(dec1.rearrange("p h t -> p (h t)"))
        dt_x, dt_e, dt_s, dt_s2, dt_p = (gt.take(n, T) for n in ("x", "e", "s", "s2", "p"))
        gt = Columns(dec0.rearrange("p h t -> p (h t)"))
        dt_v, to_end, to_end2, a_neg = (gt.take(n, w) for n, w in (("dt", T), ("te", T), ("te2", 16), ("an", 1)))

        s = Columns(scratch)
        q_g = s.take("q", 2 * T).rearrange("p (k t) -> p k t", k=2)
        k_g = s.take("k", 2 * T).rearrange("p (k t) -> p k t", k=2)
        cum = s.take("cum", 2 * T).rearrange("p (k t) -> p k t", k=2)
        g_z = s.take("g_z", 2 * T)
        g_e = s.take("g_e", 2 * T)
        z_q = s.take("z_q", 2 * T).rearrange("p (k t) -> p k t", k=2)
        z_k = s.take("z_k", 2 * T).rearrange("p (k t) -> p k t", k=2)
        dec = s.take("dec", 2 * T).rearrange("p (k t) -> p k t", k=2)
        a1 = s.take("a1", 3 * P)
        a0 = s.take("a0", T)
        a_tmp = s.take("a_tmp", T)
        vt1 = s.take("vt1", 2 * GLA_DV).rearrange("p (b f) -> p b f", b=2)
        vt0 = s.take("vt0", GLA_DV)
        o_g = s.take("o", 4 * T).rearrange("p (k t) -> p k t", k=4)
        r_g = s.take("r", 4 * T).rearrange("p (k t) -> p k t", k=4)
        o_sq = s.take("o_sq", T)
        o_rstd = a_tmp
        assert s.at <= SCRATCH, s.at
        vfm = g_e.rearrange("p (k t) -> p k t", k=2)
        th_r = g_z.rearrange("p (k t) -> p k t", k=2)
        exp_cum = th_r

        s = Columns(scratch)
        k_raw = s.take("k_raw", T)
        k_rot = s.take("k_rot", T)
        v_fm = s.take("v_fm", T)
        q_raw = s.take("q_raw", 2 * T).rearrange("p (k t) -> p k t", k=2)
        q_rot = s.take("q_rot", 2 * T).rearrange("p (k t) -> p k t", k=2)
        rot_c = s.take("rot_c", T)
        rot_s = s.take("rot_s", T)
        kv1 = s.take("kv1", 2 * P).rearrange("p (b f) -> p b f", b=2)
        kv0 = s.take("kv0", P)
        sc_w = s.take("sc_w", 2 * (2 * T - P)).rearrange("p (a t) -> p a t", a=2)
        sc_m = s.take("sc_m", 2 * N_META).rearrange("p (a t) -> p a t", a=2)
        neg_max, sums, sinks_e = (s.take(n, 6).rearrange("p (w a) -> p w a", a=2) for n in ("mx", "su", "sk"))
        p1 = s.take("p1", 2 * 3 * P).rearrange("p (a t) -> p a t", a=2)
        p0 = s.take("p0", 2 * T).rearrange("p (a t) -> p a t", a=2)
        o_f = s.take("o_f", T)
        assert s.at <= SCRATCH, s.at

        s = Columns(scratch)
        f_gate = s.take("f_gate", 2 * T).rearrange("p (k t) -> p k t", k=2)
        f_val = s.take("f_val", 2 * T).rearrange("p (k t) -> p k t", k=2)
        f_th = s.take("f_th", 2 * T).rearrange("p (k t) -> p k t", k=2)
        f_act = s.take("f_act", 2 * T).rearrange("p (k t) -> p k t", k=2)
        col_sum = s.take("col_sum", T)
        ln_mu = s.take("ln_mu", T)
        ln_rstd = s.take("ln_rstd", T)
        ln_sq = s.take("ln_sq", 8 * T).rearrange("p (b t) -> p b t", b=2)
        assert s.at <= SCRATCH, s.at

        const_in = sem("const_in")
        h0_in = sem("h0_in")
        mask1_in = sem("mask1_in")
        ones_set = sem("ones_set")
        halved = sem("halved")
        raw_in = [sem(f"raw_in{n}") for n in range(RING)]
        hi_ready = sem("hi_ready")
        lo_ready = sem("lo_ready")
        chunk_done = sem("chunk_done")
        bank_free = [sem(f"bank_free{n}") for n in range(RING)]
        h_ready = sem("h_ready")
        h_hi_ready = sem("h_hi_ready")
        feat_ready = sem("feat_ready")
        feat_hi_ready = sem("feat_hi_ready")
        dve_step, act_step = sem("dve_step"), sem("act_step")
        gates_exp, gates_rows, gates_turned, gates_cols, g_lr_ready = (sem(x) for x in (
            "gates_exp", "gates_rows", "gates_turned", "gates_cols", "g_lr_ready"))
        s_scaled, s_tanh, s_conv, s_scores, s_rows, s_bc, s_masked, s_diag, s_exp, s_mix = (sem("s_" + x) for x in (
            "scaled", "tanh", "conv", "scores", "rows", "bc", "masked", "diag", "exp", "mix"))
        s_xt, s_xd, s_y, s_ztanh, s_yread, s_yz, s_sq, s_stat, s_std, s_yn = (sem("s_" + x) for x in (
            "xt", "xd", "y", "ztanh", "yread", "yz", "sq", "stat", "std", "yn"))
        gw_in, g_mm, g_gexp, g_cum, g_sub, g_dec, g_zq, g_zend, g_sc, g_acc, g_scored, g_cross = (
            sem("g_" + x) for x in (
                "w_in", "mm", "gexp", "cum", "sub", "dec", "z", "zend", "sc", "acc", "scored", "cross"))
        g_vt, g_vcopy, g_rtanh, g_o, g_osb, g_sqr, g_st, g_std, g_yn = (sem("g_" + x) for x in (
            "vt", "vcopy", "rtanh", "o", "osb", "sqr", "st", "std", "yn"))
        a_raw, a_swap, a_rot, a_vt, a_vcopy, a_score, a_max, a_exp, a_norm, a_pt, a_p0, a_p1, a_o, a_of = (
            sem("a_" + x) for x in (
                "raw", "swap", "rot", "vt", "vcopy", "score", "max", "exp", "norm", "pt", "p0", "p1", "o", "of"))
        f_scaled, f_pair, f_tanh, f_mul = (sem("f_" + x) for x in ("scaled", "pair", "tanh", "mul"))
        l_sum, l_mean, l_mu, l_cent, l_sq, l_sqmm, l_std, l_norm = (sem("l_" + x) for x in (
            "sum", "mean", "mu", "cent", "sq", "sqmm", "std", "norm"))
        stored = sem("stored")

        block = ctx.enter_context(nc.Block())

        LN_OF = {"gla_out": 0, "down02": 1, "swa_out": 2, "down12": 3}
        OUT_PASSES = {"ssd_out": KT, "gla_out": KT, "swa_out": KT}
        for layer in range(DEPTH):
            for n, (_, tiles) in enumerate(FFN_PASSES):
                OUT_PASSES[f"down{layer}{n}"] = tiles

        FEAT = {}
        total = 0
        for name, n in [("ssd_out", SSD_GROUPS), ("gla_out", GLA_HEADS), ("swa_out", 0)]:
            FEAT[name] = (total, total + n)
            total += n
        for layer in range(DEPTH):
            if layer == 1:
                FEAT["swa_out"] = (total, total + KT)
                total += KT
            for n, (_, tiles) in enumerate(FFN_PASSES):
                FEAT[f"down{layer}{n}"] = (total, total + tiles)
                total += tiles

        def last_pass(name):
            return BASE[name] + KT == N_CHUNKS

        @block.sync
        def _(sp):
            sp.dma_start(tab[:, :], table).then_inc(const_in, 16)
            sp.dma_start(msk[:, 0:mk0.at], masks[0, :, 0:mk0.at]).then_inc(const_in, 16)

            def load(ch, k, width):
                if not ch.first_turn(k):
                    sp.wait_ge(lo_ready, ch.number(k) - (RING - 1))
                sl = ch.slot(k)
                sp.dma_start(raw[:, sl, 0:width, :].rearrange("p k n -> p (k n)"),
                             stream[ch.number(k), :, 0:width * P]).then_inc(raw_in[sl], 16)

            def load_run(base, n, width):
                whole = n // RING
                if whole > 1:
                    with sp.Fori(0, whole) as i:
                        for k in range(RING):
                            load(Chunks(base, RING, i), k, width)
                else:
                    whole = 0
                for k in range(whole * RING, n):
                    load(Chunks(base, RING, 0), k, width)

            load(Chunks(0, RING, 0), 0, KT)
            for g in range(4):
                sp.dma_start(res[:, 4 * g:4 * g + 4, :], h0[:, 4 * g:4 * g + 4, :]).then_inc(h0_in, 16)
            load(Chunks(0, RING, 0), 1, KT)
            load(Chunks(0, RING, 0), 2, KT)
            load_run(RING, BASE["up00"] - RING, KT)
            for layer in range(DEPTH):
                if layer == 1:
                    load_run(BASE["swa"], SWA_PER * SWA_KV_HEADS // 2 + KT, KT)
                for n, (_, tiles) in enumerate(FFN_PASSES):
                    load_run(BASE[f"up{layer}{n}"], 2 * tiles, KT)
                    load_run(BASE[f"down{layer}{n}"], KT, tiles)
            for g in range(4):
                sp.wait_ge(l_norm, 4 * 3 + g + 1)
                sp.dma_start(out[:, 4 * g:4 * g + 4, :], res[:, 4 * g:4 * g + 4, N_META:T]).then_inc(stored, 16)
            sp.wait_ge(stored, 64)

        @block.gpsimd
        def _(pool):
            pool.memset(ones[:, :], 1.0).then_inc(ones_set, 1)
            pool.memset(scratch[:, :], 0.0).then_inc(ones_set, 1)
            for n, v in enumerate((4 * RMS_EPS, RMS_EPS, LN_EPS)):
                pool.memset(eps[:, n:n + 1], v).then_inc(ones_set, 1)

            def gla(hd):
                ch = Chunks(BASE["gla"], GLA_PER, hd)
                if not isinstance(hd, int) or hd:
                    pool.wait_ge(g_mm, hd)
                pool.dma_start(gate_w[2 * GLA_RANK:, :], gate_w2[:, bass.ds(GLA_DK * hd, GLA_DK)]).then_inc(gw_in, 16)
                for k in range(4):
                    pool.wait_ge(bank_free[ch.slot(k)], ch.turn(k) + 1)
                for lv, half in enumerate(LEVELS):
                    lo, n = (0, T) if half < 16 else (N_META, 2 * P)
                    view = lambda x: x[:, :, lo:lo + n].rearrange("p k (n w) -> p k n w", w=2 * half)
                    pool.wait_ge(g_dec, 8 * hd + lv + 1)
                    if lv or not isinstance(hd, int) or hd:
                        pool.wait_ge(g_sc, 9 * hd + (lv + 1 if lv else 0))
                    pool.tensor_tensor(view(z_q)[:, :, :, half:], view(dec)[:, :, :, half:],
                                       view(q_g)[:, :, :, half:], ALU.mult)
                    pool.tensor_tensor(view(z_k)[:, :, :, 0:half], view(dec)[:, :, :, 0:half],
                                       view(k_g)[:, :, :, 0:half], ALU.mult).then_inc(g_zq, 1)
                pool.wait_ge(g_dec, 8 * hd + 8)
                pool.wait_ge(g_sc, 9 * hd + 8)
                pool.tensor_tensor(z_q[:, :, N_META:T], exp_cum[:, :, N_META:T], q_g[:, :, N_META:T], ALU.mult)
                pool.tensor_tensor(z_k[:, :, 0:B2[0]], dec[:, :, 0:B2[0]], k_g[:, :, 0:B2[0]],
                                   ALU.mult).then_inc(g_zq, 1)

            gla(0)
            with pool.Fori(0, GLA_HEADS - 1) as i:
                gla(i + 1)
            pool.wait_ge(g_scored, GLA_HEADS)
            pool.dma_start(msk[:, P:mk1.at], masks[1, :, P:mk1.at]).then_inc(mask1_in, 16)

        @block.scalar
        def _(act):
            step = Steps(act, act_step)
            A = nc.scalar.activation

            def split_hi(ch, k):
                sl = ch.slot(k)
                act.wait_ge(raw_in[sl], (ch.turn(k) + 1) * 16)
                if not ch.first_turn(k):
                    act.wait_ge(chunk_done, ch.number(k) - (RING - 1))
                A(w_hi[:, sl, :, :], raw[:, sl, :, :], ACT.Copy).then_inc(hi_ready, 1)

            def bank(ch, k):
                return banks[ch.slot(k)]

            act.wait_ge(h0_in, 64)
            for g in range(4):
                A(h_hi[:, 4 * g:4 * g + 4, :], res[:, 4 * g:4 * g + 4, :], ACT.Copy).then_inc(h_hi_ready, 1)
            c = Chunks(0, RING, 0)
            split_hi(c, 0)
            split_hi(c, 1)

            split_hi(c, 2)
            act.wait_ge(const_in, 32)
            act.wait_ge(ones_set, 5)
            H = SSD_HEADS
            act.wait_ge(chunk_done, 1)
            A(g_lr[H:H + GLA_RANK, :], banks[0][H:H + GLA_RANK, 0:T], ACT.Copy).then_inc(g_lr_ready, 1)
            A(dt_x[0:H, :], banks[0][0:H, 0:T], ACT.Identity, bias=tb["dt_bias"][0:H, :]).then_inc(bank_free[0], 1)
            act.wait_ge(bank_free[0], 1)
            step.link(A(dt_e[0:H, :], dt_x[0:H, :], ACT.Abs))
            A(a_neg[0:H, :], tb["a_log"][0:H, :], ACT.Exp).then_inc(gates_exp, 1)
            A(dt_e[0:H, :], dt_e[0:H, :], ACT.Exp, scale=-1.0).then_inc(gates_exp, 1)

            def ssd_conv(ch, k, g, t):
                split_hi(ch, k + 2)
                act.wait_ge(chunk_done, ch.number(k) + 1)
                n = 4 * g + t
                if t >= 2 or not isinstance(g, int) or g:
                    act.wait_ge(s_conv, n - 1)
                if t < 2 and (not isinstance(g, int) or g):
                    act.wait_ge(bank_free[ch.slot(k - 2)], ch.turn(k - 2) + 1)
                w = lambda j: tb["ssd_conv"][:, bass.ds(20 * g + 5 * t + j, 1)]
                A(pre[:, t % 2, :], bank(ch, k)[:, 0:T], ACT.Identity, bias=w(4), scale=w(3)).then_inc(s_scaled, 1)
                act.wait_ge(bank_free[ch.slot(k)], ch.turn(k) + 1)
                A(th[:, t % 2, :], pre[:, t % 2, :], ACT.Tanh).then_inc(s_tanh, 1)

            def ssd_heads(g, pair):
                for h in (2 * pair, 2 * pair + 1):
                    b = banks[5 + h % 2]
                    act.wait_ge(s_diag, 4 * g + h + 1)
                    col0 = lambda j: cols0[0:N_META, bass.ds(32 * j + 4 * g + h, 1)]
                    col1 = cols1[:, bass.ds(32 * 2 + 4 * g + h, 1)]
                    A(dec0[0:N_META, h, 0:N_META], dec0[0:N_META, h, 0:N_META], ACT.Exp)
                    A(dec1[:, h, :].rearrange("p (b t) -> p b t", b=3)[:, 0::2, :],
                      dec1[:, h, :].rearrange("p (b t) -> p b t", b=3)[:, 0::2, :], ACT.Exp)
                    A(dec0[0:N_META, h, B1[0]:B1[1]], b[0:N_META, B1[0]:B1[1]], ACT.Exp, bias=col0(1))
                    A(dec0[0:N_META, h, B2[0]:B2[1]], b[0:N_META, B2[0]:B2[1]], ACT.Exp, bias=col0(2))
                    A(dec1[:, h, P:2 * P], b[:, B2[0]:B2[1]], ACT.Exp, bias=col1).then_inc(s_exp, 1)

            def ssd_tail_a(g):
                act.wait_ge(s_yz, g + 1)
                A(ssd_z[:, :, :], ssd_y[:, :, :], ACT.Square).then_inc(s_sq, 1)

            def ssd_tail_b(g):
                act.wait_ge(s_stat, g + 1)
                A(ssd_rstd[:, :], banks[6][:, 0:T], ACT.Sqrt, scale=1.0 / (2 * P), bias=eps[:, 0:1]).then_inc(s_std, 1)
                act.wait_ge(s_yn, g + 1)
                A(feat_hi[:, bass.ds(2 * g, 2), :], ssd_y[:, :, :], ACT.Copy).then_inc(feat_hi_ready, 1)

            def ssd(g, first):
                ch = Chunks(BASE["ssd"], SSD_PER, g)
                ssd_conv(ch, 0, g, 0)
                if not first:
                    ssd_tail_a(g - 1)
                ssd_conv(ch, 1, g, 1)
                if not first:
                    ssd_tail_b(g - 1)
                ssd_conv(ch, 2, g, 2)
                ssd_heads(g, 0)
                ssd_conv(ch, 3, g, 3)
                ssd_heads(g, 1)
                for t in range(2):
                    split_hi(ch, 4 + t + 2)
                    act.wait_ge(chunk_done, ch.number(4 + t) + 1)
                    act.wait_ge(s_conv, 4 * g + t + 3)
                    A(th_z[:, t, :], bank(ch, 4 + t)[:, 0:T], ACT.Tanh, scale=0.5).then_inc(s_ztanh, 1)

            ssd(0, True)
            step.loop(SSD_GROUPS - 1, ACT_STEPS["ssd"], lambda i: ssd(i + 1, False))
            ssd_tail_a(SSD_GROUPS - 1)
            ssd_tail_b(SSD_GROUPS - 1)

            def out_pass(name):
                last = last_pass(name)
                base = BASE[name]
                split_hi(Chunks(base, RING, 0), 2)

                def body(i):
                    for k in range(RING):
                        split_hi(Chunks(base + 1, RING, i), k + 2)

                turns = KT // RING - last
                step.loop(turns, 0, body)
                if last:
                    split_hi(Chunks(base + 1, RING, turns), 0 + 2)

            out_pass("ssd_out")

            def gla_level(hd, lv):
                half = LEVELS[lv]
                lo = 0 if half < 16 else N_META
                act.wait_ge(g_sub, 7 * hd + lv + 1)
                A(dec[:, :, lo:T], dec[:, :, lo:T], ACT.Exp).then_inc(g_dec, 1)

            def gla_tail(hd):
                for j in range(4):
                    act.wait_ge(g_o, 4 * hd + j + 1)
                    if j or not isinstance(hd, int) or hd:
                        act.wait_ge(g_st, 4 * hd + j)
                    A(o_sq[:, :], banks[5 + j % 2][:, 0:T], ACT.Square).then_inc(g_sqr, 1)
                    A(o_g[:, j, :], banks[5 + j % 2][:, 0:T], ACT.Copy).then_inc(g_osb, 1)
                act.wait_ge(g_st, 4 * hd + 4)
                A(o_rstd[:, :], banks[7][:, 0:T], ACT.Sqrt, scale=1.0 / GLA_DV, bias=eps[:, 1:2]).then_inc(g_std, 1)

            def gla_tail_b(hd):
                act.wait_ge(g_yn, hd + 1)
                A(feat_hi[:, bass.ds(4 * hd, 4), :], o_g[:, :, :], ACT.Copy).then_inc(feat_hi_ready, 1)

            def gla(hd, first):
                ch = Chunks(BASE["gla"], GLA_PER, hd)
                for k in range(GLA_PER):
                    split_hi(ch, k + 2)
                    act.wait_ge(chunk_done, ch.number(k) + 1)
                    if k < 2:
                        if k == 0 and not first:
                            act.wait_ge(g_sc, 9 * hd)
                        A(q_g[:, k, :], bank(ch, k)[:, 0:T], ACT.Copy,
                          scale=float(GLA_DK) ** -0.5).then_inc(bank_free[ch.slot(k)], 1)
                        if k == 0:
                            act.wait_ge(g_mm, hd + 1)
                            if not first:
                                act.wait_ge(g_zend, hd)
                            for t in range(2):
                                last = step(A(g_z.rearrange("p (k t) -> p k t", k=2)[:, t, :], banks[3 + t][:, 0:T],
                                              ACT.Identity, bias=tb["gate_b"][:, bass.ds(2 * hd + t, 1)]))
                            step.after(last)
                            A(g_e, g_z, ACT.Abs).then_inc(g_gexp, 1)
                            act.wait_ge(g_gexp, 2 * hd + 1)
                            A(g_e, g_e, ACT.Exp, scale=-1.0).then_inc(g_gexp, 1)
                            if not first:
                                gla_tail(hd - 1)
                        if k == 1 and not first:
                            gla_tail_b(hd - 1)
                    elif k < 4:
                        A(k_g[:, k - 2, :], bank(ch, k)[:, 0:T], ACT.Copy).then_inc(bank_free[ch.slot(k)], 1)
                        if k == 3:
                            gla_level(hd, 0)
                    elif k < 8:
                        j = k - 4
                        if j >= 2 or not first:
                            act.wait_ge(g_vt, 4 * hd + j - 1)
                        A(vfm[:, j % 2, :], bank(ch, k)[:, 0:T], ACT.Copy).then_inc(bank_free[ch.slot(k)], 1)
                        gla_level(hd, k - 3)
                    else:
                        j = k - 8
                        if j >= 2:
                            act.wait_ge(bank_free[ch.slot(k - 2)], ch.turn(k - 2) + 1)
                        A(th_r[:, j % 2, :], bank(ch, k)[:, 0:T], ACT.Tanh, scale=0.5).then_inc(g_rtanh, 1)
                        if k < 10:
                            gla_level(hd, k - 3)
                        if k == 11:
                            act.wait_ge(bank_free[ch.slot(k)], ch.turn(k) + 1)
                            act.wait_ge(g_zq, 8 * hd + 7)
                            A(exp_cum[:, :, :], cum[:, :, :], ACT.Exp)
                            for t in range(2):
                                for n, (lo, hi) in enumerate((M0, B1)):
                                    ins = A(dec[:, t, lo:hi], cum[:, t, lo:hi], ACT.Exp, scale=-1.0,
                                            bias=cum[:, t, hi - 1:hi])
                            ins.then_inc(g_dec, 1)
                act.wait_ge(g_sc, 9 * hd + 9)
                A(a1[:, P:2 * P], banks[3][:, 0:P], ACT.Copy)
                A(a0[0:N_META, N_META:T], banks[3][0:N_META, P:3 * P], ACT.Copy).then_inc(g_cross, 1)

            gla(0, True)
            step.loop(GLA_HEADS - 1, ACT_STEPS["gla"], lambda i: gla(i + 1, False))
            gla_tail(GLA_HEADS - 1)
            gla_tail_b(GLA_HEADS - 1)
            out_pass("gla_out")

            def layer_norm(n, last):
                act.wait_ge(l_mean, n + 1)
                A(ln_mu[:, :], banks[3][:, 0:T], ACT.Copy, scale=1.0 / D_MODEL).then_inc(l_mu, 1)
                for g in range(4):
                    act.wait_ge(l_cent, 4 * n + g + 1)
                    if g >= 2 or n:
                        act.wait_ge(l_sqmm, 4 * n + g - 1)
                    A(ln_sq[:, g % 2, :], res[:, 4 * g:4 * g + 4, :].rearrange("p k t -> p (k t)"),
                      ACT.Square).then_inc(l_sq, 1)
                act.wait_ge(l_sqmm, 4 * n + 4)
                A(ln_rstd[:, :], banks[4][:, 0:T], ACT.Sqrt, scale=1.0 / D_MODEL, bias=eps[:, 2:3]).then_inc(l_std, 1)
                if not last:
                    for g in range(4):
                        act.wait_ge(l_norm, 4 * n + g + 1)
                        A(h_hi[:, 4 * g:4 * g + 4, :], res[:, 4 * g:4 * g + 4, :], ACT.Copy).then_inc(h_hi_ready, 1)

            def ffn_pairs(layer, base, tile0, first_pair, pairs, i, per_pair_total):
                ch = Chunks(base, 2 * pairs, i)
                for j in range(pairs):
                    q = i * pairs + j
                    n = q + per_pair_total
                    tile = q + tile0
                    for w in range(2):
                        k = 2 * j + w
                        split_hi(ch, k + 2)
                        act.wait_ge(chunk_done, ch.number(k) + 1)
                        if w == 0 and j >= 2:
                            act.wait_ge(f_mul, n - 1)
                        elif w == 0 and j == 0 and (not isinstance(n, int) or n):
                            act.wait_ge(f_mul, n)
                        dst = (f_gate, f_val)[w]
                        A(dst[:, j % 2, :], bank(ch, k)[:, 0:T], ACT.Identity,
                          bias=ffn_tab[:, layer, bass.ds(tile, 1), 4 * w + 3],
                          scale=ffn_tab[:, layer, bass.ds(tile, 1), 4 * w + 2]).then_inc(f_scaled, 1)
                        if w == 0:
                            act.wait_ge(bank_free[ch.slot(k)], ch.turn(k) + 1)
                            A(f_th[:, j % 2, :], f_gate[:, j % 2, :], ACT.Tanh).then_inc(f_tanh, 1)
                    act.wait_ge(f_mul, n + 1)
                    A(feat_hi[:, bass.ds(q + first_pair, 1), :], f_act[:, j % 2:j % 2 + 1, :],
                      ACT.Copy).then_inc(feat_hi_ready, 1)

            def ffn(layer):
                for n, (tile0, tiles) in enumerate(FFN_PASSES):
                    total = layer * FF_TILES + tile0
                    up_run(layer, n, tile0, tiles, total)
                    out_pass(f"down{layer}{n}")

            def up_run(layer, n, tile0, tiles, total):
                base = BASE[f"up{layer}{n}"]
                bodies = tiles // 6
                step.loop(bodies, 0, lambda i: ffn_pairs(layer, base, tile0, 0, 6, i, total))
                rest = tiles - 6 * bodies
                if rest:
                    done = 6 * bodies
                    ffn_pairs(layer, base + 2 * done, tile0 + done, done, rest, 0, total + done)

            layer_norm(0, False)
            ffn(0)
            layer_norm(1, False)

            def swa_exp(n):
                act.wait_ge(a_max, n + 1)
                for a in range(2):
                    A(sc_w[:, a, 0:N_META + P], sc_w[:, a, 0:N_META + P], ACT.Exp, bias=neg_max[:, 0, a:a + 1],
                      accum_out=sums[:, 0, a:a + 1])
                    A(sc_w[:, a, N_META + P:], sc_w[:, a, N_META + P:], ACT.Exp, bias=neg_max[:, 1, a:a + 1],
                      accum_out=sums[:, 1, a:a + 1])
                    A(sc_m[0:N_META, a, :], sc_m[0:N_META, a, :], ACT.Exp, bias=neg_max[0:N_META, 2, a:a + 1],
                      accum_out=sums[0:N_META, 2, a:a + 1])
                A(sinks_e[:, :, :], sinks_e[:, :, :], ACT.Exp).then_inc(a_exp, 1)

            def swa_p0(n):
                for a in range(2):
                    act.wait_ge(a_pt, 2 * n + a + 1)
                    A(p0[0:N_META, a, :], banks[5][0:N_META, 0:T], ACT.Copy).then_inc(a_p0, 1)

            def swa_out(n):
                act.wait_ge(a_o, n + 1)
                A(o_f[:, :], banks[7][:, 0:T], ACT.Copy).then_inc(a_of, 1)
                act.wait_ge(a_of, n + 1)
                A(feat_hi[:, bass.ds(n, 1), :], o_f[:, :].unsqueeze(1), ACT.Copy).then_inc(feat_hi_ready, 1)

            def swa_slot(m, k, has_before, has_own):
                for stage, lag in ((swa_out, 6), (swa_p0, 5), (swa_exp, 4)):
                    r = k - lag
                    if r >= 0 and has_own:
                        stage(4 * m + r)
                    elif 0 <= r + SWA_PER < 4 and has_before:
                        stage(4 * m + (r + SWA_PER - 4))

            def swa(m, first):
                ch = Chunks(BASE["swa"], SWA_PER, m)
                for k in range(SWA_PER):
                    split_hi(ch, k + 2)
                    act.wait_ge(chunk_done, ch.number(k) + 1)
                    if k == 0:
                        if not first:
                            act.wait_ge(a_rot, 5 * m - 4)
                        A(k_raw[:, :], bank(ch, k)[:, 0:T], ACT.Copy).then_inc(a_raw, 1)
                    elif k == 1:
                        if not first:
                            act.wait_ge(a_vt, m)
                        A(v_fm[:, :], bank(ch, k)[:, 0:T], ACT.Copy).then_inc(bank_free[ch.slot(k)], 1)
                    else:
                        r = k - 2
                        if r >= 2:
                            act.wait_ge(a_rot, 5 * m + r)
                        elif not first:
                            act.wait_ge(a_rot, 5 * m + (r - 1))
                        A(q_raw[:, r % 2, :], bank(ch, k)[:, 0:T], ACT.Copy,
                          scale=float(SWA_D) ** -0.5).then_inc(a_raw, 1)
                    swa_slot(m, k, not first, True)

            swa(0, True)
            step.loop(SWA_KV_HEADS // 2 - 1, ACT_STEPS["swa"], lambda i: swa(i + 1, False))
            for k in range(4):
                swa_slot(SWA_KV_HEADS // 2, k, True, False)
            out_pass("swa_out")
            layer_norm(2, False)
            ffn(1)
            layer_norm(3, True)

        @block.vector
        def _(dve):
            step = Steps(dve, dve_step)
            V = nc.vector
            TT, TS, STT = V.tensor_tensor, V.tensor_scalar, V.scalar_tensor_tensor

            def split_lo(ch, k):
                sl = ch.slot(k)
                dve.wait_ge(hi_ready, ch.number(k) + 1)
                TT(w_lo[:, sl, :, :], raw[:, sl, :, :], w_hi[:, sl, :, :].bitcast(F32),
                   ALU.subtract).then_inc(lo_ready, 1)

            def bank(ch, k):
                return banks[ch.slot(k)]

            def half_log1p_start(e, s_, s2, p):
                step.link(TS(s_, e, 2.0, None, ALU.add))
                step.link(V.reciprocal(s_, s_))
                step.link(TT(s_, s_, e, ALU.mult))
                step.link(TT(s2, s_, s_, ALU.mult))
                step.link(TS(p, s2, 1.0 / 15, None, ALU.mult))

            def half_log1p_end(s_, s2, p):
                for n in (13, 11, 9, 7, 5, 3):
                    step.link(STT(p, p, 1.0 / n, s2, ALU.add, ALU.mult))
                step.link(STT(p, p, 1.0, s_, ALU.add, ALU.mult))

            for g in range(4):
                dve.wait_ge(h_hi_ready, g + 1)
                TT(h_lo[:, 4 * g:4 * g + 4, :], res[:, 4 * g:4 * g + 4, :],
                   h_hi[:, 4 * g:4 * g + 4, :].bitcast(F32), ALU.subtract).then_inc(h_ready, 1)
            c = Chunks(0, RING, 0)
            split_lo(c, 0)
            split_lo(c, 1)

            dve.wait_ge(const_in, 32)
            dve.wait_ge(ones_set, 5)
            TS(tb["ssd_conv"], tb["ssd_conv"], 0.5, None, ALU.mult).then_inc(halved, 1)
            TS(tb["gla_norm"], tb["gla_norm"], 0.5, None, ALU.mult).then_inc(halved, 1)
            gates_half = tb["ffn"].rearrange("p (n w) -> p n w", w=8)[:, :, 0:4]
            TS(gates_half, gates_half, 0.5, None, ALU.mult).then_inc(halved, 1)

            split_lo(c, 2)
            H = SSD_HEADS
            dve.wait_ge(gates_exp, 2)
            half_log1p_start(dt_e[0:H, :], dt_s[0:H, :], dt_s2[0:H, :], dt_p[0:H, :])
            half_log1p_end(dt_s[0:H, :], dt_s2[0:H, :], dt_p[0:H, :])
            step.link(TS(dt_s[0:H, :], dt_x[0:H, :], 0.0, None, ALU.max))
            step.link(STT(dt_v[0:H, :], dt_p[0:H, :], 2.0, dt_s[0:H, :], ALU.mult, ALU.add))
            step.link(TS(dt_e[0:H, :], dt_v[0:H, :], a_neg[0:H, :], -1.0, ALU.mult, ALU.mult))
            for lo, hi in (M0, B1, B2):
                last = step(V.tensor_tensor_scan(acs[0:H, lo:hi], ones[0:H, 0:hi - lo], dt_e[0:H, lo:hi], 0.0,
                                                 ALU.mult, ALU.add))
            step.after(last)
            for lo, hi in (M0, B1):
                last = step(TS(to_end[0:H, lo:hi], acs[0:H, lo:hi], acs[0:H, hi - 1:hi], -1.0,
                               ALU.subtract, ALU.mult))
            step.after(last)
            TS(to_end2[0:H, :], to_end[0:H, M0[0]:M0[1]], acs[0:H, B1[1] - 1:B1[1]], None,
               ALU.add).then_inc(gates_rows, 1)
            dve.wait_ge(gates_turned, 1)
            step(V.tensor_copy(cols1[:, :], banks[3][:, 0:160]))
            V.tensor_copy(cols0[0:N_META, :], banks[3][0:N_META, 160:288]).then_inc(gates_cols, 1)
            dve.wait_ge(gates_cols, 1)

            def ssd_conv(ch, k, g, t):
                split_lo(ch, k + 2)
                u, y = bank(ch, k), pre[:, t % 2, :]
                dve.wait_ge(s_scaled, 4 * g + t + 1)
                w = lambda j: tb["ssd_conv"][:, bass.ds(20 * g + 5 * t + j, 1)]
                step.link(STT(y[:, 1:], u[:, 0:T - 1], w(2), y[:, 1:], ALU.mult, ALU.add))
                step.link(STT(y[:, 2:], u[:, 0:T - 2], w(1), y[:, 2:], ALU.mult, ALU.add))
                STT(y[:, 3:], u[:, 0:T - 3], w(0), y[:, 3:], ALU.mult, ALU.add).then_inc(bank_free[ch.slot(k)], 1)
                dve.wait_ge(s_tanh, 4 * g + t + 1)
                STT(conv_out[:, t, :], th[:, t % 2, :], 1.0, y, ALU.add, ALU.mult).then_inc(s_conv, 1)

            def ssd_heads(g, pair):
                for h in (2 * pair, 2 * pair + 1):
                    b = banks[5 + h % 2]
                    dve.wait_ge(s_bc, 4 * g + h + 1)
                    TS(dec0[0:N_META, h, 0:N_META], b[0:N_META, 0:N_META], cols0[0:N_META, bass.ds(4 * g + h, 1)],
                       0.0, ALU.subtract, ALU.min)
                    TS(dec1[:, h, 0:P], b[:, B1[0]:B1[1]], cols1[:, bass.ds(4 * g + h, 1)],
                       0.0, ALU.subtract, ALU.min)
                    TS(dec1[:, h, 2 * P:3 * P], b[:, B2[0]:B2[1]], cols1[:, bass.ds(32 + 4 * g + h, 1)],
                       0.0, ALU.subtract, ALU.min).then_inc(s_diag, 1)
                for h in (2 * pair, 2 * pair + 1):
                    dve.wait_ge(s_exp, 4 * g + h + 1)
                    TT(dec0[0:N_META, h, :], dec0[0:N_META, h, :], s_g0[0:N_META, :], ALU.mult)
                    TT(dec1[:, h, :], dec1[:, h, :], s_g1[:, :], ALU.mult).then_inc(s_mix, 1)

            def ssd_tail_a(g):
                dve.wait_ge(s_y, 2 * g + 2)
                for t in range(2):
                    ins = STT(ssd_y[:, t, :], conv_out[:, 2 + t, :], tb["ssd_d"][:, bass.ds(2 * g + t, 1)],
                              banks[(7, 5)[t]][:, 0:T], ALU.mult, ALU.add)
                ins.then_inc(s_yread, 1)
                dve.wait_ge(s_yread, g + 1)
                TT(ssd_y[:, :, :], ssd_y[:, :, :], ssd_z[:, :, :], ALU.mult).then_inc(s_yz, 1)

            def ssd_tail_b(g):
                dve.wait_ge(s_std, g + 1)
                step.link(V.reciprocal(ssd_rstd[:, :], ssd_rstd[:, :]))
                for t in range(2):
                    ins = STT(ssd_y[:, t, :], ssd_y[:, t, :], tb["ssd_norm"][:, bass.ds(2 * g + t, 1)],
                              ssd_rstd[:, :], ALU.mult, ALU.mult)
                ins.then_inc(s_yn, 1)
                dve.wait_ge(feat_hi_ready, g + 1)
                TT(feat_lo[:, bass.ds(2 * g, 2), :], ssd_y[:, :, :], feat_hi[:, bass.ds(2 * g, 2), :].bitcast(F32),
                   ALU.subtract).then_inc(feat_ready, 1)

            def ssd(g, first):
                ch = Chunks(BASE["ssd"], SSD_PER, g)
                ssd_conv(ch, 0, g, 0)
                if not first:
                    ssd_tail_a(g - 1)
                ssd_conv(ch, 1, g, 1)
                TT(head_rows[0:H, :, :], acs[0:H, :].unsqueeze(1).broadcast_to([H, 4, T]),
                   ident[0:H, bass.ds(4 * g, 4)].unsqueeze(2).broadcast_to([H, 4, T]), ALU.mult).then_inc(s_rows, 1)
                if not first:
                    ssd_tail_b(g - 1)
                ssd_conv(ch, 2, g, 2)
                dve.wait_ge(s_scores, g + 1)
                step(TT(s_g0[0:N_META, :], banks[3][0:N_META, 0:T], mk0["causal_meta"][0:N_META, :], ALU.mult))
                TT(s_g1[:, :], banks[4][:, 0:3 * P], mk0["causal"], ALU.mult).then_inc(s_masked, 1)
                dve.wait_ge(s_masked, g + 1)
                ssd_heads(g, 0)
                ssd_conv(ch, 3, g, 3)
                ssd_heads(g, 1)
                for t in range(2):
                    split_lo(ch, 4 + t + 2)
                    dve.wait_ge(s_ztanh, 2 * g + t + 1)
                    STT(ssd_z[:, t, :], th_z[:, t, :], 1.0, bank(ch, 4 + t)[:, 0:T], ALU.add,
                        ALU.mult).then_inc(bank_free[ch.slot(4 + t)], 1)
                    if t == 0:
                        dve.wait_ge(s_xt, g + 1)
                        for b in range(2):
                            step(TT(xd1[:, b, :].rearrange("p (h d) -> p h d", h=4),
                                    banks[3][:, 256 * b:256 * b + 256].rearrange("p (h d) -> p h d", h=4),
                                    cols1[:, bass.ds(96 + 32 * b + 4 * g, 4)].unsqueeze(2).broadcast_to([P, 4, SSD_P]),
                                    ALU.mult))
                        TT(xd0[0:N_META, :].rearrange("p (h d) -> p h d", h=4),
                           banks[4][0:N_META, 0:256].rearrange("p (h d) -> p h d", h=4),
                           cols0[0:N_META, bass.ds(96 + 4 * g, 4)].unsqueeze(2).broadcast_to([N_META, 4, SSD_P]),
                           ALU.mult).then_inc(s_xd, 1)

            ssd(0, True)
            step.loop(SSD_GROUPS - 1, DVE_STEPS["ssd"], lambda i: ssd(i + 1, False))
            ssd_tail_a(SSD_GROUPS - 1)
            ssd_tail_b(SSD_GROUPS - 1)

            def out_pass(name, scale):
                base, last, ln = BASE[name], last_pass(name), LN_OF.get(name)

                def one(ch, k, n, first=False):
                    if not (last and isinstance(n, int) and n >= KT - 2):
                        split_lo(ch, k + 2)
                    dve.wait_ge(chunk_done, ch.number(k) + 1)
                    r = res[:, bass.ds(n, 1), :]
                    ps = bank(ch, k)[:, 0:T].unsqueeze(1)
                    if scale:
                        STT(r, r, ALPHA, ps, ALU.mult, ALU.add).then_inc(bank_free[ch.slot(k)], 1)
                    else:
                        TT(r, r, ps, ALU.add).then_inc(bank_free[ch.slot(k)], 1)
                    if ln is not None:
                        dve.wait_ge(bank_free[ch.slot(k)], ch.turn(k) + 1)
                        cs = col_sum[:, :].unsqueeze(1)
                        if first:
                            V.tensor_copy(cs, r).then_inc(l_sum, 1)
                        else:
                            TT(cs, cs, r, ALU.add).then_inc(l_sum, 1)
                        dve.wait_ge(l_sum, n + (KT * ln + 1))

                one(Chunks(base, RING, 0), 0, 0, True)
                turns = KT // RING - last

                def body(i):
                    for k in range(RING):
                        one(Chunks(base + 1, RING, i), k, i * RING + (k + 1))

                step.loop(turns, 0, body)
                if last:
                    for k in range(RING):
                        one(Chunks(base + 1, RING, turns), k, turns * RING + k + 1)

            out_pass("ssd_out", True)

            def gla_sub(hd, lv):
                half = LEVELS[lv]
                lo, n = (0, T) if half < 16 else (N_META, 2 * P)
                view = lambda x: x[:, :, lo:lo + n].rearrange("p k (n w) -> p k n w", w=2 * half)
                ref = view(cum)[:, :, :, half - 1:half].broadcast_to([P, 2, n // (2 * half), half])
                if lv:
                    dve.wait_ge(g_zq, 8 * hd + lv)
                TT(view(dec)[:, :, :, half:], view(cum)[:, :, :, half:], ref, ALU.subtract)
                TT(view(dec)[:, :, :, 0:half], ref, view(cum)[:, :, :, 0:half], ALU.subtract).then_inc(g_sub, 1)

            def gla_acc(hd, lv):
                b = banks[3 + lv % 2]
                dve.wait_ge(g_sc, 9 * hd + lv + 1)
                mask = mk0["levels"][:, lv * P:(lv + 1) * P]
                diag = a1.rearrange("p (b t) -> p b t", b=3)[:, 0::2, :]
                both = b[:, 0:2 * P].rearrange("p (b t) -> p b t", b=2)
                mask2 = mask.unsqueeze(1).broadcast_to([P, 2, P])
                tmp = a_tmp[:, 0:2 * P].rearrange("p (b t) -> p b t", b=2)
                if lv == 0:
                    step(TT(a0[0:N_META, 0:N_META], b[0:N_META, 2 * P:T], mask[0:N_META, 0:N_META], ALU.mult))
                    TT(diag, both, mask2, ALU.mult).then_inc(g_acc, 1)
                    dve.wait_ge(g_acc, 8 * hd + 1)
                    return
                meta = lv > 0 and LEVELS[lv - 1] < 16
                if meta:
                    step(TT(a_tmp[0:N_META, 2 * P:T], b[0:N_META, 2 * P:T], mask[0:N_META, 0:N_META], ALU.mult))
                TT(tmp, both, mask2, ALU.mult).then_inc(g_acc, 1)
                dve.wait_ge(g_acc, 8 * hd + lv + 1)
                if meta:
                    step(TT(a0[0:N_META, 0:N_META], a0[0:N_META, 0:N_META], a_tmp[0:N_META, 2 * P:T], ALU.add))
                ins = TT(diag, diag, tmp, ALU.add)
                if lv == len(LEVELS):
                    ins.then_inc(g_scored, 1)
                else:
                    step.link(ins)

            def gla_tail(hd):
                dve.wait_ge(g_std, hd + 1)
                step.link(V.reciprocal(o_rstd[:, :], o_rstd[:, :]))
                for j in range(4):
                    last = step(STT(o_g[:, j, :], o_g[:, j, :], tb["gla_norm"][:, bass.ds(4 * hd + j, 1)],
                                    o_rstd[:, :], ALU.mult, ALU.mult))
                step.after(last)
                TT(o_g[:, :, :], o_g[:, :, :], r_g[:, :, :], ALU.mult).then_inc(g_yn, 1)
                dve.wait_ge(feat_hi_ready, SSD_GROUPS + hd + 1)
                TT(feat_lo[:, bass.ds(4 * hd, 4), :], o_g[:, :, :], feat_hi[:, bass.ds(4 * hd, 4), :].bitcast(F32),
                   ALU.subtract).then_inc(feat_ready, 1)

            def gla(hd, first):
                ch = Chunks(BASE["gla"], GLA_PER, hd)
                for k in range(GLA_PER):
                    split_lo(ch, k + 2)
                    if k == 0:
                        f = lambda x: x.rearrange("p k t -> p (k t)")
                        dve.wait_ge(g_gexp, 2 * hd + 2)
                        if not first:
                            dve.wait_ge(g_sc, 9 * hd)
                        half_log1p_start(g_e, f(dec), f(z_q), f(z_k))
                    if k == 1:
                        half_log1p_end(f(dec), f(z_q), f(z_k))
                        step.link(TS(g_e, g_z, 0.0, 1.0 / GLA_TAU, ALU.min, ALU.mult))
                        step.link(STT(g_e, f(z_k), -2.0 / GLA_TAU, g_e, ALU.mult, ALU.add))
                        g2 = g_e.rearrange("p (k t) -> p k t", k=2)
                        for t in range(2):
                            for lo, hi in (M0, B1, B2):
                                ins = V.tensor_tensor_scan(cum[:, t, lo:hi], ones[:, 0:hi - lo], g2[:, t, lo:hi], 0.0,
                                                           ALU.mult, ALU.add)
                        ins.then_inc(g_cum, 1)
                        dve.wait_ge(g_cum, hd + 1)
                    if k == 1 and not first:
                        gla_tail(hd - 1)
                    if k == 2:
                        gla_sub(hd, 0)
                    if 4 <= k < 10:
                        gla_sub(hd, k - 3)
                    if k == 5:
                        gla_acc(hd, 0)
                        gla_acc(hd, 1)
                    if k > 5:
                        gla_acc(hd, k - 4)
                    if 5 <= k < 9:
                        j = k - 5
                        b = banks[5 + j % 2]
                        dve.wait_ge(g_vt, 4 * hd + j + 1)
                        V.tensor_copy(vt1[:, :, j * P:(j + 1) * P],
                                      b[:, 0:2 * P].rearrange("p (b t) -> p b t", b=2))
                        V.tensor_copy(vt0[0:N_META, j * P:(j + 1) * P], b[0:N_META, 2 * P:3 * P]).then_inc(g_vcopy, 1)
                    if k >= 8:
                        j = k - 8
                        dve.wait_ge(g_rtanh, 4 * hd + j + 1)
                        STT(r_g[:, j, :], th_r[:, j % 2, :], 1.0, bank(ch, k)[:, 0:T], ALU.add,
                            ALU.mult).then_inc(bank_free[ch.slot(k)], 1)
                dve.wait_ge(g_zq, 8 * hd + 8)
                for t in range(2):
                    ins = TS(z_k[:, t, B2[0]:B2[0] + N_META], z_k[:, t, 0:N_META],
                             exp_cum[:, t, B1[1] - 1:B1[1]], None, ALU.mult)
                ins.then_inc(g_zend, 1)

            gla(0, True)
            step.loop(GLA_HEADS - 1, DVE_STEPS["gla"], lambda i: gla(i + 1, False))
            gla_tail(GLA_HEADS - 1)
            out_pass("gla_out", False)

            def layer_norm(n, last):
                dve.wait_ge(l_mu, n + 1)
                wide = lambda x: x[:, :].unsqueeze(1).broadcast_to([P, 4, T])
                for g in range(4):
                    r = res[:, 4 * g:4 * g + 4, :]
                    TT(r, r, wide(ln_mu), ALU.subtract).then_inc(l_cent, 1)
                dve.wait_ge(l_std, n + 1)
                step.link(V.reciprocal(ln_rstd[:, :], ln_rstd[:, :]))

                def lo_part(g):
                    dve.wait_ge(h_hi_ready, 4 * (n + 1) + g + 1)
                    TT(h_lo[:, 4 * g:4 * g + 4, :], res[:, 4 * g:4 * g + 4, :],
                       h_hi[:, 4 * g:4 * g + 4, :].bitcast(F32), ALU.subtract).then_inc(h_ready, 1)

                for g in range(4):
                    r = res[:, 4 * g:4 * g + 4, :]
                    step.link(TT(r, r, wide(ln_rstd), ALU.mult))
                    for j in range(4 * g, 4 * g + 4):
                        ins = TS(res[:, j, :], res[:, j, :], ln_tab[:, n, 0, j:j + 1], ln_tab[:, n, 1, j:j + 1],
                                 ALU.mult, ALU.add)
                    ins.then_inc(l_norm, 1)
                    if g and not last:
                        lo_part(g - 1)
                if not last:
                    lo_part(3)

            def ffn_pairs(layer, base, tile0, first_pair, pairs, i, total, feat_before):
                ch = Chunks(base, 2 * pairs, i)
                for j in range(pairs):
                    q = i * pairs + j
                    n = q + total
                    tile = q + tile0
                    for w in range(2):
                        k = 2 * j + w
                        split_lo(ch, k + 2)
                        dve.wait_ge(f_scaled, n * 2 + w + 1)
                        u, y = bank(ch, k), (f_gate, f_val)[w][:, j % 2, :]
                        tap = lambda x: ffn_tab[:, layer, bass.ds(tile, 1), 4 * w + x]
                        step.link(STT(y[:, 1:], u[:, 0:T - 1], tap(1), y[:, 1:], ALU.mult, ALU.add))
                        STT(y[:, 2:], u[:, 0:T - 2], tap(0), y[:, 2:], ALU.mult, ALU.add).then_inc(
                            bank_free[ch.slot(k)], 1)
                    dve.wait_ge(f_tanh, n + 1)
                    step.link(STT(f_act[:, j % 2, :], f_th[:, j % 2, :], 1.0, f_gate[:, j % 2, :], ALU.add, ALU.mult))
                    TT(f_act[:, j % 2, :], f_act[:, j % 2, :], f_val[:, j % 2, :], ALU.mult).then_inc(f_mul, 1)
                    dve.wait_ge(feat_hi_ready, q + (feat_before + 1))
                    TT(feat_lo[:, bass.ds(q + first_pair, 1), :], f_act[:, j % 2:j % 2 + 1, :],
                       feat_hi[:, bass.ds(q + first_pair, 1), :].bitcast(F32), ALU.subtract).then_inc(feat_ready, 1)

            def ffn(layer):
                for n, (tile0, tiles) in enumerate(FFN_PASSES):
                    total = layer * FF_TILES + tile0
                    base, before = BASE[f"up{layer}{n}"], FEAT[f"down{layer}{n}"][0]
                    bodies = tiles // 6
                    step.loop(bodies, DVE_STEPS["up"],
                              lambda i: ffn_pairs(layer, base, tile0, 0, 6, i, total, before))
                    done = 6 * bodies
                    if tiles > done:
                        ffn_pairs(layer, base + 2 * done, tile0 + done, done, tiles - done, 0, total + done,
                                  before + done)
                    out_pass(f"down{layer}{n}", n == 0)

            layer_norm(0, False)
            ffn(0)
            layer_norm(1, False)

            def rotate(ch, k, n, src, dst):
                dve.wait_ge(a_swap, n + 1)
                if not isinstance(n, int) or n:
                    dve.wait_ge(a_rot, n)
                step(TT(rot_c[:, :], src, mk1["cos"], ALU.mult))
                TT(rot_s[:, :], bank(ch, k)[:, 0:T], mk1["sin"], ALU.mult).then_inc(bank_free[ch.slot(k)], 1)
                dve.wait_ge(bank_free[ch.slot(k)], ch.turn(k) + 1)
                TT(dst, rot_c[:, :], rot_s[:, :], ALU.add).then_inc(a_rot, 1)

            W1 = N_META + P
            W = 2 * T - P

            def swa_softmax(n, m, r):
                sink = tb["sinks"].rearrange("p (m a r) -> p m a r", a=2, r=4)[:, bass.ds(m, 1), :, r]
                sink3 = sink.broadcast_to([P, 3, 2])
                dve.wait_ge(a_score, n + 1)
                step(TT(sc_w[:, :, :], psum[:, 3:5, 0:W], mk1["window"].unsqueeze(1).broadcast_to([P, 2, W]), ALU.add))
                step(TT(sc_m[0:N_META, :, :], psum[0:N_META, 3:5, W:W + N_META],
                        mk1["window_meta"][0:N_META, :].unsqueeze(1).broadcast_to([N_META, 2, N_META]), ALU.add))
                step.link(V.tensor_copy(neg_max[:, 2:3, :], sink))
                step(V.reduce_max(neg_max[:, 0, :], sc_w[:, :, 0:W1], axis=AX.X))
                step(V.reduce_max(neg_max[:, 1, :], sc_w[:, :, W1:], axis=AX.X))
                step.link(V.reduce_max(neg_max[0:N_META, 2, :], sc_m[0:N_META, :, :], axis=AX.X))
                step.link(TT(neg_max[:, :, :], neg_max[:, :, :], sink3, ALU.max))
                step.link(TS(neg_max[:, :, :], neg_max[:, :, :], -1.0, None, ALU.mult))
                TT(sinks_e[:, :, :], neg_max[:, :, :], sink3, ALU.add).then_inc(a_max, 1)
                dve.wait_ge(a_exp, n + 1)
                step.link(TT(sums[:, :, :], sums[:, :, :], sinks_e[:, :, :], ALU.add))
                step.link(V.reciprocal(sums[:, :, :], sums[:, :, :]))
                by = lambda w, rows, n_: sums[0:rows, w, :].unsqueeze(2).broadcast_to([rows, 2, n_])
                TT(sc_w[:, :, 0:W1], sc_w[:, :, 0:W1], by(0, P, W1), ALU.mult)
                TT(sc_w[:, :, W1:], sc_w[:, :, W1:], by(1, P, W - W1), ALU.mult)
                TT(sc_m[0:N_META, :, :], sc_m[0:N_META, :, :], by(2, N_META, N_META), ALU.mult).then_inc(a_norm, 1)

            def swa_p1(n, m, r):
                for a in range(2):
                    dve.wait_ge(a_pt, 2 * n + a + 1)
                    V.tensor_copy(p1[:, a, :], banks[6][:, 0:3 * P]).then_inc(a_p1, 1)

            def swa_lo(n, m, r):
                dve.wait_ge(feat_hi_ready, n + (FEAT["swa_out"][0] + 1))
                TT(feat_lo[:, bass.ds(n, 1), :], o_f[:, :].unsqueeze(1), feat_hi[:, bass.ds(n, 1), :].bitcast(F32),
                   ALU.subtract).then_inc(feat_ready, 1)

            def swa_slot(m, k, has_before, has_own):
                for stage, lag in ((swa_lo, 6), (swa_p1, 5), (swa_softmax, 4)):
                    r = k - lag
                    if r >= 0 and has_own:
                        stage(4 * m + r, m, r)
                    elif 0 <= r + SWA_PER < 4 and has_before:
                        stage(4 * m + (r + SWA_PER - 4), m - 1, r + SWA_PER)

            def swa(m, first):
                ch, prev = Chunks(BASE["swa"], SWA_PER, m), Chunks(BASE["swa"] - SWA_PER, SWA_PER, m)
                for k in range(SWA_PER):
                    split_lo(ch, k + 2)
                    if k == 0 and not first:
                        rotate(prev, 5, 5 * m - 1, q_raw[:, 1, :], q_rot[:, 1, :])
                    if k >= 3:
                        r = k - 3
                        rotate(ch, k - 1, 5 * m + (r + 1), q_raw[:, r % 2, :], q_rot[:, r % 2, :])
                    swa_slot(m, k, not first, True)
                    if k == 1:
                        rotate(ch, 0, 5 * m, k_raw[:, :], k_rot[:, :])
                    if k == 3:
                        dve.wait_ge(a_vt, m + 1)
                        V.tensor_copy(kv1[:, :, :], banks[5][:, 0:2 * P].rearrange("p (b f) -> p b f", b=2))
                        V.tensor_copy(kv0[0:N_META, :], banks[5][0:N_META, 2 * P:3 * P]).then_inc(a_vcopy, 1)

            dve.wait_ge(mask1_in, 16)
            step.link(V.memset(sums[:, :, :], 0.0))
            swa(0, True)
            step.loop(SWA_KV_HEADS // 2 - 1, DVE_STEPS["swa"], lambda i: swa(i + 1, False))
            end = SWA_KV_HEADS // 2
            rotate(Chunks(BASE["swa"] - SWA_PER, SWA_PER, end), 5, 5 * end - 1, q_raw[:, 1, :], q_rot[:, 1, :])
            for k in range(4):
                swa_slot(end, k, True, False)
            out_pass("swa_out", True)
            layer_norm(2, False)
            ffn(1)
            layer_norm(3, True)

        @block.tensor
        def _(pe):
            MM = nc.tensor.matmul

            def project(ch, k, hi, lo, tiles=KT, tile_wait=None):
                sl = ch.slot(k)
                pe.wait_ge(lo_ready, ch.number(k) + 1)
                if not ch.first_turn(k):
                    pe.wait_ge(bank_free[sl], ch.turn(k))
                for j in range(tiles):
                    if tile_wait is not None:
                        tile_wait(j)
                    for n, (w, x) in enumerate(((w_hi, hi), (w_hi, lo), (w_lo, hi))):
                        ins = MM(banks[sl][:, 0:T], w[:, sl, j, :], x[:, j, :], start=(j == 0 and n == 0),
                                 stop=(j == tiles - 1 and n == 2))
                ins.then_inc(chunk_done, 1)

            def turn(out, in_, rows):
                return nc.tensor.transpose(out, in_, ident[0:rows, 0:rows])

            pe.wait_ge(const_in, 32)
            pe.wait_ge(ones_set, 5)

            project(Chunks(0, RING, 0), 0, h_hi, h_lo, tile_wait=lambda j: j % 4 or pe.wait_ge(h_ready, j // 4 + 1))
            pe.wait_ge(gates_rows, 1)
            H = SSD_HEADS
            for n, (rows, (lo, hi)) in enumerate(((acs, B1), (acs, B2), (to_end, B1), (dt_v, B1), (dt_v, B2))):
                turn(banks[3][:, 32 * n:32 * n + 32], rows[0:H, lo:hi], H)
            for n, rows in enumerate((acs, to_end, to_end2, dt_v)):
                ins = turn(banks[3][0:N_META, 160 + 32 * n:192 + 32 * n], rows[0:H, 0:N_META], H)
            ins.then_inc(gates_turned, 1)

            def ssd_rows(g, h):
                if h >= 2:
                    pe.wait_ge(s_exp, 4 * g + h - 1)
                MM(banks[5 + h % 2][:, 0:T], ones[0:H, :], head_rows[0:H, h, :], start=True,
                   stop=True).then_inc(s_bc, 1)

            def ssd_y_tile(g, t):
                pe.wait_ge(s_mix, 4 * g + 2 * t + 2)
                pe.wait_ge(s_xd, g + 1)
                out_ = banks[(7, 5)[t]]
                for a in range(2):
                    h, rows = 2 * t + a, slice(SSD_P * a, SSD_P * a + SSD_P)
                    f = slice(SSD_P * h, SSD_P * h + SSD_P)
                    MM(out_[rows, 0:T], xd0[0:N_META, f], dec0[0:N_META, h, :], start=True, stop=False)
                    MM(out_[rows, B1[0]:T], xd1[:, 0, f], dec1[:, h, 0:2 * P], start=False, stop=False)
                    ins = MM(out_[rows, B2[0]:T], xd1[:, 1, f], dec1[:, h, 2 * P:3 * P], start=False, stop=True)
                ins.then_inc(s_y, 1)

            def ssd_stats(g):
                pe.wait_ge(s_sq, g + 1)
                for t in range(2):
                    ins = MM(banks[6][:, 0:T], ones[:, :], ssd_z[:, t, :], start=t == 0, stop=t == 1)
                ins.then_inc(s_stat, 1)

            def ssd(g, first):
                ch = Chunks(BASE["ssd"], SSD_PER, g)
                project(ch, 0, h_hi, h_lo)
                project(ch, 1, h_hi, h_lo)
                if not first:
                    ssd_stats(g - 1)
                project(ch, 2, h_hi, h_lo)
                if first:
                    pe.wait_ge(gates_cols, 1)
                else:
                    pe.wait_ge(s_xd, g)
                    pe.wait_ge(s_yread, g)
                    pe.wait_ge(s_std, g)
                pe.wait_ge(s_conv, 4 * g + 2)
                bt, ct = conv_out[:, 0, :], conv_out[:, 1, :]
                MM(banks[3][0:N_META, 0:T], bt[:, 0:N_META], ct[:, 0:T], start=True, stop=True)
                MM(banks[4][:, 0:2 * P], bt[:, B1[0]:B1[1]], ct[:, B1[0]:T], start=True, stop=True)
                MM(banks[4][:, 2 * P:3 * P], bt[:, B2[0]:B2[1]], ct[:, B2[0]:T], start=True,
                   stop=True).then_inc(s_scores, 1)
                pe.wait_ge(s_rows, g + 1)
                ssd_rows(g, 0)
                ssd_rows(g, 1)
                project(ch, 3, h_hi, h_lo)
                ssd_rows(g, 2)
                ssd_rows(g, 3)
                project(ch, 4, h_hi, h_lo)
                pe.wait_ge(s_conv, 4 * g + 4)
                pe.wait_ge(s_masked, g + 1)
                for t in range(2):
                    x = conv_out[:, 2 + t, :]
                    for b, (lo, hi) in enumerate((B1, B2)):
                        turn(banks[3][:, 256 * b + P * t:256 * b + P * t + P], x[:, lo:hi], P)
                    ins = turn(banks[4][0:N_META, P * t:P * t + P], x[:, 0:N_META], P)
                ins.then_inc(s_xt, 1)
                project(ch, 5, h_hi, h_lo)
                ssd_y_tile(g, 0)
                ssd_y_tile(g, 1)

            ssd(0, True)
            with pe.Fori(0, SSD_GROUPS - 1) as i:
                ssd(i + 1, False)
            ssd_stats(SSD_GROUPS - 1)

            def out_pass(name):
                base, tiles = BASE[name], OUT_PASSES[name]
                pe.wait_ge(feat_ready, FEAT[name][1])
                project(Chunks(base, RING, 0), 0, feat_hi, feat_lo, tiles)
                with pe.Fori(0, KT // RING) as i:
                    for k in range(RING):
                        project(Chunks(base + 1, RING, i), k, feat_hi, feat_lo, tiles)

            out_pass("ssd_out")

            def gla_gate(hd):
                if not isinstance(hd, int) or hd:
                    pe.wait_ge(g_cross, hd)
                    pe.wait_ge(g_acc, 8 * hd)
                pe.wait_ge(gw_in, 16 * (hd + 1))
                r = slice(2 * GLA_RANK, 3 * GLA_RANK)
                for t in range(2):
                    ins = MM(banks[3 + t][:, 0:T], gate_w[r, P * t:P * t + P], g_lr[r, :], start=True, stop=True)
                ins.then_inc(g_mm, 1)

            def gla_scores(hd, lv, ch):
                b = banks[3 + lv % 2]
                if lv < 2:
                    pe.wait_ge(g_gexp, 2 * hd + 1)
                else:
                    pe.wait_ge(g_acc, 8 * hd + lv - 1)
                if lv:
                    pe.wait_ge(g_zq, 8 * hd + lv)
                else:
                    pe.wait_ge(bank_free[ch.slot(3)], ch.turn(3) + 1)
                k_, q_ = (z_k, z_q) if lv else (k_g, q_g)
                pairs = [(slice(0, P), slice(0, P), B1), (slice(0, P), slice(P, 2 * P), B2)]
                if lv == 0 or LEVELS[lv - 1] < 16:
                    pairs.append((slice(0, N_META), slice(2 * P, T), M0))
                for rows, cols, (lo, hi) in pairs:
                    for t in range(2):
                        ins = MM(b[rows, cols], k_[:, t, lo:hi], q_[:, t, lo:hi], start=t == 0, stop=t == 1)
                ins.then_inc(g_sc, 1)

            def gla_cross(hd):
                b = banks[3]
                pe.wait_ge(g_zend, hd + 1)
                pe.wait_ge(g_acc, 8 * hd + 7)
                for rows, cols, (klo, khi), (lo, hi) in (
                        (slice(0, P), slice(0, P), B1, B2),
                        (slice(0, N_META), slice(P, 2 * P), M0, B1),
                        (slice(0, N_META), slice(2 * P, 3 * P), (B2[0], B2[0] + N_META), B2)):
                    for t in range(2):
                        ins = MM(b[rows, cols], z_k[:, t, klo:khi], z_q[:, t, lo:hi], start=t == 0, stop=t == 1)
                ins.then_inc(g_sc, 1)

            def gla_turn_v(hd, ch, j):
                pe.wait_ge(bank_free[ch.slot(4 + j)], ch.turn(4 + j) + 1)
                if j >= 2:
                    pe.wait_ge(g_vcopy, 4 * hd + j - 1)
                b, v = banks[5 + j % 2], vfm[:, j % 2, :]
                turn(b[:, 0:P], v[:, B1[0]:B1[1]], P)
                turn(b[:, P:2 * P], v[:, B2[0]:B2[1]], P)
                turn(b[0:N_META, 2 * P:3 * P], v[:, 0:N_META], P).then_inc(g_vt, 1)

            def gla_o(hd, j):
                if j >= 2:
                    pe.wait_ge(g_osb, 4 * hd + j - 1)
                b, f = banks[5 + j % 2], slice(P * j, P * j + P)
                MM(b[:, 0:T], vt0[0:N_META, f], a0[0:N_META, :], start=True, stop=False)
                MM(b[:, B1[0]:T], vt1[:, 0, f], a1[:, 0:2 * P], start=False, stop=False)
                MM(b[:, B2[0]:T], vt1[:, 1, f], a1[:, 2 * P:3 * P], start=False, stop=True).then_inc(g_o, 1)

            def gla_stat(hd, j):
                if j == 0 and (not isinstance(hd, int) or hd):
                    pe.wait_ge(g_std, hd)
                pe.wait_ge(g_sqr, 4 * hd + j + 1)
                MM(banks[7][:, 0:T], ones[:, :], o_sq[:, :], start=j == 0, stop=j == 3).then_inc(g_st, 1)

            def gla_outputs(hd):
                pe.wait_ge(g_cross, hd + 1)
                pe.wait_ge(g_scored, hd + 1)
                pe.wait_ge(g_vcopy, 4 * hd + 4)
                gla_o(hd, 0)
                gla_o(hd, 1)
                gla_stat(hd, 0)
                gla_o(hd, 2)
                gla_stat(hd, 1)
                gla_o(hd, 3)
                gla_stat(hd, 2)
                gla_stat(hd, 3)

            def gla(hd, first):
                ch = Chunks(BASE["gla"], GLA_PER, hd)
                for k in range(GLA_PER):
                    project(ch, k, h_hi, h_lo)
                    if k == 0:
                        gla_gate(hd)
                        if not first:
                            gla_outputs(hd - 1)
                    if k == 4:
                        gla_scores(hd, 0, ch)
                    if 4 <= k < 11:
                        gla_scores(hd, k - 3, ch)
                    if 5 <= k < 9:
                        gla_turn_v(hd, ch, k - 5)
                gla_cross(hd)

            gla(0, True)
            with pe.Fori(0, GLA_HEADS - 1) as i:
                gla(i + 1, False)
            gla_outputs(GLA_HEADS - 1)
            out_pass("gla_out")

            def layer_norm(n):
                pe.wait_ge(l_sum, KT * (n + 1))
                MM(banks[3][:, 0:T], ones[:, :], col_sum[:, :], start=True, stop=True).then_inc(l_mean, 1)
                for g in range(4):
                    pe.wait_ge(l_sq, 4 * n + g + 1)
                    for j in range(4):
                        ins = MM(banks[4][:, 0:T], ones[:, :], ln_sq[:, g % 2, j * T:(j + 1) * T],
                                 start=g == 0 and j == 0, stop=g == 3 and j == 3)
                    ins.then_inc(l_sqmm, 1)

            def ffn(layer):
                pe.wait_ge(h_ready, 4 * (2 * layer + 2))
                for n, (_, tiles) in enumerate(FFN_PASSES):
                    base = BASE[f"up{layer}{n}"]
                    bodies = tiles // 6
                    with pe.Fori(0, bodies) as i:
                        for k in range(12):
                            project(Chunks(base, 12, i), k, h_hi, h_lo)
                    for k in range(12 * bodies, 2 * tiles):
                        project(Chunks(base, RING, 0), k, h_hi, h_lo)
                    out_pass(f"down{layer}{n}")

            layer_norm(0)
            ffn(0)
            layer_norm(1)

            def swa_swap(ch, k, n):
                pe.wait_ge(a_raw, n + 1)
                src = k_raw[:, :] if k == 0 else q_raw[:, k % 2, :]
                MM(banks[ch.slot(k)][:, 0:T], mk1["swap"], src, start=True, stop=True).then_inc(a_swap, 1)

            W1, W = N_META + P, 2 * T - P

            def swa_scores(n, m, r):
                pe.wait_ge(a_rot, 5 * m + (r + 2))
                if not isinstance(n, int) or n:
                    pe.wait_ge(a_max, n)
                for a in range(2):
                    f = slice(SWA_D * a, SWA_D * a + SWA_D)
                    q, k_, b = q_rot[f, r % 2, :], k_rot[f, :], banks[3 + a]
                    MM(b[:, 0:W1], q[:, B1[0]:B1[1]], k_[:, 0:W1], start=True, stop=True)
                    MM(b[:, W1:W], q[:, B2[0]:B2[1]], k_[:, 0:T], start=True, stop=True)
                    ins = MM(b[0:N_META, W:W + N_META], q[:, 0:N_META], k_[:, 0:N_META], start=True, stop=True)
                ins.then_inc(a_score, 1)

            def swa_turn_p(n, m, r):
                pe.wait_ge(a_norm, n + 1)
                for a in range(2):
                    if a or not isinstance(n, int) or n:
                        pe.wait_ge(a_p0, 2 * n + a)
                        pe.wait_ge(a_p1, 2 * n + a)
                    turn(banks[5][0:N_META, B1[0]:B1[1]], sc_w[:, a, 0:N_META], P)
                    turn(banks[5][0:N_META, 0:N_META], sc_m[0:N_META, a, :], N_META)
                    turn(banks[5][0:N_META, B2[0]:B2[1]], sc_w[:, a, W1:W1 + N_META], P)
                    turn(banks[6][:, 0:P], sc_w[:, a, N_META:W1], P)
                    turn(banks[6][:, P:2 * P], sc_w[:, a, W1 + N_META:W1 + W1], P)
                    turn(banks[6][:, 2 * P:3 * P], sc_w[:, a, 2 * W1:W], P).then_inc(a_pt, 1)

            def swa_o(n, m, r):
                pe.wait_ge(a_p0, 2 * n + 2)
                pe.wait_ge(a_p1, 2 * n + 2)
                pe.wait_ge(a_vcopy, m + 1)
                if not isinstance(n, int) or n:
                    pe.wait_ge(a_of, n)
                for a in range(2):
                    f = slice(SWA_D * a, SWA_D * a + SWA_D)
                    b = banks[7]
                    MM(b[f, 0:T], kv0[0:N_META, f], p0[0:N_META, a, :], start=True, stop=False)
                    MM(b[f, B1[0]:T], kv1[:, 0, f], p1[:, a, 0:2 * P], start=False, stop=False)
                    ins = MM(b[f, B2[0]:T], kv1[:, 1, f], p1[:, a, 2 * P:3 * P], start=False, stop=True)
                ins.then_inc(a_o, 1)

            def swa_slot(m, k, has_before, has_own):
                for stage, lag in ((swa_o, 6), (swa_turn_p, 5), (swa_scores, 4)):
                    r = k - lag
                    if r >= 0 and has_own:
                        stage(4 * m + r, m, r)
                    elif 0 <= r + SWA_PER < 4 and has_before:
                        stage(4 * m + (r + SWA_PER - 4), m - 1, r + SWA_PER)

            def swa(m, first):
                ch, prev = Chunks(BASE["swa"], SWA_PER, m), Chunks(BASE["swa"] - SWA_PER, SWA_PER, m)
                for k in range(SWA_PER):
                    project(ch, k, h_hi, h_lo)
                    if k == 0 and not first:
                        swa_swap(prev, 5, 5 * m - 1)
                    if k == 1:
                        swa_swap(ch, 0, 5 * m)
                    if k >= 3:
                        swa_swap(ch, k - 1, 5 * m + (k - 2))
                    swa_slot(m, k, not first, True)
                    if k == 3:
                        pe.wait_ge(bank_free[ch.slot(1)], ch.turn(1) + 1)
                        if not first:
                            pe.wait_ge(a_p0, 8 * m)
                        turn(banks[5][:, 0:P], v_fm[:, B1[0]:B1[1]], P)
                        turn(banks[5][:, P:2 * P], v_fm[:, B2[0]:B2[1]], P)
                        turn(banks[5][0:N_META, 2 * P:3 * P], v_fm[:, 0:N_META], P).then_inc(a_vt, 1)

            pe.wait_ge(mask1_in, 16)
            pe.wait_ge(h_ready, 4 * 3)
            swa(0, True)
            with pe.Fori(0, SWA_KV_HEADS // 2 - 1) as i:
                swa(i + 1, False)
            end = SWA_KV_HEADS // 2
            swa_swap(Chunks(BASE["swa"] - SWA_PER, SWA_PER, end), 5, 5 * end - 1)
            for k in range(4):
                swa_slot(end, k, True, False)
            out_pass("swa_out")
            layer_norm(2)
            ffn(1)
            layer_norm(3)


def pack_chunks(w, columns):
    rows = w.shape[0]
    out = np.zeros((len(columns), P, KT, P), w.dtype)
    tiles = rows // P
    for n, cols in enumerate(columns):
        out[n, :, 0:tiles, :] = w[:, cols].reshape(tiles, P, len(cols)).transpose(1, 0, 2)
    return out.reshape(len(columns), P, KT * P)


def span(at, n=P):
    return np.arange(at, at + n)


def pack_stream(x):
    w_in = x["hyb_w_in"][0]
    o_z = 0
    o_x = o_z + SSD_INNER
    o_b = o_x + SSD_INNER
    o_c = o_b + SSD_GROUPS * SSD_N
    o_dt = o_c + SSD_GROUPS * SSD_N
    o_q = o_dt + SSD_HEADS
    o_k = o_q + D_MODEL // 2
    o_v = o_k + D_MODEL // 2
    o_lr = o_v + D_MODEL
    o_r = o_lr + GLA_RANK
    small = np.zeros((D_MODEL, P), w_in.dtype)
    small[:, 0:SSD_HEADS] = w_in[:, o_dt:o_dt + SSD_HEADS]
    small[:, SSD_HEADS:SSD_HEADS + GLA_RANK] = w_in[:, o_lr:o_lr + GLA_RANK]
    parts = [pack_chunks(small, [span(0)])]
    cols = []
    for g in range(SSD_GROUPS):
        cols += [span(o_b + P * g), span(o_c + P * g), span(o_x + 2 * P * g), span(o_x + 2 * P * g + P),
                 span(o_z + 2 * P * g), span(o_z + 2 * P * g + P)]
    parts.append(pack_chunks(w_in, cols))
    out_cols = [span(P * n) for n in range(KT)]
    parts.append(pack_chunks(x["hyb_w_out"][0][0:SSD_INNER], out_cols))
    cols = []
    for hd in range(GLA_HEADS):
        cols += [span(o_q + GLA_DK * hd + P * t) for t in range(2)]
        cols += [span(o_k + GLA_DK * hd + P * t) for t in range(2)]
        cols += [span(o_v + GLA_DV * hd + P * t) for t in range(4)]
        cols += [span(o_r + GLA_DV * hd + P * t) for t in range(4)]
    parts.append(pack_chunks(w_in, cols))
    parts.append(pack_chunks(x["hyb_w_out"][0][SSD_INNER:], out_cols))
    for layer in range(DEPTH):
        if layer == 1:
            heads = [(8 * m + r, 8 * m + 4 + r) for m in range(SWA_KV_HEADS // 2) for r in range(4)]
            q_cols = [np.concatenate([span(SWA_D * a, SWA_D), span(SWA_D * b, SWA_D)]) for a, b in heads]
            kv = SWA_Q_HEADS * SWA_D
            cols = []
            for m in range(SWA_KV_HEADS // 2):
                cols += [span(kv + P * m), span(kv + SWA_KV_HEADS * SWA_D + P * m)] + q_cols[4 * m:4 * m + 4]
            parts.append(pack_chunks(x["swa_w_qkv"][0], cols))
            parts.append(pack_chunks(x["swa_w_out"][0][np.concatenate(q_cols)], out_cols))
        for tile0, tiles in FFN_PASSES:
            cols = []
            for t in range(tile0, tile0 + tiles):
                cols += [span(P * t), span(D_FF + P * t)]
            parts.append(pack_chunks(x["ffn_w_up"][layer], cols))
            parts.append(pack_chunks(x["ffn_w_down"][layer][P * tile0:P * (tile0 + tiles)], out_cols))
    return np.concatenate(parts)


def pack_table(x):
    t = table_columns()
    out = np.zeros((P, t.at), np.float32)

    def put(name, a, rows=P):
        at, n = t.where[name]
        out[0:rows, at:at + n] = a.reshape(rows, n)

    fm = lambda v: np.ascontiguousarray(v.reshape(-1, P).T)
    taps = np.stack([fm(w) for w in x["hyb_conv_w"][0]] + [fm(x["hyb_conv_b"][0])], axis=2)
    xt, bt = SSD_INNER // P, SSD_GROUPS
    order = [i for g in range(SSD_GROUPS) for i in (xt + g, xt + bt + g, 2 * g, 2 * g + 1)]
    put("ssd_conv", taps[:, order, :])
    put("ssd_d", fm(np.repeat(x["ssd_d"][0], SSD_P)))
    put("ssd_norm", fm(x["ssd_norm_w"][0]))
    put("gla_norm", fm(x["gla_norm_w"][0]))
    put("gate_b", fm(x["gla_gate_b"][0]))
    ln = []
    for layer in range(DEPTH):
        for kind in ("mix", "ffn"):
            ln += [fm(x[f"ln_{kind}_g"][layer]), fm(x[f"ln_{kind}_b"][layer])]
    put("ln", np.stack(ln, axis=1))
    ffn = []
    for layer in range(DEPTH):
        v = [fm(w) for w in x["ffn_conv_w"][layer]] + [fm(x["ffn_conv_b"][layer])]
        ffn.append(np.stack([a[:, 0:FF_TILES] for a in v] + [a[:, FF_TILES:] for a in v], axis=2))
    put("ffn", np.stack(ffn, axis=1))
    put("sinks", np.repeat(x["swa_sinks"][0][None], P, axis=0))
    put("dt_bias", x["ssd_dt_bias"][0], SSD_HEADS)
    put("a_log", x["ssd_a_log"][0], SSD_HEADS)
    return out


def shape_masks():
    out = np.zeros((DEPTH, P, MASK_COLS), np.float32)
    key, query = np.arange(P)[:, None], np.arange(P)[None, :]
    causal = (query >= key).astype(np.float32)
    for layer in range(DEPTH):
        t = mask_columns(layer)

        def put(name, a, rows=P):
            at, n = t.where[name]
            out[layer, 0:rows, at:at + n] = a

        put("ident", np.eye(P))
        if layer == 0:
            put("causal", np.concatenate([causal, np.ones((P, P)), causal], axis=1))
            put("causal_meta", np.concatenate([causal[0:N_META, 0:N_META], np.ones((N_META, T - N_META))], axis=1),
                N_META)
            levels = [np.eye(P)]
            for half in LEVELS:
                same = query // (2 * half) == key // (2 * half)
                levels.append(same & (query % (2 * half) >= half) & (key % (2 * half) < half))
            put("levels", np.concatenate(levels, axis=1))
        else:
            half = ROPE_DIM // 2
            swap = np.zeros((P, P))
            for head in range(P // SWA_D):
                for d in range(half):
                    a, b = SWA_D * head + d, SWA_D * head + half + d
                    swap[b, a] = -1.0
                    swap[a, b] = 1.0
            put("swap", swap)
            freq = np.float32(ROPE_THETA) ** (-np.arange(half, dtype=np.float32) / np.float32(half))
            angle = np.arange(T, dtype=np.float32)[None, :] * freq.astype(np.float32)[:, None]
            cos, sin = np.ones((P, T)), np.zeros((P, T))
            for head in range(P // SWA_D):
                for part in range(2):
                    rows = slice(SWA_D * head + half * part, SWA_D * head + half * part + half)
                    cos[rows], sin[rows] = np.cos(angle), np.sin(angle)
            put("cos", cos)
            put("sin", sin)
            hide = np.float32(-1e30)
            q, k = np.arange(P)[:, None], np.arange(P)[None, :]
            meta = np.zeros((P, N_META))
            own, before = np.where(k <= q, 0, hide), np.where(k > q, 0, hide)
            put("window", np.concatenate([meta, own, meta, before, own], axis=1))
            put("window_meta", np.where(k[:, 0:N_META] <= q[0:N_META], 0, hide), N_META)
    return out


def kernel(**inputs):
    import concourse.bacc as bacc
    from concourse.bass_utils import run_bass_kernel_spmd

    x = {name: np.asarray(a) for name, a in inputs.items()}
    tokens = np.concatenate([x["meta_tokens"], x["x"][0]])
    arrays = {
        "stream": pack_stream(x),
        "h0": np.ascontiguousarray(tokens.T.reshape(KT, P, T).transpose(1, 0, 2)),
        "table": pack_table(x),
        "masks": shape_masks(),
        "gate_w2": np.ascontiguousarray(x["gla_gate_w2"][0]),
    }
    nc = bacc.Bacc("TRN2", target_bir_lowering=False, num_devices=1)
    args = [nc.dram_tensor(f"in_{name}", a.shape, mybir.dt.from_np(a.dtype), kind="ExternalInput").ap()
            for name, a in arrays.items()]
    out = nc.dram_tensor("out", (P, KT, SEQ), F32, kind="ExternalOutput").ap()
    trunk_kernel(nc, *args, out)
    r = run_bass_kernel_spmd(nc, [{f"in_{name}": a for name, a in arrays.items()}], core_ids=[0])
    y = np.asarray(r.results[0]["out"])
    return np.ascontiguousarray(y.transpose(1, 0, 2).reshape(D_MODEL, SEQ).T)[None]
```

```python
from contextlib import ExitStack

import numpy as np

import concourse.bass as bass
from concourse import mybir

F32, F32R = mybir.dt.float32, mybir.dt.float32r
ALU, ACT, AX = mybir.AluOpType, mybir.ActivationFunctionType, mybir.AxisListType

D_MODEL, SEQ, N_META, DEPTH = 2048, 256, 16, 2
T = SEQ + N_META
P = 128
KT = D_MODEL // P
ALPHA = (2.0 * DEPTH) ** 0.25
LN_EPS, RMS_EPS = 1e-5, 1e-6

SSD_HEADS, SSD_GROUPS, SSD_HPG, SSD_P, SSD_N, SSD_TAPS = 32, 8, 4, 64, 128, 4
SSD_INNER = SSD_HEADS * SSD_P
SSD_CONV_DIM = SSD_INNER + 2 * SSD_GROUPS * SSD_N
GLA_HEADS, GLA_DK, GLA_DV, GLA_RANK, GLA_TAU = 4, 256, 512, 16, 16.0
SWA_Q_HEADS, SWA_KV_HEADS, SWA_D, SWA_WINDOW = 32, 8, 64, 128
ROPE_DIM, ROPE_THETA = SWA_D // 4, 500000.0
D_FF, FFN_TAPS = 5504, 3
FF_TILES = D_FF // P

M0, B1, B2 = (0, N_META), (N_META, N_META + P), (N_META + P, T)
Q0 = N_META - 2
NQ = N_META - Q0
LN_FROM = [0, 0, Q0, N_META]
RING = 3
FFN_BODY = 6
H_GROUPS = [(0, 2), (2, 2), (4, 4), (8, 4), (12, 2), (14, 2)]
HG = len(H_GROUPS)
LEVELS = [1, 2, 4, 8, 16, 32, 64]

SSD_PER, GLA_PER, SWA_PER = 6, 12, 6
FFN_PASSES = [(0, 15), (15, 14), (29, 14)]


def chunk_bases():
    at, base = 0, {}

    def take(name, n):
        nonlocal at
        base[name] = at
        at += n

    take("gates", 1)
    take("ssd", SSD_GROUPS * SSD_PER)
    take("ssd_out", KT)
    take("gla", GLA_HEADS * GLA_PER)
    take("gla_out", KT)
    for layer in range(DEPTH):
        if layer == 1:
            take("swa", SWA_PER * SWA_KV_HEADS // 2)
            take("swa_out", KT)
        for n, (_, tiles) in enumerate(FFN_PASSES):
            take(f"up{layer}{n}", 2 * tiles)
            take(f"down{layer}{n}", KT)
    return base, at


BASE, N_CHUNKS = chunk_bases()


class Chunks:

    def __init__(self, base, per, g):
        self.base, self.per, self.g = base, per, g

    def number(self, k):
        return self.base + k + self.g * self.per

    def slot(self, k):
        return (self.base + k) % RING if self.per % RING == 0 else (self.base + k + self.g * self.per) % RING

    def turn(self, k):
        if self.per % RING:
            return (self.base + k + self.g * self.per) // RING
        return (self.base + k) // RING + self.g * (self.per // RING)

    def first_turn(self, k):
        return isinstance(self.g, int) and self.base + k + self.per * self.g < RING


class Steps:

    def __init__(self, engine, sem):
        self.engine, self.sem, self.count, self.before, self.per, self.i = engine, sem, 0, 0, 0, None

    def __call__(self, ins):
        ins.then_inc(self.sem, 1)
        self.count += 1
        return self.count

    def after(self, step):
        self.engine.wait_ge(self.sem, self.before + step + (0 if self.i is None else self.i * self.per))

    def link(self, ins):
        self.after(self(ins))

    def loop(self, turns, per, body):
        outer = self.before + self.count
        with self.engine.Fori(0, turns) as i:
            self.before, self.count, self.per, self.i = outer, 0, per, i
            body(i)
            assert self.count == per, f"{self.count} steps in a body, not {per}"
        self.before, self.count, self.per, self.i = 0, outer + turns * per, 0, None


DVE_STEPS = {"ssd": 12, "gla": 34, "swa": 45, "up": 18}
ACT_STEPS = {"ssd": 0, "gla": 2, "swa": 0}


class Columns:

    def __init__(self, tile=None):
        self.tile, self.at, self.where = tile, 0, {}

    def take(self, name, n):
        self.where[name] = (self.at, n)
        self.at += n
        return self.tile[:, self.at - n:self.at] if self.tile is not None else None

    def __getitem__(self, name):
        a, n = self.where[name]
        return self.tile[:, a:a + n]


def table_columns(tile=None):
    t = Columns(tile)
    t.take("ssd_conv", SSD_GROUPS * 4 * 5)
    t.take("ssd_d", KT)
    t.take("ssd_norm", KT)
    t.take("gla_norm", KT)
    t.take("gate_b", GLA_HEADS * 2)
    t.take("ln", 4 * 2 * KT)
    t.take("ffn", DEPTH * FF_TILES * 8)
    t.take("sinks", SWA_Q_HEADS)
    t.take("dt_bias", 1)
    t.take("a_log", 1)
    return t


def mask_columns(layer, tile=None):
    t = Columns(tile)
    t.take("ident", P)
    if layer == 0:
        t.take("causal", 3 * P)
        t.take("causal_meta", T)
        t.take("levels", (1 + len(LEVELS)) * P)
    else:
        t.take("swap", P)
        t.take("cos", T)
        t.take("sin", T)
        t.take("window", 2 * T - P)
        t.take("window_meta", N_META)
    return t


TABLE_COLS = table_columns().at
MASK_COLS = max(mask_columns(0).at, mask_columns(1).at)


def trunk_kernel(nc, stream, h0, table, masks, gate_w2, out):
    ctx = ExitStack()
    with ctx:
        def sb(name, shape, dt=F32):
            return ctx.enter_context(nc.sbuf_tensor(name, shape, dt))

        def sem(name):
            return ctx.enter_context(nc.semaphore(name))

        raw = sb("raw", [P, RING, KT, P])
        w_hi = sb("w_hi", [P, RING, KT, P], F32R)
        w_lo = sb("w_lo", [P, RING, KT, P], F32R)
        res = sb("res", [P, KT, T])
        h_hi = sb("h_hi", [P, KT, T], F32R)
        h_lo = sb("h_lo", [P, KT, T], F32R)
        feat_hi = sb("feat_hi", [P, KT, T], F32R)
        feat_lo = sb("feat_lo", [P, KT, T], F32R)
        tab = sb("tab", [P, TABLE_COLS])
        msk = sb("msk", [P, MASK_COLS])
        ones = sb("ones", [P, P])
        eps = sb("eps", [P, 3])
        gate_w = sb("gate_w", [3 * GLA_RANK, GLA_DK])
        g_lr = sb("g_lr", [3 * GLA_RANK, T])
        SCRATCH = 9400
        scratch = sb("scratch", [P, SCRATCH])
        psum = ctx.enter_context(nc.psum_tensor("psum", [P, 8, 512], F32))
        banks = [psum[:, b, :] for b in range(8)]
        tb, mk0, mk1 = table_columns(tab), mask_columns(0, msk), mask_columns(1, msk)
        ident = mk0["ident"]
        ln_tab = tb["ln"].rearrange("p (l w n) -> p l w n", l=4, w=2)
        ffn_tab = tb["ffn"].rearrange("p (l n w) -> p l n w", l=DEPTH, n=FF_TILES)

        s = Columns(scratch)
        conv_out = s.take("conv_out", 4 * T).rearrange("p (k t) -> p k t", k=4)
        pre = s.take("pre", 2 * T).rearrange("p (k t) -> p k t", k=2)
        th = s.take("th", 2 * T).rearrange("p (k t) -> p k t", k=2)
        s_g1 = s.take("s_g1", 3 * P)
        s_g0 = s.take("s_g0", T)
        head_rows = s.take("head_rows", 4 * T).rearrange("p (h t) -> p h t", h=4)
        dec1 = s.take("dec1", 4 * 3 * P).rearrange("p (h t) -> p h t", h=4)
        dec0 = s.take("dec0", 4 * T).rearrange("p (h t) -> p h t", h=4)
        xd1 = s.take("xd1", 4 * P).rearrange("p (b f) -> p b f", b=2)
        xd0 = s.take("xd0", 2 * P)
        ssd_y = s.take("ssd_y", 2 * T).rearrange("p (k t) -> p k t", k=2)
        ssd_z = s.take("ssd_z", 2 * T).rearrange("p (k t) -> p k t", k=2)
        ssd_rstd = s.take("ssd_rstd", T)
        acs = s.take("acs", T)
        cols1 = s.take("cols1", 5 * 32)
        cols0 = s.take("cols0", 4 * 32)
        assert s.at <= SCRATCH, s.at
        th_z = pre
        gt = Columns(dec1.rearrange("p h t -> p (h t)"))
        dt_x, dt_e, dt_s, dt_s2, dt_p = (gt.take(n, T) for n in ("x", "e", "s", "s2", "p"))
        gt = Columns(dec0.rearrange("p h t -> p (h t)"))
        dt_v, to_end, to_end2, a_neg = (gt.take(n, w) for n, w in (("dt", T), ("te", T), ("te2", 16), ("an", 1)))

        s = Columns(scratch)
        q_g = s.take("q", 2 * T).rearrange("p (k t) -> p k t", k=2)
        k_g = s.take("k", 2 * T).rearrange("p (k t) -> p k t", k=2)
        cum = s.take("cum", 2 * T).rearrange("p (k t) -> p k t", k=2)
        g_z = s.take("g_z", 2 * T)
        g_e = s.take("g_e", 2 * T)
        z_q = s.take("z_q", 2 * T).rearrange("p (k t) -> p k t", k=2)
        z_k = s.take("z_k", 2 * T).rearrange("p (k t) -> p k t", k=2)
        dec = s.take("dec", 2 * T).rearrange("p (k t) -> p k t", k=2)
        a1 = s.take("a1", 3 * P)
        a0 = s.take("a0", T)
        a_tmp = s.take("a_tmp", T)
        vt1 = s.take("vt1", 2 * GLA_DV).rearrange("p (b f) -> p b f", b=2)
        vt0 = s.take("vt0", GLA_DV)
        o_g = s.take("o", 4 * T).rearrange("p (k t) -> p k t", k=4)
        r_g = s.take("r", 4 * T).rearrange("p (k t) -> p k t", k=4)
        o_sq = s.take("o_sq", T)
        o_rstd = a_tmp
        assert s.at <= SCRATCH, s.at
        vfm = g_e.rearrange("p (k t) -> p k t", k=2)
        th_r = g_z.rearrange("p (k t) -> p k t", k=2)
        exp_cum = vfm

        s = Columns(scratch)
        k_raw = s.take("k_raw", T)
        k_rot = s.take("k_rot", T)
        v_fm = s.take("v_fm", T)
        q_raw = s.take("q_raw", 2 * T).rearrange("p (k t) -> p k t", k=2)
        q_rot = s.take("q_rot", 2 * T).rearrange("p (k t) -> p k t", k=2)
        rot_c = s.take("rot_c", T)
        rot_s = s.take("rot_s", T)
        kv1 = s.take("kv1", 2 * P).rearrange("p (b f) -> p b f", b=2)
        kv0 = s.take("kv0", P)
        sc_w2 = s.take("sc_w", 4 * (2 * T - P)).rearrange("p (b a t) -> p b a t", b=2, a=2)
        sc_m2 = s.take("sc_m", 4 * N_META).rearrange("p (b a t) -> p b a t", b=2, a=2)
        neg_max, sums, sinks_e = (s.take(n, 6).rearrange("p (w a) -> p w a", a=2) for n in ("mx", "su", "sk"))
        p1 = s.take("p1", 2 * 3 * P).rearrange("p (a t) -> p a t", a=2)
        p0 = s.take("p0", 2 * T).rearrange("p (a t) -> p a t", a=2)
        o_f = s.take("o_f", T)
        assert s.at <= SCRATCH, s.at

        s = Columns(scratch)
        f_gate = s.take("f_gate", 2 * T).rearrange("p (k t) -> p k t", k=2)
        f_val = s.take("f_val", 2 * T).rearrange("p (k t) -> p k t", k=2)
        f_th = s.take("f_th", 2 * T).rearrange("p (k t) -> p k t", k=2)
        f_act = s.take("f_act", 2 * T).rearrange("p (k t) -> p k t", k=2)
        ln_pivot, ln_mu, ln_msq, ln_rstd = (s.take(n, T) for n in ("pivot", "mu", "msq", "rstd"))
        ln_d = s.take("ln_d", 3 * 2 * T).rearrange("p (b w t) -> p b w t", b=3, w=2)
        ln_sums = s.take("ln_sums", 2 * T).rearrange("p (w t) -> p w t", w=2)
        assert s.at <= SCRATCH, s.at

        const_in = sem("const_in")
        h0_in = [sem(f"h0_in{n}") for n in range(HG)]
        mask1_in = sem("mask1_in")
        ones_set = sem("ones_set")
        halved = sem("halved")
        raw_in = [sem(f"raw_in{n}") for n in range(RING)]
        hi_ready = sem("hi_ready")
        lo_ready = sem("lo_ready")
        chunk_done = sem("chunk_done")
        bank_free = [sem(f"bank_free{n}") for n in range(RING)]
        h_ready = sem("h_ready")
        h_hi_ready = sem("h_hi_ready")
        feat_ready = sem("feat_ready")
        feat_hi_ready = sem("feat_hi_ready")
        dve_step, act_step = sem("dve_step"), sem("act_step")
        gates_exp, gates_rows, gates_turned, gates_cols, g_lr_ready = (sem(x) for x in (
            "gates_exp", "gates_rows", "gates_turned", "gates_cols", "g_lr_ready"))
        s_scaled, s_tanh, s_conv, s_scores, s_rows, s_bc, s_masked, s_diag, s_exp, s_mix = (sem("s_" + x) for x in (
            "scaled", "tanh", "conv", "scores", "rows", "bc", "masked", "diag", "exp", "mix"))
        s_xt, s_xd, s_y, s_ztanh, s_yread, s_yz, s_sq, s_stat, s_std, s_yn = (sem("s_" + x) for x in (
            "xt", "xd", "y", "ztanh", "yread", "yz", "sq", "stat", "std", "yn"))
        gw_in, g_mm, g_gexp, g_cum, g_sub, g_dec, g_zq, g_zend, g_sc, g_acc, g_scored, g_cross = (
            sem("g_" + x) for x in (
                "w_in", "mm", "gexp", "cum", "sub", "dec", "z", "zend", "sc", "acc", "scored", "cross"))
        g_vt, g_vcopy, g_rtanh, g_o, g_osb, g_sqr, g_st, g_std, g_yn = (sem("g_" + x) for x in (
            "vt", "vcopy", "rtanh", "o", "osb", "sqr", "st", "std", "yn"))
        a_raw, a_swap, a_rot, a_vt, a_vcopy, a_score, a_max, a_exp, a_norm, a_pt, a_p0, a_p1, a_o, a_of = (
            sem("a_" + x) for x in (
                "raw", "swap", "rot", "vt", "vcopy", "score", "max", "exp", "norm", "pt", "p0", "p1", "o", "of"))
        f_scaled, f_pair, f_tanh, f_mul = (sem("f_" + x) for x in ("scaled", "pair", "tanh", "mul"))
        l_pivot_sum, l_pivot, l_d, l_sq, l_acc, l_mean, l_msq, l_var, l_std, l_scaled, l_norm = (
            sem("l_" + x) for x in (
                "pivot_sum", "pivot", "d", "sq", "acc", "mean", "msq", "var", "std", "scaled", "norm"))
        stored = sem("stored")

        block = ctx.enter_context(nc.Block())

        def first_token(name):
            return Q0 if name == "swa_out" else N_META if name.startswith("down1") else 0

        LN_OF = {"gla_out": 0, "down02": 1, "swa_out": 2, "down12": 3}
        OUT_PASSES = {"ssd_out": KT, "gla_out": KT, "swa_out": KT}
        for layer in range(DEPTH):
            for n, (_, tiles) in enumerate(FFN_PASSES):
                OUT_PASSES[f"down{layer}{n}"] = tiles

        FEAT = {}
        total = 0
        for name, n in [("ssd_out", SSD_GROUPS), ("gla_out", GLA_HEADS), ("swa_out", 0)]:
            FEAT[name] = (total, total + n)
            total += n
        for layer in range(DEPTH):
            if layer == 1:
                FEAT["swa_out"] = (total, total + KT)
                total += KT
            for n, (_, tiles) in enumerate(FFN_PASSES):
                FEAT[f"down{layer}{n}"] = (total, total + tiles)
                total += tiles

        def last_pass(name):
            return BASE[name] + KT == N_CHUNKS

        AFTER_LN = [BASE["up00"], BASE["swa"], BASE["up10"]]

        def ln_buf(n):
            return (n - 1) % 3

        def swa_tile(m, k, lag, has_before, has_own=True):
            r = k - lag
            if r >= 0 and has_own:
                return 4 * m + r, m, r
            if 0 <= r + SWA_PER < 4 and has_before:
                return 4 * m + (r + SWA_PER - 4), m - 1, r + SWA_PER
            return None

        @block.sync
        def _(sp):
            def load(ch, k, width):
                if not ch.first_turn(k):
                    sp.wait_ge(lo_ready, ch.number(k) - (RING - 1))
                sl = ch.slot(k)
                sp.dma_start(raw[:, sl, 0:width, :].rearrange("p k n -> p (k n)"),
                             stream[ch.number(k), :, 0:width * P]).then_inc(raw_in[sl], 16)

            def load_run(base, n, width):
                whole = n // RING
                if whole > 1:
                    with sp.Fori(0, whole) as i:
                        for k in range(RING):
                            load(Chunks(base, RING, i), k, width)
                else:
                    whole = 0
                for k in range(whole * RING, n):
                    load(Chunks(base, RING, 0), k, width)

            load(Chunks(0, RING, 0), 0, KT)
            for g, (at, n) in enumerate(H_GROUPS):
                sp.dma_start(res[:, at:at + n, :], h0[:, at:at + n, :]).then_inc(h0_in[g], 16)
            load(Chunks(0, RING, 0), 1, KT)
            sp.dma_start(tab[:, :], table).then_inc(const_in, 16)
            sp.dma_start(msk[:, 0:mk0.at], masks[0, :, 0:mk0.at]).then_inc(const_in, 16)
            load(Chunks(0, RING, 0), 2, KT)
            load_run(RING, BASE["up00"] - RING, KT)
            for layer in range(DEPTH):
                if layer == 1:
                    load_run(BASE["swa"], SWA_PER * SWA_KV_HEADS // 2 + KT, KT)
                for n, (_, tiles) in enumerate(FFN_PASSES):
                    load_run(BASE[f"up{layer}{n}"], 2 * tiles, KT)
                    load_run(BASE[f"down{layer}{n}"], KT, tiles)
            for g, (at, n) in enumerate(H_GROUPS):
                sp.wait_ge(l_norm, HG * (2 * DEPTH - 1) + g + 1)
                sp.dma_start(out[:, at:at + n, :], res[:, at:at + n, N_META:T]).then_inc(stored, 16)
            sp.wait_ge(stored, 16 * HG)

        @block.gpsimd
        def _(pool):
            pool.memset(ones[:, :], 1.0).then_inc(ones_set, 1)
            pool.memset(scratch[:, :], 0.0).then_inc(ones_set, 1)
            for n, v in enumerate((4 * RMS_EPS, RMS_EPS, LN_EPS)):
                pool.memset(eps[:, n:n + 1], v).then_inc(ones_set, 1)

            def gla(hd):
                ch = Chunks(BASE["gla"], GLA_PER, hd)
                if not isinstance(hd, int) or hd:
                    pool.wait_ge(g_mm, hd)
                pool.dma_start(gate_w[2 * GLA_RANK:, :], gate_w2[:, bass.ds(GLA_DK * hd, GLA_DK)]).then_inc(gw_in, 16)
                for k in range(4):
                    pool.wait_ge(bank_free[ch.slot(k)], ch.turn(k) + 1)
                for lv, half in enumerate(LEVELS):
                    lo, n = (0, T) if half < 16 else (N_META, 2 * P)
                    view = lambda x: x[:, :, lo:lo + n].rearrange("p k (n w) -> p k n w", w=2 * half)
                    pool.wait_ge(g_dec, 8 * hd + lv + 1)
                    if lv or not isinstance(hd, int) or hd:
                        pool.wait_ge(g_sc, 9 * hd + (lv + 1 if lv else 0))
                    pool.tensor_tensor(view(z_q)[:, :, :, half:], view(dec)[:, :, :, half:],
                                       view(q_g)[:, :, :, half:], ALU.mult)
                    pool.tensor_tensor(view(z_k)[:, :, :, 0:half], view(dec)[:, :, :, 0:half],
                                       view(k_g)[:, :, :, 0:half], ALU.mult).then_inc(g_zq, 1)
                pool.wait_ge(g_dec, 8 * hd + 8)
                pool.wait_ge(g_sc, 9 * hd + 8)
                pool.tensor_tensor(z_q[:, :, N_META:T], exp_cum[:, :, N_META:T], q_g[:, :, N_META:T], ALU.mult)
                pool.tensor_tensor(z_k[:, :, 0:B2[0]], dec[:, :, 0:B2[0]], k_g[:, :, 0:B2[0]],
                                   ALU.mult).then_inc(g_zq, 1)

            gla(0)
            with pool.Fori(0, GLA_HEADS - 1) as i:
                gla(i + 1)
            pool.wait_ge(g_scored, GLA_HEADS)
            pool.dma_start(msk[:, P:mk1.at], masks[1, :, P:mk1.at]).then_inc(mask1_in, 16)

            for ln, t0 in enumerate(LN_FROM):
                def add(n, buf):
                    pool.wait_ge(l_sq, KT * ln + n + 1)
                    pool.wait_ge(l_acc, (KT - 1) * ln + n)
                    pool.tensor_tensor(ln_sums[:, :, t0:T], ln_sums[:, :, t0:T], ln_d[:, buf, :, t0:T],
                                       ALU.add).then_inc(l_acc, 1)

                pool.wait_ge(l_sq, KT * ln + 1)
                if ln:
                    pool.wait_ge(l_mean, ln)
                pool.tensor_copy(ln_sums[:, :, t0:T], ln_d[:, ln_buf(0), :, t0:T]).then_inc(l_acc, 1)
                with pool.Fori(0, 4) as i:
                    for k in range(3):
                        add(i * 3 + (k + 1), k)
                for n in (13, 14):
                    add(n, ln_buf(n))
                if ln < 2 * DEPTH - 1:
                    for g, (at, n) in enumerate(H_GROUPS):
                        r = slice(at, at + n)
                        pool.wait_ge(h_hi_ready, HG * (ln + 1) + g + 1)
                        pool.tensor_tensor(h_lo[:, r, t0:T], res[:, r, t0:T], h_hi[:, r, t0:T].bitcast(F32),
                                           ALU.subtract).then_inc(h_ready, 1)

        @block.scalar
        def _(act):
            step = Steps(act, act_step)
            A = nc.scalar.activation

            def split_hi(ch, k):
                sl = ch.slot(k)
                act.wait_ge(raw_in[sl], (ch.turn(k) + 1) * 16)
                if not ch.first_turn(k):
                    act.wait_ge(chunk_done, ch.number(k) - (RING - 1))
                A(w_hi[:, sl, :, :], raw[:, sl, :, :], ACT.Copy).then_inc(hi_ready, 1)

            def bank(ch, k):
                return banks[ch.slot(k)]

            c = Chunks(0, RING, 0)
            split_hi(c, 0)
            for g, (at, n) in enumerate(H_GROUPS):
                act.wait_ge(h0_in[g], 16)
                A(h_hi[:, at:at + n, :], res[:, at:at + n, :], ACT.Copy).then_inc(h_hi_ready, 1)
            split_hi(c, 1)

            split_hi(c, 2)
            act.wait_ge(const_in, 32)
            act.wait_ge(ones_set, 5)
            H = SSD_HEADS
            act.wait_ge(chunk_done, 1)
            A(g_lr[H:H + GLA_RANK, :], banks[0][H:H + GLA_RANK, 0:T], ACT.Copy).then_inc(g_lr_ready, 1)
            A(dt_x[0:H, :], banks[0][0:H, 0:T], ACT.Identity, bias=tb["dt_bias"][0:H, :]).then_inc(bank_free[0], 1)
            act.wait_ge(bank_free[0], 1)
            step.link(A(dt_e[0:H, :], dt_x[0:H, :], ACT.Abs))
            A(a_neg[0:H, :], tb["a_log"][0:H, :], ACT.Exp).then_inc(gates_exp, 1)
            A(dt_e[0:H, :], dt_e[0:H, :], ACT.Exp, scale=-1.0).then_inc(gates_exp, 1)

            act.wait_ge(halved, 3)

            def ssd_conv(ch, k, g, t):
                act.wait_ge(chunk_done, ch.number(k) + 1)
                n = 4 * g + t
                if t >= 2 or not isinstance(g, int) or g:
                    act.wait_ge(s_conv, n - 1)
                if t < 2 and (not isinstance(g, int) or g):
                    act.wait_ge(bank_free[ch.slot(k - 2)], ch.turn(k - 2) + 1)
                w = lambda j: tb["ssd_conv"][:, bass.ds(20 * g + 5 * t + j, 1)]
                A(pre[:, t % 2, :], bank(ch, k)[:, 0:T], ACT.Identity, bias=w(4), scale=w(3)).then_inc(s_scaled, 1)
                act.wait_ge(bank_free[ch.slot(k)], ch.turn(k) + 1)
                A(th[:, t % 2, :], pre[:, t % 2, :], ACT.Tanh).then_inc(s_tanh, 1)

            def ssd_heads(g, pair):
                for h in (2 * pair, 2 * pair + 1):
                    b = banks[5 + h % 2]
                    act.wait_ge(s_diag, 4 * g + h + 1)
                    col0 = lambda j: cols0[0:N_META, bass.ds(32 * j + 4 * g + h, 1)]
                    col1 = cols1[:, bass.ds(32 * 2 + 4 * g + h, 1)]
                    A(dec0[0:N_META, h, 0:N_META], dec0[0:N_META, h, 0:N_META], ACT.Exp)
                    A(dec1[:, h, :].rearrange("p (b t) -> p b t", b=3)[:, 0::2, :],
                      dec1[:, h, :].rearrange("p (b t) -> p b t", b=3)[:, 0::2, :], ACT.Exp)
                    A(dec0[0:N_META, h, B1[0]:B1[1]], b[0:N_META, B1[0]:B1[1]], ACT.Exp, bias=col0(1))
                    A(dec0[0:N_META, h, B2[0]:B2[1]], b[0:N_META, B2[0]:B2[1]], ACT.Exp, bias=col0(2))
                    A(dec1[:, h, P:2 * P], b[:, B2[0]:B2[1]], ACT.Exp, bias=col1).then_inc(s_exp, 1)

            def ssd_square(g):
                act.wait_ge(s_yz, g + 1)
                A(ssd_z[:, :, :], ssd_y[:, :, :], ACT.Square).then_inc(s_sq, 1)

            def ssd_sqrt(g):
                act.wait_ge(s_stat, g + 1)
                A(ssd_rstd[:, :], banks[7][:, 0:T], ACT.Sqrt, scale=1.0 / (2 * P), bias=eps[:, 0:1]).then_inc(s_std, 1)

            def ssd_hi(g):
                act.wait_ge(s_yn, g + 1)
                A(feat_hi[:, bass.ds(2 * g, 2), :], ssd_y[:, :, :], ACT.Copy).then_inc(feat_hi_ready, 1)

            def ssd(g, first):
                ch = Chunks(BASE["ssd"], SSD_PER, g)
                split_hi(ch, 2)
                if not first:
                    ssd_square(g - 1)
                ssd_conv(ch, 0, g, 0)
                split_hi(ch, 3)
                if not first:
                    ssd_sqrt(g - 1)
                ssd_conv(ch, 1, g, 1)
                split_hi(ch, 4)
                if first:
                    ssd_conv(ch, 2, g, 2)
                    ssd_heads(g, 0)
                else:
                    ssd_heads(g, 0)
                    ssd_conv(ch, 2, g, 2)
                split_hi(ch, 5)
                ssd_conv(ch, 3, g, 3)
                split_hi(ch, 6)
                ssd_heads(g, 1)
                for t in range(2):
                    if t:
                        split_hi(ch, 7)
                    act.wait_ge(chunk_done, ch.number(4 + t) + 1)
                    act.wait_ge(s_conv, 4 * g + t + 3)
                    A(th_z[:, t, :], bank(ch, 4 + t)[:, 0:T], ACT.Tanh, scale=0.5).then_inc(s_ztanh, 1)
                if not first:
                    ssd_hi(g - 1)

            ssd(0, True)
            step.loop(SSD_GROUPS - 1, ACT_STEPS["ssd"], lambda i: ssd(i + 1, False))
            split_hi(Chunks(BASE["ssd_out"], RING, 0), 2)
            ssd_square(SSD_GROUPS - 1)
            ssd_sqrt(SSD_GROUPS - 1)
            ssd_hi(SSD_GROUPS - 1)

            def out_pass(name, split_2=True):
                base, last, ln = BASE[name], last_pass(name), LN_OF.get(name)
                t0 = first_token(name)
                if split_2:
                    split_hi(Chunks(base, RING, 0), 2)
                if ln is None:
                    def body(i):
                        for k in range(RING):
                            split_hi(Chunks(base + 1, RING, i), k + 2)

                    step.loop(KT // RING, 0, body)
                    return

                def square(n, buf):
                    act.wait_ge(l_d, n + (KT * ln + 1))
                    A(ln_d[:, buf, 1, t0:T], ln_d[:, buf, 0, t0:T], ACT.Square).then_inc(l_sq, 1)

                ch = Chunks(base + 1, RING, 0)
                split_hi(ch, 2)
                split_hi(ch, 3)
                act.wait_ge(l_pivot_sum, ln + 1)
                A(ln_pivot[:, t0:T], banks[3][:, t0:T], ACT.Copy, scale=1.0 / P).then_inc(l_pivot, 1)
                split_hi(ch, 4)
                for n in range(3):
                    square(n, ln_buf(n))

                def body(i):
                    for k in range(RING):
                        split_hi(Chunks(base + 4, RING, i), k + 2)
                        square(i * RING + (k + 3), (k + 2) % 3)

                step.loop(3, 0, body)
                for n in range(13, KT):
                    if not last or n + 2 < KT:
                        split_hi(Chunks(base, RING, 0), n + 2)
                    square(n - 1, ln_buf(n - 1))
                square(KT - 1, ln_buf(KT - 1))

            out_pass("ssd_out", False)

            def gla_level(hd, lv):
                half = LEVELS[lv]
                lo = 0 if half < 16 else N_META
                act.wait_ge(g_sub, 7 * hd + lv + 1)
                A(dec[:, :, lo:T], dec[:, :, lo:T], ACT.Exp).then_inc(g_dec, 1)

            def gla_tail(hd):
                for j in range(4):
                    act.wait_ge(g_o, 4 * hd + j + 1)
                    if j or not isinstance(hd, int) or hd:
                        act.wait_ge(g_st, 4 * hd + j)
                    A(o_sq[:, :], banks[5 + j % 2][:, 0:T], ACT.Square).then_inc(g_sqr, 1)
                    A(o_g[:, j, :], banks[5 + j % 2][:, 0:T], ACT.Copy).then_inc(g_osb, 1)

            def gla_cross(hd):
                act.wait_ge(g_sc, 9 * hd + 9)
                A(a1[:, P:2 * P], banks[3][:, 0:P], ACT.Copy)
                A(a0[0:N_META, N_META:T], banks[3][0:N_META, P:3 * P], ACT.Copy).then_inc(g_cross, 1)

            def gla_sqrt(hd):
                act.wait_ge(g_st, 4 * hd + 4)
                A(o_rstd[:, :], banks[7][:, 0:T], ACT.Sqrt, scale=1.0 / GLA_DV, bias=eps[:, 1:2]).then_inc(g_std, 1)

            def gla_hi(hd):
                act.wait_ge(g_yn, hd + 1)
                A(feat_hi[:, bass.ds(4 * hd, 4), :], o_g[:, :, :], ACT.Copy).then_inc(feat_hi_ready, 1)

            def gla(hd, first):
                ch = Chunks(BASE["gla"], GLA_PER, hd)
                for k in range(GLA_PER):
                    split_hi(ch, k + 2)
                    if k == 0 and not first:
                        gla_cross(hd - 1)
                    if 3 <= k < 10:
                        gla_level(hd, k - 3)
                    act.wait_ge(chunk_done, ch.number(k) + 1)
                    if k < 2:
                        A(q_g[:, k, :], bank(ch, k)[:, 0:T], ACT.Copy,
                          scale=float(GLA_DK) ** -0.5).then_inc(bank_free[ch.slot(k)], 1)
                        if k == 0:
                            act.wait_ge(g_mm, hd + 1)
                            if not first:
                                act.wait_ge(g_zend, hd)
                                act.wait_ge(bank_free[ch.slot(-1)], ch.turn(-1) + 1)
                            for t in range(2):
                                last = step(A(g_z.rearrange("p (k t) -> p k t", k=2)[:, t, :], banks[3 + t][:, 0:T],
                                              ACT.Identity, bias=tb["gate_b"][:, bass.ds(2 * hd + t, 1)]))
                            step.after(last)
                            A(g_e, g_z, ACT.Abs).then_inc(g_gexp, 1)
                            act.wait_ge(g_gexp, 2 * hd + 1)
                            A(g_e, g_e, ACT.Exp, scale=-1.0).then_inc(g_gexp, 1)
                            if not first:
                                gla_tail(hd - 1)
                        if k == 1 and not first:
                            gla_sqrt(hd - 1)
                    elif k < 4:
                        A(k_g[:, k - 2, :], bank(ch, k)[:, 0:T], ACT.Copy).then_inc(bank_free[ch.slot(k)], 1)
                    elif k < 8:
                        j = k - 4
                        if j >= 2 or not first:
                            act.wait_ge(g_vt, 4 * hd + j - 1)
                        A(vfm[:, j % 2, :], bank(ch, k)[:, 0:T], ACT.Copy).then_inc(bank_free[ch.slot(k)], 1)
                        if k == 4 and not first:
                            gla_hi(hd - 1)
                    else:
                        j = k - 8
                        if j >= 2:
                            act.wait_ge(bank_free[ch.slot(k - 2)], ch.turn(k - 2) + 1)
                        A(th_r[:, j % 2, :], bank(ch, k)[:, 0:T], ACT.Tanh, scale=0.5).then_inc(g_rtanh, 1)
                        if k == 10:
                            act.wait_ge(g_vt, 4 * hd + 4)
                            act.wait_ge(g_zq, 8 * hd + 7)
                            A(exp_cum[:, :, :], cum[:, :, :], ACT.Exp)
                            for t in range(2):
                                for n, (lo, hi) in enumerate((M0, B1)):
                                    ins = A(dec[:, t, lo:hi], cum[:, t, lo:hi], ACT.Exp, scale=-1.0,
                                            bias=cum[:, t, hi - 1:hi])
                            ins.then_inc(g_dec, 1)
            gla(0, True)
            step.loop(GLA_HEADS - 1, ACT_STEPS["gla"], lambda i: gla(i + 1, False))
            split_hi(Chunks(BASE["gla_out"], RING, 0), 2)
            gla_cross(GLA_HEADS - 1)
            gla_tail(GLA_HEADS - 1)
            gla_sqrt(GLA_HEADS - 1)
            gla_hi(GLA_HEADS - 1)
            out_pass("gla_out", False)

            def layer_norm(n, last):
                t0 = LN_FROM[n]
                act.wait_ge(l_mean, n + 1)
                A(ln_msq[:, t0:T], banks[3][:, t0:T], ACT.Square, scale=1.0 / D_MODEL).then_inc(l_msq, 1)
                act.wait_ge(l_var, n + 1)
                A(ln_rstd[:, t0:T], ln_rstd[:, t0:T], ACT.Sqrt, bias=eps[:, 2:3]).then_inc(l_std, 1)
                if not last:
                    split_hi(Chunks(AFTER_LN[n], RING, 0), 2)
                for g, (at, tiles) in enumerate(H_GROUPS):
                    act.wait_ge(l_scaled, HG * n + g + 1)
                    for j in range(at, at + tiles):
                        ins = A(res[:, j, t0:T], res[:, j, t0:T], ACT.Identity, scale=ln_tab[:, n, 0, j:j + 1],
                                bias=ln_tab[:, n, 1, j:j + 1])
                    ins.then_inc(l_norm, 1)
                    if not last:
                        act.wait_ge(l_norm, HG * n + g + 1)
                        A(h_hi[:, at:at + tiles, t0:T], res[:, at:at + tiles, t0:T], ACT.Copy).then_inc(h_hi_ready, 1)

            def ffn_hi(t0, q, n, buf):
                act.wait_ge(f_mul, n + 1)
                A(feat_hi[:, bass.ds(q, 1), t0:T], f_act[:, buf:buf + 1, t0:T], ACT.Copy).then_inc(feat_hi_ready, 1)

            def ffn_pair(layer, ch, j, q, n, tile, buf, first):
                t0 = N_META * layer
                after_ln = isinstance(tile, int) and tile == 0
                for w in range(2):
                    k = 2 * j + w
                    if w or not first or not after_ln:
                        split_hi(ch, k + 2)
                    if w == 1:
                        act.wait_ge(bank_free[ch.slot(k - 1)], ch.turn(k - 1) + 1)
                        A(f_th[:, buf, t0:T], f_gate[:, buf, t0:T], ACT.Tanh).then_inc(f_tanh, 1)
                    act.wait_ge(chunk_done, ch.number(k) + 1)
                    if w == 0 and not (isinstance(n, int) and n < 2):
                        act.wait_ge(f_mul, n - 1)
                    A((f_gate, f_val)[w][:, buf, t0:T], bank(ch, k)[:, t0:T], ACT.Identity,
                      bias=ffn_tab[:, layer, bass.ds(tile, 1), 4 * w + 3],
                      scale=ffn_tab[:, layer, bass.ds(tile, 1), 4 * w + 2]).then_inc(f_scaled, 1)
                    if w == 0 and not first:
                        ffn_hi(t0, q - 1, n - 1, 1 - buf)

            def ffn(layer):
                for p, (tile0, tiles) in enumerate(FFN_PASSES):
                    name, total, rest = f"up{layer}{p}", layer * FF_TILES + tile0, tiles % FFN_BODY
                    for j in range(rest):
                        ffn_pair(layer, Chunks(BASE[name], RING, 0), j, j, total + j, tile0 + j, j % 2, j == 0)

                    def body(i):
                        for j in range(FFN_BODY):
                            q = i * FFN_BODY + (rest + j)
                            ffn_pair(layer, Chunks(BASE[name] + 2 * rest, 2 * FFN_BODY, i), j, q, q + total,
                                     q + tile0, (rest + j) % 2, False)

                    step.loop(tiles // FFN_BODY, 0, body)
                    ffn_hi(N_META * layer, tiles - 1, total + tiles - 1, (tiles - 1) % 2)
                    out_pass(f"down{layer}{p}")

            layer_norm(0, False)
            ffn(0)
            layer_norm(1, False)

            def swa_exp(n, m, r):
                act.wait_ge(a_max, n + 1)
                sc_w, sc_m = sc_w2[:, r % 2, :, :], sc_m2[:, r % 2, :, :]
                for a in range(2):
                    A(sc_w[:, a, 0:N_META + P], sc_w[:, a, 0:N_META + P], ACT.Exp, bias=neg_max[:, 0, a:a + 1],
                      accum_out=sums[:, 0, a:a + 1])
                    A(sc_w[:, a, N_META + P:], sc_w[:, a, N_META + P:], ACT.Exp, bias=neg_max[:, 1, a:a + 1],
                      accum_out=sums[:, 1, a:a + 1])
                    A(sc_m[0:NQ, a, :], sc_m[0:NQ, a, :], ACT.Exp, bias=neg_max[0:NQ, 2, a:a + 1],
                      accum_out=sums[0:NQ, 2, a:a + 1])
                A(sinks_e[:, :, :], sinks_e[:, :, :], ACT.Exp).then_inc(a_exp, 1)

            def swa_p0(n, a):
                act.wait_ge(a_pt, 2 * n + a + 1)
                A(p0[0:N_META, a, Q0:T], banks[5][0:N_META, Q0:T], ACT.Copy).then_inc(a_p0, 1)

            def swa_out(n):
                act.wait_ge(a_o, n + 1)
                A(o_f[:, Q0:T], banks[7][:, Q0:T], ACT.Copy).then_inc(a_of, 1)
                act.wait_ge(a_of, n + 1)
                A(feat_hi[:, bass.ds(n, 1), Q0:T], o_f[:, Q0:T].unsqueeze(1), ACT.Copy).then_inc(feat_hi_ready, 1)

            def swa_slot(m, k, has_before, has_own=True):
                at = lambda lag: swa_tile(m, k, lag, has_before, has_own)
                if at(7):
                    swa_out(at(7)[0])
                if at(6):
                    swa_p0(at(6)[0], 0)
                if at(5):
                    swa_exp(*at(5))
                if at(6):
                    swa_p0(at(6)[0], 1)

            def swa(m, first):
                ch = Chunks(BASE["swa"], SWA_PER, m)
                for k in range(SWA_PER):
                    if k or not first:
                        split_hi(ch, k + 2)
                    swa_slot(m, k, not first)
                    act.wait_ge(chunk_done, ch.number(k) + 1)
                    if k == 0:
                        if not first:
                            act.wait_ge(a_rot, 5 * m - 4)
                        A(k_raw[:, :], bank(ch, k)[:, 0:T], ACT.Copy).then_inc(a_raw, 1)
                    elif k == 1:
                        if not first:
                            act.wait_ge(a_vt, m)
                        A(v_fm[:, :], bank(ch, k)[:, 0:T], ACT.Copy).then_inc(bank_free[ch.slot(k)], 1)
                    else:
                        r = k - 2
                        if r >= 2:
                            act.wait_ge(a_rot, 5 * m + r)
                        elif not first:
                            act.wait_ge(a_rot, 5 * m + (r - 1))
                        A(q_raw[:, r % 2, Q0:T], bank(ch, k)[:, Q0:T], ACT.Copy,
                          scale=float(SWA_D) ** -0.5).then_inc(a_raw, 1)

            swa(0, True)
            step.loop(SWA_KV_HEADS // 2 - 1, ACT_STEPS["swa"], lambda i: swa(i + 1, False))
            split_hi(Chunks(BASE["swa_out"], RING, 0), 2)
            for k in range(5):
                swa_slot(SWA_KV_HEADS // 2, k, True, False)
            out_pass("swa_out", False)
            layer_norm(2, False)
            ffn(1)
            layer_norm(3, True)

        @block.vector
        def _(dve):
            step = Steps(dve, dve_step)
            V = nc.vector
            TT, TS, STT = V.tensor_tensor, V.tensor_scalar, V.scalar_tensor_tensor

            def split_lo(ch, k):
                sl = ch.slot(k)
                dve.wait_ge(hi_ready, ch.number(k) + 1)
                TT(w_lo[:, sl, :, :], raw[:, sl, :, :], w_hi[:, sl, :, :].bitcast(F32),
                   ALU.subtract).then_inc(lo_ready, 1)

            def bank(ch, k):
                return banks[ch.slot(k)]

            def half_log1p_start(e, s_, s2, p):
                step.link(TS(s_, e, 2.0, None, ALU.add))
                step.link(V.reciprocal(s_, s_))
                step.link(TT(s_, s_, e, ALU.mult))
                step.link(TT(s2, s_, s_, ALU.mult))
                step.link(TS(p, s2, 1.0 / 15, None, ALU.mult))

            def half_log1p_terms(s2, p, terms):
                for n in terms:
                    step.link(STT(p, p, 1.0 / n, s2, ALU.add, ALU.mult))

            def half_log1p_end(s_, s2, p, terms):
                half_log1p_terms(s2, p, terms)
                step.link(STT(p, p, 1.0, s_, ALU.add, ALU.mult))

            c = Chunks(0, RING, 0)
            split_lo(c, 0)
            for g, (at, n) in enumerate(H_GROUPS):
                dve.wait_ge(h_hi_ready, g + 1)
                TT(h_lo[:, at:at + n, :], res[:, at:at + n, :], h_hi[:, at:at + n, :].bitcast(F32),
                   ALU.subtract).then_inc(h_ready, 1)
            split_lo(c, 1)

            dve.wait_ge(const_in, 32)
            dve.wait_ge(ones_set, 5)
            TS(tb["ssd_conv"], tb["ssd_conv"], 0.5, None, ALU.mult).then_inc(halved, 1)
            TS(tb["gla_norm"], tb["gla_norm"], 0.5, None, ALU.mult).then_inc(halved, 1)
            gates_half = tb["ffn"].rearrange("p (n w) -> p n w", w=8)[:, :, 0:4]
            TS(gates_half, gates_half, 0.5, None, ALU.mult).then_inc(halved, 1)

            split_lo(c, 2)
            H = SSD_HEADS
            dve.wait_ge(gates_exp, 2)
            half_log1p_start(dt_e[0:H, :], dt_s[0:H, :], dt_s2[0:H, :], dt_p[0:H, :])

            def gates_sums():
                half_log1p_end(dt_s[0:H, :], dt_s2[0:H, :], dt_p[0:H, :], (13, 11, 9, 7, 5, 3))
                step.link(TS(dt_s[0:H, :], dt_x[0:H, :], 0.0, None, ALU.max))
                step.link(STT(dt_v[0:H, :], dt_p[0:H, :], 2.0, dt_s[0:H, :], ALU.mult, ALU.add))
                step.link(TS(dt_e[0:H, :], dt_v[0:H, :], a_neg[0:H, :], -1.0, ALU.mult, ALU.mult))
                for lo, hi in (M0, B1, B2):
                    last = step(V.tensor_tensor_scan(acs[0:H, lo:hi], ones[0:H, 0:hi - lo], dt_e[0:H, lo:hi], 0.0,
                                                     ALU.mult, ALU.add))
                step.after(last)
                for lo, hi in (M0, B1):
                    last = step(TS(to_end[0:H, lo:hi], acs[0:H, lo:hi], acs[0:H, hi - 1:hi], -1.0,
                                   ALU.subtract, ALU.mult))
                step.after(last)
                TS(to_end2[0:H, :], to_end[0:H, M0[0]:M0[1]], acs[0:H, B1[1] - 1:B1[1]], None,
                   ALU.add).then_inc(gates_rows, 1)

            def gates_columns():
                dve.wait_ge(gates_turned, 1)
                step(V.tensor_copy(cols1[:, :], banks[7][:, 0:160]))
                V.tensor_copy(cols0[0:N_META, :], banks[7][0:N_META, 160:288]).then_inc(gates_cols, 1)
                dve.wait_ge(gates_cols, 1)

            def ssd_conv(ch, k, g, t):
                split_lo(ch, k + 2)
                u, y = bank(ch, k), pre[:, t % 2, :]
                dve.wait_ge(s_scaled, 4 * g + t + 1)
                w = lambda j: tb["ssd_conv"][:, bass.ds(20 * g + 5 * t + j, 1)]
                step.link(STT(y[:, 1:], u[:, 0:T - 1], w(2), y[:, 1:], ALU.mult, ALU.add))
                step.link(STT(y[:, 2:], u[:, 0:T - 2], w(1), y[:, 2:], ALU.mult, ALU.add))
                STT(y[:, 3:], u[:, 0:T - 3], w(0), y[:, 3:], ALU.mult, ALU.add).then_inc(bank_free[ch.slot(k)], 1)
                dve.wait_ge(s_tanh, 4 * g + t + 1)
                STT(conv_out[:, t, :], th[:, t % 2, :], 1.0, y, ALU.add, ALU.mult).then_inc(s_conv, 1)

            def ssd_exponents(g, pair):
                for h in (2 * pair, 2 * pair + 1):
                    b = banks[5 + h % 2]
                    dve.wait_ge(s_bc, 4 * g + h + 1)
                    TS(dec0[0:N_META, h, 0:N_META], b[0:N_META, 0:N_META], cols0[0:N_META, bass.ds(4 * g + h, 1)],
                       0.0, ALU.subtract, ALU.min)
                    TS(dec1[:, h, 0:P], b[:, B1[0]:B1[1]], cols1[:, bass.ds(4 * g + h, 1)],
                       0.0, ALU.subtract, ALU.min)
                    TS(dec1[:, h, 2 * P:3 * P], b[:, B2[0]:B2[1]], cols1[:, bass.ds(32 + 4 * g + h, 1)],
                       0.0, ALU.subtract, ALU.min).then_inc(s_diag, 1)

            def ssd_mix(g, pair):
                for h in (2 * pair, 2 * pair + 1):
                    dve.wait_ge(s_exp, 4 * g + h + 1)
                    TT(dec0[0:N_META, h, :], dec0[0:N_META, h, :], s_g0[0:N_META, :], ALU.mult)
                    TT(dec1[:, h, :], dec1[:, h, :], s_g1[:, :], ALU.mult).then_inc(s_mix, 1)

            def ssd_gated(g):
                dve.wait_ge(s_y, 2 * g + 2)
                for t in range(2):
                    ins = STT(ssd_y[:, t, :], conv_out[:, 2 + t, :], tb["ssd_d"][:, bass.ds(2 * g + t, 1)],
                              banks[(7, 5)[t]][:, 0:T], ALU.mult, ALU.add)
                ins.then_inc(s_yread, 1)
                dve.wait_ge(s_yread, g + 1)
                TT(ssd_y[:, :, :], ssd_y[:, :, :], ssd_z[:, :, :], ALU.mult).then_inc(s_yz, 1)

            def ssd_normalise(g):
                dve.wait_ge(s_std, g + 1)
                step.link(V.reciprocal(ssd_rstd[:, :], ssd_rstd[:, :]))
                for t in range(2):
                    ins = STT(ssd_y[:, t, :], ssd_y[:, t, :], tb["ssd_norm"][:, bass.ds(2 * g + t, 1)],
                              ssd_rstd[:, :], ALU.mult, ALU.mult)
                ins.then_inc(s_yn, 1)

            def ssd_lo(g):
                dve.wait_ge(feat_hi_ready, g + 1)
                TT(feat_lo[:, bass.ds(2 * g, 2), :], ssd_y[:, :, :], feat_hi[:, bass.ds(2 * g, 2), :].bitcast(F32),
                   ALU.subtract).then_inc(feat_ready, 1)

            def ssd_head_rows(g):
                TT(head_rows[0:H, :, :], acs[0:H, :].unsqueeze(1).broadcast_to([H, 4, T]),
                   ident[0:H, bass.ds(4 * g, 4)].unsqueeze(2).broadcast_to([H, 4, T]), ALU.mult).then_inc(s_rows, 1)

            def ssd(g, first):
                ch = Chunks(BASE["ssd"], SSD_PER, g)
                ssd_conv(ch, 0, g, 0)
                if first:
                    gates_sums()
                    dve.wait_ge(gates_rows, 1)
                else:
                    dve.wait_ge(s_bc, 4 * g)
                ssd_head_rows(g)
                ssd_conv(ch, 1, g, 1)
                if first:
                    ssd_conv(ch, 2, g, 2)
                    gates_columns()
                    ssd_exponents(g, 0)
                else:
                    ssd_exponents(g, 0)
                    ssd_conv(ch, 2, g, 2)
                dve.wait_ge(s_scores, g + 1)
                step(TT(s_g0[0:N_META, :], banks[3][0:N_META, 0:T], mk0["causal_meta"][0:N_META, :], ALU.mult))
                TT(s_g1[:, :], banks[4][:, 0:3 * P], mk0["causal"], ALU.mult).then_inc(s_masked, 1)
                dve.wait_ge(s_masked, g + 1)
                ssd_mix(g, 0)
                ssd_conv(ch, 3, g, 3)
                ssd_exponents(g, 1)
                for t in range(2):
                    split_lo(ch, 4 + t + 2)
                    dve.wait_ge(s_ztanh, 2 * g + t + 1)
                    if t == 0 and not first:
                        dve.wait_ge(s_stat, g)
                    STT(ssd_z[:, t, :], th_z[:, t, :], 1.0, bank(ch, 4 + t)[:, 0:T], ALU.add,
                        ALU.mult).then_inc(bank_free[ch.slot(4 + t)], 1)
                    if t == 0:
                        ssd_mix(g, 1)
                        dve.wait_ge(s_xt, g + 1)
                        for b in range(2):
                            step(TT(xd1[:, b, :].rearrange("p (h d) -> p h d", h=4),
                                    banks[3][:, 256 * b:256 * b + 256].rearrange("p (h d) -> p h d", h=4),
                                    cols1[:, bass.ds(96 + 32 * b + 4 * g, 4)].unsqueeze(2).broadcast_to([P, 4, SSD_P]),
                                    ALU.mult))
                        TT(xd0[0:N_META, :].rearrange("p (h d) -> p h d", h=4),
                           banks[4][0:N_META, 0:256].rearrange("p (h d) -> p h d", h=4),
                           cols0[0:N_META, bass.ds(96 + 4 * g, 4)].unsqueeze(2).broadcast_to([N_META, 4, SSD_P]),
                           ALU.mult).then_inc(s_xd, 1)
                        if not first:
                            ssd_normalise(g - 1)
                if not first:
                    ssd_lo(g - 1)
                    dve.wait_ge(feat_ready, g)
                ssd_gated(g)

            ssd(0, True)
            step.loop(SSD_GROUPS - 1, DVE_STEPS["ssd"], lambda i: ssd(i + 1, False))
            split_lo(Chunks(BASE["ssd_out"], RING, 0), 2)
            ssd_normalise(SSD_GROUPS - 1)
            ssd_lo(SSD_GROUPS - 1)

            def out_pass(name, scale, split_2=True):
                base, last, ln = BASE[name], last_pass(name), LN_OF.get(name)
                t0 = first_token(name)

                def one(ch, k, n, split=True):
                    if split:
                        split_lo(ch, k + 2)
                    dve.wait_ge(chunk_done, ch.number(k) + 1)
                    r = res[:, bass.ds(n, 1), t0:T]
                    ps = bank(ch, k)[:, t0:T].unsqueeze(1)
                    if scale:
                        STT(r, r, ALPHA, ps, ALU.mult, ALU.add).then_inc(bank_free[ch.slot(k)], 1)
                    else:
                        TT(r, r, ps, ALU.add).then_inc(bank_free[ch.slot(k)], 1)
                    if ln is not None:
                        dve.wait_ge(bank_free[ch.slot(k)], ch.turn(k) + 1)

                def centre(n, buf):
                    if not isinstance(n, int) or n >= 3:
                        dve.wait_ge(l_acc, n + ((KT - 1) * ln - 2))
                    TT(ln_d[:, buf, 0:1, t0:T], res[:, bass.ds(n, 1), t0:T], ln_pivot[:, t0:T].unsqueeze(1),
                       ALU.subtract).then_inc(l_d, 1)

                one(Chunks(base, RING, 0), 0, 0, split_2)
                if ln is None:
                    def body(i):
                        for k in range(RING):
                            one(Chunks(base + 1, RING, i), k, i * RING + (k + 1))

                    step.loop(KT // RING, 0, body)
                    return

                one(Chunks(base, RING, 0), 1, 1)
                one(Chunks(base, RING, 0), 2, 2)
                dve.wait_ge(l_pivot, ln + 1)
                for n in range(3):
                    centre(n, ln_buf(n))
                one(Chunks(base, RING, 0), 3, 3)
                centre(3, ln_buf(3))

                def body(i):
                    for k in range(RING):
                        n = i * RING + (k + 4)
                        one(Chunks(base + 4, RING, i), k, n)
                        centre(n, k)

                step.loop(3, 0, body)
                for n in range(13, KT):
                    one(Chunks(base, RING, 0), n, n, not last or n + 2 < KT)
                    centre(n, ln_buf(n))

            out_pass("ssd_out", True, False)

            def gla_sub(hd, lv):
                half = LEVELS[lv]
                lo, n = (0, T) if half < 16 else (N_META, 2 * P)
                view = lambda x: x[:, :, lo:lo + n].rearrange("p k (n w) -> p k n w", w=2 * half)
                ref = view(cum)[:, :, :, half - 1:half].broadcast_to([P, 2, n // (2 * half), half])
                if lv:
                    dve.wait_ge(g_zq, 8 * hd + lv)
                TT(view(dec)[:, :, :, half:], view(cum)[:, :, :, half:], ref, ALU.subtract)
                TT(view(dec)[:, :, :, 0:half], ref, view(cum)[:, :, :, 0:half], ALU.subtract).then_inc(g_sub, 1)

            def gla_acc(hd, lv):
                b = banks[3 + lv % 2]
                dve.wait_ge(g_sc, 9 * hd + lv + 1)
                mask = mk0["levels"][:, lv * P:(lv + 1) * P]
                diag = a1.rearrange("p (b t) -> p b t", b=3)[:, 0::2, :]
                both = b[:, 0:2 * P].rearrange("p (b t) -> p b t", b=2)
                mask2 = mask.unsqueeze(1).broadcast_to([P, 2, P])
                tmp = a_tmp[:, 0:2 * P].rearrange("p (b t) -> p b t", b=2)
                if lv == 0:
                    step(TT(a0[0:N_META, 0:N_META], b[0:N_META, 2 * P:T], mask[0:N_META, 0:N_META], ALU.mult))
                    TT(diag, both, mask2, ALU.mult).then_inc(g_acc, 1)
                    dve.wait_ge(g_acc, 8 * hd + 1)
                    return
                meta = lv > 0 and LEVELS[lv - 1] < 16
                if meta:
                    step(TT(a_tmp[0:N_META, 2 * P:T], b[0:N_META, 2 * P:T], mask[0:N_META, 0:N_META], ALU.mult))
                TT(tmp, both, mask2, ALU.mult).then_inc(g_acc, 1)
                dve.wait_ge(g_acc, 8 * hd + lv + 1)
                if meta:
                    step(TT(a0[0:N_META, 0:N_META], a0[0:N_META, 0:N_META], a_tmp[0:N_META, 2 * P:T], ALU.add))
                ins = TT(diag, diag, tmp, ALU.add)
                if lv == len(LEVELS):
                    ins.then_inc(g_scored, 1)
                else:
                    step.link(ins)

            def gla_normalise(hd):
                dve.wait_ge(g_std, hd + 1)
                step.link(V.reciprocal(o_rstd[:, :], o_rstd[:, :]))
                for j in range(4):
                    last = step(STT(o_g[:, j, :], o_g[:, j, :], tb["gla_norm"][:, bass.ds(4 * hd + j, 1)],
                                    o_rstd[:, :], ALU.mult, ALU.mult))
                step.after(last)
                TT(o_g[:, :, :], o_g[:, :, :], r_g[:, :, :], ALU.mult).then_inc(g_yn, 1)

            def gla_lo(hd):
                dve.wait_ge(feat_hi_ready, SSD_GROUPS + hd + 1)
                TT(feat_lo[:, bass.ds(4 * hd, 4), :], o_g[:, :, :], feat_hi[:, bass.ds(4 * hd, 4), :].bitcast(F32),
                   ALU.subtract).then_inc(feat_ready, 1)

            def gla(hd, first):
                ch = Chunks(BASE["gla"], GLA_PER, hd)
                for k in range(GLA_PER):
                    if 4 <= k < 10:
                        gla_sub(hd, k - 3)
                    split_lo(ch, k + 2)
                    if k == 0:
                        f = lambda x: x.rearrange("p k t -> p (k t)")
                        dve.wait_ge(g_gexp, 2 * hd + 2)
                        if not first:
                            dve.wait_ge(g_sc, 9 * hd)
                        half_log1p_start(g_e, f(dec), f(z_q), f(z_k))
                    if k == 1:
                        half_log1p_terms(f(z_q), f(z_k), (13, 11, 9, 7, 5, 3))
                    if k == 2:
                        half_log1p_end(f(dec), f(z_q), f(z_k), ())
                        step.link(TS(g_e, g_z, 0.0, 1.0 / GLA_TAU, ALU.min, ALU.mult))
                        step.link(STT(g_e, f(z_k), -2.0 / GLA_TAU, g_e, ALU.mult, ALU.add))
                        g2 = g_e.rearrange("p (k t) -> p k t", k=2)
                        for t in range(2):
                            for lo, hi in (M0, B1, B2):
                                ins = V.tensor_tensor_scan(cum[:, t, lo:hi], ones[:, 0:hi - lo], g2[:, t, lo:hi], 0.0,
                                                           ALU.mult, ALU.add)
                        ins.then_inc(g_cum, 1)
                        dve.wait_ge(g_cum, hd + 1)
                        gla_sub(hd, 0)
                    if k == 3 and not first:
                        gla_normalise(hd - 1)
                    if k == 5 and not first:
                        gla_lo(hd - 1)
                    if k == 5:
                        gla_acc(hd, 0)
                        gla_acc(hd, 1)
                    if k > 5:
                        gla_acc(hd, k - 4)
                    if 5 <= k < 9:
                        j = k - 5
                        b = banks[5 + j % 2]
                        dve.wait_ge(g_vt, 4 * hd + j + 1)
                        V.tensor_copy(vt1[:, :, j * P:(j + 1) * P],
                                      b[:, 0:2 * P].rearrange("p (b t) -> p b t", b=2))
                        V.tensor_copy(vt0[0:N_META, j * P:(j + 1) * P], b[0:N_META, 2 * P:3 * P]).then_inc(g_vcopy, 1)
                    if k == 11:
                        dve.wait_ge(g_zq, 8 * hd + 8)
                        for t in range(2):
                            ins = TS(z_k[:, t, B2[0]:B2[0] + N_META], z_k[:, t, 0:N_META],
                                     exp_cum[:, t, B1[1] - 1:B1[1]], None, ALU.mult)
                        ins.then_inc(g_zend, 1)
                    if k >= 8:
                        j = k - 8
                        dve.wait_ge(g_rtanh, 4 * hd + j + 1)
                        STT(r_g[:, j, :], th_r[:, j % 2, :], 1.0, bank(ch, k)[:, 0:T], ALU.add,
                            ALU.mult).then_inc(bank_free[ch.slot(k)], 1)

            gla(0, True)
            step.loop(GLA_HEADS - 1, DVE_STEPS["gla"], lambda i: gla(i + 1, False))
            split_lo(Chunks(BASE["gla_out"], RING, 0), 2)
            gla_normalise(GLA_HEADS - 1)
            gla_lo(GLA_HEADS - 1)
            out_pass("gla_out", False, False)

            def layer_norm(n):
                t0 = LN_FROM[n]
                wide = lambda x, g: x[:, t0:T].unsqueeze(1).broadcast_to([P, H_GROUPS[g][1], T - t0])
                part = lambda g: res[:, H_GROUPS[g][0]:sum(H_GROUPS[g]), t0:T]
                dve.wait_ge(l_msq, n + 1)
                STT(ln_rstd[:, t0:T], banks[4][:, t0:T], 1.0 / D_MODEL, ln_msq[:, t0:T], ALU.mult,
                    ALU.subtract).then_inc(l_var, 1)
                step.link(STT(ln_mu[:, t0:T], banks[3][:, t0:T], 1.0 / D_MODEL, ln_pivot[:, t0:T], ALU.mult, ALU.add))
                centred = step(TT(part(0), part(0), wide(ln_mu, 0), ALU.subtract))
                dve.wait_ge(l_std, n + 1)
                step.link(V.reciprocal(ln_rstd[:, t0:T], ln_rstd[:, t0:T]))
                step.after(centred)
                for g in range(HG):
                    TT(part(g), part(g), wide(ln_rstd, g), ALU.mult).then_inc(l_scaled, 1)
                    if g < HG - 1:
                        step.link(TT(part(g + 1), part(g + 1), wide(ln_mu, g + 1), ALU.subtract))
                if n < len(AFTER_LN):
                    split_lo(Chunks(AFTER_LN[n], RING, 0), 2)

            def ffn_lo(t0, q, feat, buf):
                dve.wait_ge(feat_hi_ready, feat + 1)
                TT(feat_lo[:, bass.ds(q, 1), t0:T], f_act[:, buf:buf + 1, t0:T],
                   feat_hi[:, bass.ds(q, 1), t0:T].bitcast(F32), ALU.subtract).then_inc(feat_ready, 1)

            def ffn_pair(layer, ch, j, q, n, tile, buf, before, first):
                t0 = N_META * layer
                after_ln = isinstance(tile, int) and tile == 0
                for w in range(2):
                    k = 2 * j + w
                    if w or not first or not after_ln:
                        split_lo(ch, k + 2)
                    dve.wait_ge(f_scaled, n * 2 + w + 1)
                    u, y = bank(ch, k), (f_gate, f_val)[w][:, buf, :]
                    tap = lambda x: ffn_tab[:, layer, bass.ds(tile, 1), 4 * w + x]
                    t1, t2 = max(t0, 1), max(t0, 2)
                    step.link(STT(y[:, t1:T], u[:, t1 - 1:T - 1], tap(1), y[:, t1:T], ALU.mult, ALU.add))
                    STT(y[:, t2:T], u[:, t2 - 2:T - 2], tap(0), y[:, t2:T], ALU.mult, ALU.add).then_inc(
                        bank_free[ch.slot(k)], 1)
                    if w == 0 and not first:
                        ffn_lo(t0, q - 1, q + (before - 1), 1 - buf)
                dve.wait_ge(f_tanh, n + 1)
                a, th_, g, v = (x[:, buf, t0:T] for x in (f_act, f_th, f_gate, f_val))
                step.link(STT(a, th_, 1.0, g, ALU.add, ALU.mult))
                TT(a, a, v, ALU.mult).then_inc(f_mul, 1)

            def ffn(layer):
                for p, (tile0, tiles) in enumerate(FFN_PASSES):
                    name, total, rest = f"up{layer}{p}", layer * FF_TILES + tile0, tiles % FFN_BODY
                    before = FEAT[f"down{layer}{p}"][0]
                    for j in range(rest):
                        ffn_pair(layer, Chunks(BASE[name], RING, 0), j, j, total + j, tile0 + j, j % 2, before,
                                 j == 0)

                    def body(i):
                        for j in range(FFN_BODY):
                            q = i * FFN_BODY + (rest + j)
                            ffn_pair(layer, Chunks(BASE[name] + 2 * rest, 2 * FFN_BODY, i), j, q, q + total,
                                     q + tile0, (rest + j) % 2, before, False)

                    step.loop(tiles // FFN_BODY, DVE_STEPS["up"], body)
                    ffn_lo(N_META * layer, tiles - 1, before + tiles - 1, (tiles - 1) % 2)
                    out_pass(f"down{layer}{p}", p == 0)

            layer_norm(0)
            ffn(0)
            layer_norm(1)

            def rotate(ch, k, n, src, dst, t0):
                dve.wait_ge(a_swap, n + 1)
                if not isinstance(n, int) or n:
                    dve.wait_ge(a_rot, n)
                step(TT(rot_c[:, t0:T], src[:, t0:T], mk1["cos"][:, t0:T], ALU.mult))
                TT(rot_s[:, t0:T], bank(ch, k)[:, t0:T], mk1["sin"][:, t0:T],
                   ALU.mult).then_inc(bank_free[ch.slot(k)], 1)
                dve.wait_ge(bank_free[ch.slot(k)], ch.turn(k) + 1)
                TT(dst[:, t0:T], rot_c[:, t0:T], rot_s[:, t0:T], ALU.add).then_inc(a_rot, 1)

            W1 = N_META + P
            W = 2 * T - P

            def swa_maxima(n, m, r):
                sc_w, sc_m = sc_w2[:, r % 2, :, :], sc_m2[:, r % 2, :, :]
                sink = tb["sinks"].rearrange("p (m a r) -> p m a r", a=2, r=4)[:, bass.ds(m, 1), :, r]
                sink3 = sink.broadcast_to([P, 3, 2])
                dve.wait_ge(a_score, n + 1)
                step(TT(sc_w[:, :, :], psum[:, 3:5, 0:W], mk1["window"].unsqueeze(1).broadcast_to([P, 2, W]), ALU.add))
                step(TT(sc_m[0:NQ, :, :], psum[0:NQ, 3:5, W:W + N_META],
                        mk1["window_meta"][0:NQ, :].unsqueeze(1).broadcast_to([NQ, 2, N_META]), ALU.add))
                step.link(V.tensor_copy(neg_max[:, 2:3, :], sink))
                step(V.reduce_max(neg_max[:, 0, :], sc_w[:, :, 0:W1], axis=AX.X))
                step(V.reduce_max(neg_max[:, 1, :], sc_w[:, :, W1:], axis=AX.X))
                step.link(V.reduce_max(neg_max[0:NQ, 2, :], sc_m[0:NQ, :, :], axis=AX.X))
                step.link(TT(neg_max[:, :, :], neg_max[:, :, :], sink3, ALU.max))
                step.link(TS(neg_max[:, :, :], neg_max[:, :, :], -1.0, None, ALU.mult))
                TT(sinks_e[:, :, :], neg_max[:, :, :], sink3, ALU.add).then_inc(a_max, 1)

            def swa_divide(n, m, r):
                sc_w, sc_m = sc_w2[:, r % 2, :, :], sc_m2[:, r % 2, :, :]
                dve.wait_ge(a_exp, n + 1)
                step.link(TT(sums[:, :, :], sums[:, :, :], sinks_e[:, :, :], ALU.add))
                step.link(V.reciprocal(sums[:, :, :], sums[:, :, :]))
                by = lambda w, rows, n_: sums[0:rows, w, :].unsqueeze(2).broadcast_to([rows, 2, n_])
                TT(sc_w[:, :, 0:W1], sc_w[:, :, 0:W1], by(0, P, W1), ALU.mult)
                TT(sc_w[:, :, W1:], sc_w[:, :, W1:], by(1, P, W - W1), ALU.mult)
                TT(sc_m[0:NQ, :, :], sc_m[0:NQ, :, :], by(2, NQ, N_META), ALU.mult).then_inc(a_norm, 1)

            def swa_p1(n, a):
                dve.wait_ge(a_pt, 2 * n + a + 1)
                V.tensor_copy(p1[:, a, :], banks[6][:, 0:3 * P]).then_inc(a_p1, 1)

            def swa_lo(n, m, r):
                dve.wait_ge(feat_hi_ready, n + (FEAT["swa_out"][0] + 1))
                TT(feat_lo[:, bass.ds(n, 1), Q0:T], o_f[:, Q0:T].unsqueeze(1),
                   feat_hi[:, bass.ds(n, 1), Q0:T].bitcast(F32),
                   ALU.subtract).then_inc(feat_ready, 1)

            def swa_slot(m, k, has_before, has_own, split, rotate_k):
                at = lambda lag: swa_tile(m, k, lag, has_before, has_own)
                if at(5):
                    swa_maxima(*at(5))
                rotate_k()
                if at(6):
                    swa_p1(at(6)[0], 0)
                split()
                if at(7):
                    swa_lo(*at(7))
                if at(6):
                    swa_p1(at(6)[0], 1)
                if at(5):
                    swa_divide(*at(5))

            def swa(m, first):
                ch, prev = Chunks(BASE["swa"], SWA_PER, m), Chunks(BASE["swa"] - SWA_PER, SWA_PER, m)

                def rotate_k():
                    rotate(ch, 0, 5 * m, k_raw[:, :], k_rot[:, :], 0)

                for k in range(SWA_PER):
                    swa_slot(m, k, not first, True, (lambda: split_lo(ch, k + 2)) if k or not first else lambda: None,
                             rotate_k if k == 2 else lambda: None)
                    if k == 0 and not first:
                        rotate(prev, 5, 5 * m - 1, q_raw[:, 1, :], q_rot[:, 1, :], Q0)
                    if k >= 3:
                        r = k - 3
                        rotate(ch, k - 1, 5 * m + (r + 1), q_raw[:, r % 2, :], q_rot[:, r % 2, :], Q0)
                    if k == 4:
                        dve.wait_ge(a_vt, m + 1)
                        V.tensor_copy(kv1[:, :, :], banks[5][:, 0:2 * P].rearrange("p (b f) -> p b f", b=2))
                        V.tensor_copy(kv0[0:N_META, :], banks[5][0:N_META, 2 * P:3 * P]).then_inc(a_vcopy, 1)

            dve.wait_ge(mask1_in, 16)
            step.link(V.memset(sums[:, :, :], 0.0))
            swa(0, True)
            step.loop(SWA_KV_HEADS // 2 - 1, DVE_STEPS["swa"], lambda i: swa(i + 1, False))
            end = SWA_KV_HEADS // 2
            nothing = lambda: None
            for k in range(5):
                swa_slot(end, k, True, False,
                         nothing if k else lambda: split_lo(Chunks(BASE["swa_out"], RING, 0), 2), nothing)
                if k == 0:
                    rotate(Chunks(BASE["swa"] - SWA_PER, SWA_PER, end), 5, 5 * end - 1, q_raw[:, 1, :],
                           q_rot[:, 1, :], Q0)
            out_pass("swa_out", True, False)
            layer_norm(2)
            ffn(1)
            layer_norm(3)

        @block.tensor
        def _(pe):
            MM = nc.tensor.matmul

            def project(ch, k, hi, lo, tiles=KT, tile_wait=None, t0=0, part=None):
                at, end = part or (0, tiles)
                sl = ch.slot(k)
                if at == 0:
                    pe.wait_ge(lo_ready, ch.number(k) + 1)
                    if not ch.first_turn(k):
                        pe.wait_ge(bank_free[sl], ch.turn(k))
                for j in range(at, end):
                    if tile_wait is not None:
                        tile_wait(j)
                    for n, (w, x) in enumerate(((w_hi, hi), (w_hi, lo), (w_lo, hi))):
                        ins = MM(banks[sl][:, t0:T], w[:, sl, j, :], x[:, j, t0:T], start=(j == 0 and n == 0),
                                 stop=(j == tiles - 1 and n == 2))
                if end == tiles:
                    ins.then_inc(chunk_done, 1)

            def turn(out, in_, rows):
                return nc.tensor.transpose(out, in_, ident[0:rows, 0:rows])

            def h_wait(n):
                def wait(j):
                    for g, (at, _) in enumerate(H_GROUPS):
                        if j == at:
                            pe.wait_ge(h_ready, HG * (n + 1) + g + 1)
                return wait

            project(Chunks(0, RING, 0), 0, h_hi, h_lo, tile_wait=h_wait(-1))
            H = SSD_HEADS

            def gates_turn():
                pe.wait_ge(gates_rows, 1)
                pe.wait_ge(const_in, 32)
                pe.wait_ge(ones_set, 5)
                for n, (rows, (lo, hi)) in enumerate(((acs, B1), (acs, B2), (to_end, B1), (dt_v, B1), (dt_v, B2))):
                    turn(banks[7][:, 32 * n:32 * n + 32], rows[0:H, lo:hi], H)
                for n, rows in enumerate((acs, to_end, to_end2, dt_v)):
                    ins = turn(banks[7][0:N_META, 160 + 32 * n:192 + 32 * n], rows[0:H, 0:N_META], H)
                ins.then_inc(gates_turned, 1)

            def ssd_rows(g, h):
                if h >= 2:
                    pe.wait_ge(s_exp, 4 * g + h - 1)
                MM(banks[5 + h % 2][:, 0:T], ones[0:H, :], head_rows[0:H, h, :], start=True,
                   stop=True).then_inc(s_bc, 1)

            def ssd_y_tile(g, t):
                pe.wait_ge(s_mix, 4 * g + 2 * t + 2)
                pe.wait_ge(s_xd, g + 1)
                if t == 0 and not (isinstance(g, int) and g == 0):
                    pe.wait_ge(s_std, g)
                out_ = banks[(7, 5)[t]]
                for part in range(3):
                    for a in range(2):
                        h, rows = 2 * t + a, slice(SSD_P * a, SSD_P * a + SSD_P)
                        f = slice(SSD_P * h, SSD_P * h + SSD_P)
                        at, x, d = ((0, xd0[0:N_META, f], dec0[0:N_META, h, :]),
                                    (B1[0], xd1[:, 0, f], dec1[:, h, 0:2 * P]),
                                    (B2[0], xd1[:, 1, f], dec1[:, h, 2 * P:3 * P]))[part]
                        ins = MM(out_[rows, at:T], x, d, start=part == 0, stop=part == 2)
                ins.then_inc(s_y, 1)

            def ssd_stats(g):
                pe.wait_ge(s_sq, g + 1)
                for t in range(2):
                    ins = MM(banks[7][:, 0:T], ones[:, :], ssd_z[:, t, :], start=t == 0, stop=t == 1)
                ins.then_inc(s_stat, 1)

            def ssd(g, first):
                ch = Chunks(BASE["ssd"], SSD_PER, g)
                project(ch, 0, h_hi, h_lo)
                if not first:
                    ssd_stats(g - 1)
                project(ch, 1, h_hi, h_lo)
                if first:
                    project(ch, 2, h_hi, h_lo)
                    gates_turn()
                else:
                    pe.wait_ge(s_yread, g)
                pe.wait_ge(s_rows, g + 1)
                ssd_rows(g, 0)
                ssd_rows(g, 1)
                if not first:
                    project(ch, 2, h_hi, h_lo)
                    pe.wait_ge(s_xd, g)
                pe.wait_ge(s_conv, 4 * g + 2)
                bt, ct = conv_out[:, 0, :], conv_out[:, 1, :]
                MM(banks[3][0:N_META, 0:T], bt[:, 0:N_META], ct[:, 0:T], start=True, stop=True)
                MM(banks[4][:, 0:2 * P], bt[:, B1[0]:B1[1]], ct[:, B1[0]:T], start=True, stop=True)
                MM(banks[4][:, 2 * P:3 * P], bt[:, B2[0]:B2[1]], ct[:, B2[0]:T], start=True,
                   stop=True).then_inc(s_scores, 1)
                project(ch, 3, h_hi, h_lo)
                ssd_rows(g, 2)
                ssd_rows(g, 3)
                project(ch, 4, h_hi, h_lo)
                pe.wait_ge(s_conv, 4 * g + 4)
                pe.wait_ge(s_masked, g + 1)
                for t in range(2):
                    x = conv_out[:, 2 + t, :]
                    for b, (lo, hi) in enumerate((B1, B2)):
                        turn(banks[3][:, 256 * b + P * t:256 * b + P * t + P], x[:, lo:hi], P)
                    ins = turn(banks[4][0:N_META, P * t:P * t + P], x[:, 0:N_META], P)
                ins.then_inc(s_xt, 1)
                project(ch, 5, h_hi, h_lo)
                ssd_y_tile(g, 0)
                ssd_y_tile(g, 1)

            ssd(0, True)
            with pe.Fori(0, SSD_GROUPS - 1) as i:
                ssd(i + 1, False)
            def out_pass(name, early=(), early_tiles=0):
                base, tiles, t0 = BASE[name], OUT_PASSES[name], first_token(name)
                before, all_in = FEAT[name]
                per = tiles // (all_in - before)
                ch = Chunks(base, RING, 0)

                def feat_wait(j):
                    if j == 0:
                        pe.wait_ge(feat_ready, all_in - ((tiles - early_tiles) // per if early else 2))
                    elif j >= (early_tiles or tiles - 2 * per) and j % per == 0:
                        pe.wait_ge(feat_ready, before + j // per + 1)

                for n, (within, after) in enumerate(early):
                    def tile_wait(j):
                        if n == 0:
                            feat_wait(j)
                        within(j)

                    project(ch, n, feat_hi, feat_lo, tiles, tile_wait=tile_wait, t0=t0, part=(0, early_tiles))
                    after()
                for n in range(max(1, len(early))):
                    project(ch, n, feat_hi, feat_lo, tiles, tile_wait=feat_wait if n == 0 else None, t0=t0,
                            part=(early_tiles, tiles))
                done = max(1, len(early))
                if name in LN_OF or early:
                    for n in range(1, 4):
                        if n >= done:
                            project(ch, n, feat_hi, feat_lo, tiles, t0=t0)
                        if n == 2 and name in LN_OF:
                            pe.wait_ge(bank_free[ch.slot(0)], ch.turn(0) + 1)
                            MM(banks[3][:, t0:T], ones[:, :], res[:, 0, t0:T], start=True,
                               stop=True).then_inc(l_pivot_sum, 1)
                    done = 4
                with pe.Fori(0, (KT - done) // RING) as i:
                    for k in range(RING):
                        project(Chunks(base + done, RING, i), k, feat_hi, feat_lo, tiles, t0=t0)

            nothing = lambda *_: None
            out_pass("ssd_out", ((nothing, lambda: ssd_stats(SSD_GROUPS - 1)), (nothing, nothing)), KT - 4)

            def gla_gate(hd):
                if not isinstance(hd, int) or hd:
                    pe.wait_ge(g_cross, hd)
                    pe.wait_ge(g_acc, 8 * hd)
                pe.wait_ge(gw_in, 16 * (hd + 1))
                r = slice(2 * GLA_RANK, 3 * GLA_RANK)
                for t in range(2):
                    ins = MM(banks[3 + t][:, 0:T], gate_w[r, P * t:P * t + P], g_lr[r, :], start=True, stop=True)
                ins.then_inc(g_mm, 1)

            def gla_scores(hd, lv, ch):
                b = banks[3 + lv % 2]
                if lv < 2:
                    pe.wait_ge(g_gexp, 2 * hd + 1)
                else:
                    pe.wait_ge(g_acc, 8 * hd + lv - 1)
                if lv:
                    pe.wait_ge(g_zq, 8 * hd + lv)
                else:
                    pe.wait_ge(bank_free[ch.slot(3)], ch.turn(3) + 1)
                k_, q_ = (z_k, z_q) if lv else (k_g, q_g)
                pairs = [(slice(0, P), slice(0, P), B1), (slice(0, P), slice(P, 2 * P), B2)]
                if lv == 0 or LEVELS[lv - 1] < 16:
                    pairs.append((slice(0, N_META), slice(2 * P, T), M0))
                for rows, cols, (lo, hi) in pairs:
                    for t in range(2):
                        ins = MM(b[rows, cols], k_[:, t, lo:hi], q_[:, t, lo:hi], start=t == 0, stop=t == 1)
                ins.then_inc(g_sc, 1)

            def gla_cross(hd):
                b = banks[3]
                pe.wait_ge(g_zend, hd + 1)
                pe.wait_ge(g_acc, 8 * hd + 7)
                for rows, cols, (klo, khi), (lo, hi) in (
                        (slice(0, P), slice(0, P), B1, B2),
                        (slice(0, N_META), slice(P, 2 * P), M0, B1),
                        (slice(0, N_META), slice(2 * P, 3 * P), (B2[0], B2[0] + N_META), B2)):
                    for t in range(2):
                        ins = MM(b[rows, cols], z_k[:, t, klo:khi], z_q[:, t, lo:hi], start=t == 0, stop=t == 1)
                ins.then_inc(g_sc, 1)

            def gla_turn_v(hd, ch, j):
                pe.wait_ge(bank_free[ch.slot(4 + j)], ch.turn(4 + j) + 1)
                if j >= 2:
                    pe.wait_ge(g_vcopy, 4 * hd + j - 1)
                b, v = banks[5 + j % 2], vfm[:, j % 2, :]
                turn(b[:, 0:P], v[:, B1[0]:B1[1]], P)
                turn(b[:, P:2 * P], v[:, B2[0]:B2[1]], P)
                turn(b[0:N_META, 2 * P:3 * P], v[:, 0:N_META], P).then_inc(g_vt, 1)

            def gla_o(hd, j):
                if j >= 2:
                    pe.wait_ge(g_osb, 4 * hd + j - 1)
                b, f = banks[5 + j % 2], slice(P * j, P * j + P)
                MM(b[:, 0:T], vt0[0:N_META, f], a0[0:N_META, :], start=True, stop=False)
                MM(b[:, B1[0]:T], vt1[:, 0, f], a1[:, 0:2 * P], start=False, stop=False)
                MM(b[:, B2[0]:T], vt1[:, 1, f], a1[:, 2 * P:3 * P], start=False, stop=True).then_inc(g_o, 1)

            def gla_stat(hd, j):
                if j == 0 and (not isinstance(hd, int) or hd):
                    pe.wait_ge(g_std, hd)
                pe.wait_ge(g_sqr, 4 * hd + j + 1)
                MM(banks[7][:, 0:T], ones[:, :], o_sq[:, :], start=j == 0, stop=j == 3).then_inc(g_st, 1)

            def gla_outputs(hd):
                pe.wait_ge(g_cross, hd + 1)
                pe.wait_ge(g_scored, hd + 1)
                pe.wait_ge(g_vcopy, 4 * hd + 4)
                gla_o(hd, 0)
                gla_o(hd, 1)

            def gla_within(hd, k, first):
                def within(j):
                    if k == 0 and not first and j == 3:
                        gla_cross(hd - 1)
                    if k == 1 and not first:
                        if j in (1, 4, 7, 10):
                            gla_stat(hd - 1, j // 3)
                        if j in (1, 4):
                            gla_o(hd - 1, 2 + j // 3)
                    if k == 5 and j == 1:
                        gla_scores(hd, 0, Chunks(BASE["gla"], GLA_PER, hd))
                    if k >= 5 and j == 7:
                        gla_scores(hd, k - 4, Chunks(BASE["gla"], GLA_PER, hd))

                return within

            def gla(hd, first):
                ch = Chunks(BASE["gla"], GLA_PER, hd)
                for k in range(GLA_PER):
                    project(ch, k, h_hi, h_lo, tile_wait=gla_within(hd, k, first))
                    if k == 0:
                        gla_gate(hd)
                        if not first:
                            gla_outputs(hd - 1)
                    if 5 <= k < 9:
                        gla_turn_v(hd, ch, k - 5)

            gla(0, True)
            with pe.Fori(0, GLA_HEADS - 1) as i:
                gla(i + 1, False)

            def last_outputs():
                gla_outputs(GLA_HEADS - 1)
                for j in range(KT):
                    gla_within(GLA_HEADS, 1, False)(j)

            out_pass("gla_out", ((gla_within(GLA_HEADS, 0, False), last_outputs), (nothing, nothing),
                                 (nothing, nothing)), KT - 4)

            def layer_norm(n):
                t0 = LN_FROM[n]
                pe.wait_ge(l_acc, (KT - 1) * (n + 1))
                for w in range(2):
                    MM(banks[3 + w][:, t0:T], ones[:, :], ln_sums[:, w, t0:T], start=True, stop=False)
                for w, ready in enumerate((l_d, l_sq)):
                    pe.wait_ge(ready, KT * (n + 1))
                    ins = MM(banks[3 + w][:, t0:T], ones[:, :], ln_d[:, ln_buf(KT - 1), w, t0:T], start=False,
                             stop=True)
                ins.then_inc(l_mean, 1)

            def first_two(n, t0):
                for at, group in H_GROUPS:
                    for k in range(2):
                        project(Chunks(AFTER_LN[n], RING, 0), k, h_hi, h_lo, t0=t0, part=(at, at + group),
                                tile_wait=None if k else h_wait(n))

            def ffn(layer):
                for p, (_, tiles) in enumerate(FFN_PASSES):
                    base, rest = BASE[f"up{layer}{p}"], tiles % FFN_BODY
                    if p == 0:
                        first_two(2 * layer, Q0 * layer)
                    for k in range(0 if p else 2, 2 * rest):
                        project(Chunks(base, RING, 0), k, h_hi, h_lo, t0=Q0 * layer)
                    with pe.Fori(0, tiles // FFN_BODY) as i:
                        for k in range(2 * FFN_BODY):
                            project(Chunks(base + 2 * rest, 2 * FFN_BODY, i), k, h_hi, h_lo, t0=Q0 * layer)
                    out_pass(f"down{layer}{p}")

            layer_norm(0)
            ffn(0)
            layer_norm(1)

            def swa_swap(ch, k, n):
                pe.wait_ge(a_raw, n + 1)
                src, t0 = (k_raw[:, :], 0) if k == 0 else (q_raw[:, k % 2, :], Q0)
                MM(banks[ch.slot(k)][:, t0:T], mk1["swap"], src[:, t0:T], start=True, stop=True).then_inc(a_swap, 1)

            W1, W = N_META + P, 2 * T - P

            def swa_scores(n, m, r):
                pe.wait_ge(a_rot, 5 * m + (r + 2))
                if not isinstance(n, int) or n:
                    pe.wait_ge(a_max, n)
                for rows, cols, (lo, hi), keys in ((P, slice(0, W1), B1, W1), (P, slice(W1, W), B2, T),
                                                   (NQ, slice(W, W + N_META), (Q0, N_META), N_META)):
                    for a in range(2):
                        f = slice(SWA_D * a, SWA_D * a + SWA_D)
                        ins = MM(banks[3 + a][0:rows, cols], q_rot[f, r % 2, lo:hi], k_rot[f, 0:keys], start=True,
                                 stop=True)
                ins.then_inc(a_score, 1)

            def swa_turn_p(n, m, r, a):
                sc_w, sc_m = sc_w2[:, r % 2, :, :], sc_m2[:, r % 2, :, :]
                pe.wait_ge(a_norm, n + 1)
                if a or not isinstance(n, int) or n:
                    pe.wait_ge(a_p0, 2 * n + a)
                    pe.wait_ge(a_p1, 2 * n + a)
                turn(banks[5][0:N_META, B1[0]:B1[1]], sc_w[:, a, 0:N_META], P)
                turn(banks[5][0:N_META, Q0:N_META], sc_m[0:NQ, a, :], NQ)
                turn(banks[5][0:N_META, B2[0]:B2[1]], sc_w[:, a, W1:W1 + N_META], P)
                turn(banks[6][:, 0:P], sc_w[:, a, N_META:W1], P)
                turn(banks[6][:, P:2 * P], sc_w[:, a, W1 + N_META:W1 + W1], P)
                turn(banks[6][:, 2 * P:3 * P], sc_w[:, a, 2 * W1:W], P).then_inc(a_pt, 1)

            def swa_o(n, m, r):
                pe.wait_ge(a_p0, 2 * n + 2)
                pe.wait_ge(a_p1, 2 * n + 2)
                pe.wait_ge(a_vcopy, m + 1)
                if not isinstance(n, int) or n:
                    pe.wait_ge(a_of, n)
                for part in range(3):
                    for a in range(2):
                        f = slice(SWA_D * a, SWA_D * a + SWA_D)
                        at, v, p = ((Q0, kv0[0:N_META, f], p0[0:N_META, a, Q0:T]),
                                    (B1[0], kv1[:, 0, f], p1[:, a, 0:2 * P]),
                                    (B2[0], kv1[:, 1, f], p1[:, a, 2 * P:3 * P]))[part]
                        ins = MM(banks[7][f, at:T], v, p, start=part == 0, stop=part == 2)
                ins.then_inc(a_o, 1)

            def swa_within(m, k, has_before, has_own=True):
                at = lambda lag: swa_tile(m, k, lag, has_before, has_own)

                def within(j):
                    if j == 2 and at(7):
                        swa_o(*at(7))
                    if j in (5, 10) and at(6):
                        swa_turn_p(*at(6), j // 10)

                return within

            def swa(m, first):
                ch, prev = Chunks(BASE["swa"], SWA_PER, m), Chunks(BASE["swa"] - SWA_PER, SWA_PER, m)
                for k in range(SWA_PER):
                    if first and k == 0:
                        first_two(1, 0)
                    if not first or k >= 2:
                        project(ch, k, h_hi, h_lo, t0=0 if k < 2 else Q0, tile_wait=swa_within(m, k, not first))
                    if first and k == 0:
                        pe.wait_ge(mask1_in, 16)
                    if k == 0 and not first:
                        swa_swap(prev, 5, 5 * m - 1)
                    if k == 1:
                        swa_swap(ch, 0, 5 * m)
                    if k >= 3:
                        swa_swap(ch, k - 1, 5 * m + (k - 2))
                    if swa_tile(m, k, 4, not first):
                        swa_scores(*swa_tile(m, k, 4, not first))
                    if k == 4:
                        pe.wait_ge(bank_free[ch.slot(1)], ch.turn(1) + 1)
                        if not first:
                            pe.wait_ge(a_p0, 8 * m)
                        turn(banks[5][:, 0:P], v_fm[:, B1[0]:B1[1]], P)
                        turn(banks[5][:, P:2 * P], v_fm[:, B2[0]:B2[1]], P)
                        turn(banks[5][0:N_META, 2 * P:3 * P], v_fm[:, 0:N_META], P).then_inc(a_vt, 1)

            swa(0, True)
            with pe.Fori(0, SWA_KV_HEADS // 2 - 1) as i:
                swa(i + 1, False)
            end = SWA_KV_HEADS // 2

            def swa_after(k):
                if k == 0:
                    swa_swap(Chunks(BASE["swa"] - SWA_PER, SWA_PER, end), 5, 5 * end - 1)
                if k < 2:
                    swa_scores(*swa_tile(end, k, 4, True, False))
                if k == 2:
                    for later in (3, 4):
                        for j in range(KT):
                            swa_within(end, later, True, False)(j)

            out_pass("swa_out", [(swa_within(end, k, True, False), lambda k=k: swa_after(k)) for k in range(3)],
                     KT - 4)
            layer_norm(2)
            ffn(1)
            layer_norm(3)


def pack_chunks(w, columns):
    rows = w.shape[0]
    out = np.zeros((len(columns), P, KT, P), w.dtype)
    tiles = rows // P
    for n, cols in enumerate(columns):
        out[n, :, 0:tiles, :] = w[:, cols].reshape(tiles, P, len(cols)).transpose(1, 0, 2)
    return out.reshape(len(columns), P, KT * P)


def span(at, n=P):
    return np.arange(at, at + n)


def pack_stream(x):
    w_in = x["hyb_w_in"][0]
    o_z = 0
    o_x = o_z + SSD_INNER
    o_b = o_x + SSD_INNER
    o_c = o_b + SSD_GROUPS * SSD_N
    o_dt = o_c + SSD_GROUPS * SSD_N
    o_q = o_dt + SSD_HEADS
    o_k = o_q + D_MODEL // 2
    o_v = o_k + D_MODEL // 2
    o_lr = o_v + D_MODEL
    o_r = o_lr + GLA_RANK
    small = np.zeros((D_MODEL, P), w_in.dtype)
    small[:, 0:SSD_HEADS] = w_in[:, o_dt:o_dt + SSD_HEADS]
    small[:, SSD_HEADS:SSD_HEADS + GLA_RANK] = w_in[:, o_lr:o_lr + GLA_RANK]
    parts = [pack_chunks(small, [span(0)])]
    cols = []
    for g in range(SSD_GROUPS):
        cols += [span(o_b + P * g), span(o_c + P * g), span(o_x + 2 * P * g), span(o_x + 2 * P * g + P),
                 span(o_z + 2 * P * g), span(o_z + 2 * P * g + P)]
    parts.append(pack_chunks(w_in, cols))
    out_cols = [span(P * n) for n in range(KT)]
    parts.append(pack_chunks(x["hyb_w_out"][0][0:SSD_INNER], out_cols))
    cols = []
    for hd in range(GLA_HEADS):
        cols += [span(o_q + GLA_DK * hd + P * t) for t in range(2)]
        cols += [span(o_k + GLA_DK * hd + P * t) for t in range(2)]
        cols += [span(o_v + GLA_DV * hd + P * t) for t in range(4)]
        cols += [span(o_r + GLA_DV * hd + P * t) for t in range(4)]
    parts.append(pack_chunks(w_in, cols))
    parts.append(pack_chunks(x["hyb_w_out"][0][SSD_INNER:], out_cols))
    for layer in range(DEPTH):
        if layer == 1:
            heads = [(8 * m + r, 8 * m + 4 + r) for m in range(SWA_KV_HEADS // 2) for r in range(4)]
            q_cols = [np.concatenate([span(SWA_D * a, SWA_D), span(SWA_D * b, SWA_D)]) for a, b in heads]
            kv = SWA_Q_HEADS * SWA_D
            cols = []
            for m in range(SWA_KV_HEADS // 2):
                cols += [span(kv + P * m), span(kv + SWA_KV_HEADS * SWA_D + P * m)] + q_cols[4 * m:4 * m + 4]
            parts.append(pack_chunks(x["swa_w_qkv"][0], cols))
            parts.append(pack_chunks(x["swa_w_out"][0][np.concatenate(q_cols)], out_cols))
        for tile0, tiles in FFN_PASSES:
            cols = []
            for t in range(tile0, tile0 + tiles):
                cols += [span(P * t), span(D_FF + P * t)]
            parts.append(pack_chunks(x["ffn_w_up"][layer], cols))
            parts.append(pack_chunks(x["ffn_w_down"][layer][P * tile0:P * (tile0 + tiles)], out_cols))
    return np.concatenate(parts)


def pack_table(x):
    t = table_columns()
    out = np.zeros((P, t.at), np.float32)

    def put(name, a, rows=P):
        at, n = t.where[name]
        out[0:rows, at:at + n] = a.reshape(rows, n)

    fm = lambda v: np.ascontiguousarray(v.reshape(-1, P).T)
    taps = np.stack([fm(w) for w in x["hyb_conv_w"][0]] + [fm(x["hyb_conv_b"][0])], axis=2)
    xt, bt = SSD_INNER // P, SSD_GROUPS
    order = [i for g in range(SSD_GROUPS) for i in (xt + g, xt + bt + g, 2 * g, 2 * g + 1)]
    put("ssd_conv", taps[:, order, :])
    put("ssd_d", fm(np.repeat(x["ssd_d"][0], SSD_P)))
    put("ssd_norm", fm(x["ssd_norm_w"][0]))
    put("gla_norm", fm(x["gla_norm_w"][0]))
    put("gate_b", fm(x["gla_gate_b"][0]))
    ln = []
    for layer in range(DEPTH):
        for kind in ("mix", "ffn"):
            ln += [fm(x[f"ln_{kind}_g"][layer]), fm(x[f"ln_{kind}_b"][layer])]
    put("ln", np.stack(ln, axis=1))
    ffn = []
    for layer in range(DEPTH):
        v = [fm(w) for w in x["ffn_conv_w"][layer]] + [fm(x["ffn_conv_b"][layer])]
        ffn.append(np.stack([a[:, 0:FF_TILES] for a in v] + [a[:, FF_TILES:] for a in v], axis=2))
    put("ffn", np.stack(ffn, axis=1))
    put("sinks", np.repeat(x["swa_sinks"][0][None], P, axis=0))
    put("dt_bias", x["ssd_dt_bias"][0], SSD_HEADS)
    put("a_log", x["ssd_a_log"][0], SSD_HEADS)
    return out


def shape_masks():
    out = np.zeros((DEPTH, P, MASK_COLS), np.float32)
    key, query = np.arange(P)[:, None], np.arange(P)[None, :]
    causal = (query >= key).astype(np.float32)
    for layer in range(DEPTH):
        t = mask_columns(layer)

        def put(name, a, rows=P):
            at, n = t.where[name]
            out[layer, 0:rows, at:at + n] = a

        put("ident", np.eye(P))
        if layer == 0:
            put("causal", np.concatenate([causal, np.ones((P, P)), causal], axis=1))
            put("causal_meta", np.concatenate([causal[0:N_META, 0:N_META], np.ones((N_META, T - N_META))], axis=1),
                N_META)
            levels = [np.eye(P)]
            for half in LEVELS:
                same = query // (2 * half) == key // (2 * half)
                levels.append(same & (query % (2 * half) >= half) & (key % (2 * half) < half))
            put("levels", np.concatenate(levels, axis=1))
        else:
            half = ROPE_DIM // 2
            swap = np.zeros((P, P))
            for head in range(P // SWA_D):
                for d in range(half):
                    a, b = SWA_D * head + d, SWA_D * head + half + d
                    swap[b, a] = -1.0
                    swap[a, b] = 1.0
            put("swap", swap)
            freq = np.float32(ROPE_THETA) ** (-np.arange(half, dtype=np.float32) / np.float32(half))
            angle = np.arange(T, dtype=np.float32)[None, :] * freq.astype(np.float32)[:, None]
            cos, sin = np.ones((P, T)), np.zeros((P, T))
            for head in range(P // SWA_D):
                for part in range(2):
                    rows = slice(SWA_D * head + half * part, SWA_D * head + half * part + half)
                    cos[rows], sin[rows] = np.cos(angle), np.sin(angle)
            put("cos", cos)
            put("sin", sin)
            hide = np.float32(-1e30)
            q, k = np.arange(P)[:, None], np.arange(P)[None, :]
            meta = np.zeros((P, N_META))
            own, before = np.where(k <= q, 0, hide), np.where(k > q, 0, hide)
            put("window", np.concatenate([meta, own, meta, before, own], axis=1))
            put("window_meta", np.where(k[:, 0:N_META] <= q[Q0:N_META], 0, hide), NQ)
    return out


def kernel(**inputs):
    import concourse.bacc as bacc
    from concourse.bass_utils import run_bass_kernel_spmd

    x = {name: np.asarray(a) for name, a in inputs.items()}
    tokens = np.concatenate([x["meta_tokens"], x["x"][0]])
    arrays = {
        "stream": pack_stream(x),
        "h0": np.ascontiguousarray(tokens.T.reshape(KT, P, T).transpose(1, 0, 2)),
        "table": pack_table(x),
        "masks": shape_masks(),
        "gate_w2": np.ascontiguousarray(x["gla_gate_w2"][0]),
    }
    nc = bacc.Bacc("TRN2", target_bir_lowering=False, num_devices=1)
    args = [nc.dram_tensor(f"in_{name}", a.shape, mybir.dt.from_np(a.dtype), kind="ExternalInput").ap()
            for name, a in arrays.items()]
    out = nc.dram_tensor("out", (P, KT, SEQ), F32, kind="ExternalOutput").ap()
    trunk_kernel(nc, *args, out)
    r = run_bass_kernel_spmd(nc, [{f"in_{name}": a for name, a in arrays.items()}], core_ids=[0])
    y = np.asarray(r.results[0]["out"])
    return np.ascontiguousarray(y.transpose(1, 0, 2).reshape(D_MODEL, SEQ).T)[None]
```
